# Optimizing a Trainium2 kernel written in Bass

```python
import jax, jax.numpy as jnp
from jax import lax
import numpy as np

D_MODEL = 2048
BATCH = 1
SEQ = 256
DEPTH = 1
DEC_BATCH = 1
DEC_SEQ = 32
PAST_LEN = 256

CHUNK = 64
Q_BLOCK = 128
ROPE_THETA = 500000.0
EPS = 1e-6

A_HEADS = 8
A_KV_HEADS = 2
A_HEAD_DIM = 128
A_ROT = A_HEAD_DIM // 4
A_WIDTH = A_HEADS * A_HEAD_DIM
IDX_HEADS = 16
IDX_DIM = 64
IDX_ROT = IDX_DIM // 4
TOPK_MAX = 256

B_HEADS = 8
Q_LORA = 512
KV_LORA = 512
NOPE_DIM = 128
ROPE_DIM = 64
V_DIM = 128
B_WIDTH = B_HEADS * V_DIM

SPLIT_SIZES = (A_WIDTH, A_KV_HEADS * A_HEAD_DIM, A_KV_HEADS * A_HEAD_DIM, A_WIDTH,
               IDX_HEADS * IDX_DIM, IDX_DIM, IDX_HEADS,
               Q_LORA, KV_LORA, ROPE_DIM, B_WIDTH, 2 * D_MODEL)
PROJ_WIDTH = sum(SPLIT_SIZES)

kernel_name = 'dsa_mla_gated_hybrid_stream_step'

def rmsnorm(x, g):
    xf = x.astype(jnp.float32)
    xf = xf * lax.rsqrt(jnp.mean(xf * xf, axis=-1, keepdims=True) + EPS)
    return xf.astype(x.dtype) * g

def rope(x, pos, rot):
    half = rot // 2
    inv_freq = ROPE_THETA ** (-jnp.arange(half, dtype=jnp.float32) * (2.0 / rot))
    ang = pos.astype(jnp.float32)[:, None] * inv_freq[None, :]
    cos = jnp.cos(ang)[:, None, :]
    sin = jnp.sin(ang)[:, None, :]
    x1 = x[..., :half].astype(jnp.float32)
    x2 = x[..., half:rot].astype(jnp.float32)
    r = jnp.concatenate([x1 * cos - x2 * sin, x2 * cos + x1 * sin], axis=-1).astype(x.dtype)
    return jnp.concatenate([r, x[..., rot:]], axis=-1)

def split_proj(z):
    parts, off = [], 0
    for s in SPLIT_SIZES:
        parts.append(z[..., off:off + s])
        off += s
    return parts

def sweep_blocks(fn, qpos, *qs):
    T = qpos.shape[0]
    bs = min(T, Q_BLOCK)
    nb = T // bs
    def blk(a):
        return jnp.moveaxis(a.reshape((a.shape[0], nb, bs) + a.shape[2:]), 1, 0)
    out = lax.map(lambda args: fn(*args), (qpos.reshape(nb, bs),) + tuple(blk(a) for a in qs))
    out = jnp.moveaxis(out, 0, 1)
    return out.reshape((out.shape[0], T) + out.shape[3:])

def dsa_attend(q, k, v, iq, ik, iw, qpos, kpos):
    L = k.shape[1]
    topk = min(TOPK_MAX, L // 4)
    grp = A_HEADS // A_KV_HEADS
    kchunk = kpos // CHUNK
    ikf = ik.astype(jnp.float32)

    def block(qp, qb, iqb, iwb):
        B, Tb = qb.shape[0], qb.shape[1]
        qchunk = qp // CHUNK
        allowed = kchunk[None, :] <= qchunk[:, None]
        rel = jax.nn.relu(jnp.einsum('bthd,bsd->bths', iqb.astype(jnp.float32), ikf) * IDX_DIM ** -0.5)
        score = jnp.einsum('bths,bth->bts', rel, iwb.astype(jnp.float32))
        score = jnp.where(allowed[None], score, -jnp.inf)
        _, sel = lax.top_k(score, topk)
        valid = kchunk[sel] <= qchunk[None, :, None]
        ks = jax.vmap(lambda kk, ii: kk[ii])(k, sel)
        vs = jax.vmap(lambda vv, ii: vv[ii])(v, sel)
        qg = qb.reshape(B, Tb, A_KV_HEADS, grp, A_HEAD_DIM)
        s = jnp.einsum('btkgd,btskd->btkgs', qg, ks).astype(jnp.float32) * A_HEAD_DIM ** -0.5
        s = jnp.where(valid[:, :, None, None, :], s, -jnp.inf)
        p = jax.nn.softmax(s, axis=-1).astype(vs.dtype)
        o = jnp.einsum('btkgs,btskd->btkgd', p, vs)
        return o.reshape(B, Tb, A_WIDTH)

    return sweep_blocks(block, qpos, q, iq, iw)

def mla_attend(q_nope, q_rope, ckv, krope, w_uk, w_uv, qpos, kpos):
    k_nope = jnp.einsum('bsc,chd->bshd', ckv, w_uk)
    v = jnp.einsum('bsc,chd->bshd', ckv, w_uv)
    kchunk = kpos // CHUNK
    scale = (NOPE_DIM + ROPE_DIM) ** -0.5

    def block(qp, qn, qr):
        B, Tb = qn.shape[0], qn.shape[1]
        allowed = kchunk[None, :] <= (qp // CHUNK)[:, None]
        s = (jnp.einsum('bthd,bshd->bhts', qn, k_nope)
             + jnp.einsum('bthr,bsr->bhts', qr, krope)).astype(jnp.float32) * scale
        s = jnp.where(allowed[None, None], s, -jnp.inf)
        p = jax.nn.softmax(s, axis=-1).astype(v.dtype)
        o = jnp.einsum('bhts,bshd->bthd', p, v)
        return o.reshape(B, Tb, B_WIDTH)

    return sweep_blocks(block, qpos, q_nope, q_rope)

def layer(h, qpos, past, norm_g, w_in, w_uq, q_norm_g, kv_norm_g, w_uk, w_uv, w_o_a, w_o_b, w_out):
    B, T, _ = h.shape
    pk, pv, pik, pckv, pkr = past
    L = pk.shape[1] + T
    kpos = jnp.arange(L, dtype=jnp.int32)
    xn = rmsnorm(h, norm_g)
    aq, ak, av, agate, iq, ik, iw, cq, ckv, kr, bgate, mg = split_proj(xn @ w_in)
    aq = rope(aq.reshape(B, T, A_HEADS, A_HEAD_DIM), qpos, A_ROT)
    ak = rope(ak.reshape(B, T, A_KV_HEADS, A_HEAD_DIM), qpos, A_ROT)
    av = av.reshape(B, T, A_KV_HEADS, A_HEAD_DIM)
    iq = rope(iq.reshape(B, T, IDX_HEADS, IDX_DIM), qpos, IDX_ROT)
    ik = rope(ik[:, :, None, :], qpos, IDX_ROT)[:, :, 0, :]
    iw = iw * IDX_HEADS ** -0.5
    o_a = dsa_attend(aq, jnp.concatenate([pk, ak], axis=1), jnp.concatenate([pv, av], axis=1),
                     iq, jnp.concatenate([pik, ik], axis=1), iw, qpos, kpos)
    y_a = (o_a * jax.nn.silu(agate)) @ w_o_a
    cq = rmsnorm(cq, q_norm_g)
    qb = jnp.einsum('btc,chd->bthd', cq, w_uq)
    q_nope = qb[..., :NOPE_DIM]
    q_rope = rope(qb[..., NOPE_DIM:], qpos, ROPE_DIM)
    ckv = rmsnorm(ckv, kv_norm_g)
    kr = rope(kr[:, :, None, :], qpos, ROPE_DIM)[:, :, 0, :]
    o_b = mla_attend(q_nope, q_rope, jnp.concatenate([pckv, ckv], axis=1),
                     jnp.concatenate([pkr, kr], axis=1), w_uk, w_uv, qpos, kpos)
    y_b = (o_b * jax.nn.silu(bgate)) @ w_o_b
    g = jax.nn.sigmoid(mg.astype(jnp.float32)).astype(h.dtype)
    m = g[..., :D_MODEL] * y_a + g[..., D_MODEL:] * y_b
    h = h + m @ w_out
    return h, (ak, av, ik, ckv, kr)

def trunk(x, caches, final_g, params):
    past_len = caches[0].shape[2]
    qpos = past_len + jnp.arange(x.shape[1], dtype=jnp.int32)
    h = x
    new = []
    for l in range(DEPTH):
        h, rows = layer(h, qpos, tuple(c[l] for c in caches), *(p[l] for p in params))
        new.append(rows)
    y = rmsnorm(h, final_g)
    stacked = [jnp.stack([r[i] for r in new], axis=0) for i in range(5)]
    return y, stacked

def setup_inputs(seed: int = 0) -> dict:
    key = jax.random.key(seed)
    ks = jax.random.split(key, 20)
    f32 = jnp.float32
    nrm = lambda k, shape, s: jax.random.normal(k, shape, f32) * s
    return {
        'x_prompt': nrm(ks[0], (BATCH, SEQ, D_MODEL), 1.0),
        'x_sample': nrm(ks[1], (DEC_BATCH, DEC_SEQ, D_MODEL), 1.0),
        'cache_a_k': nrm(ks[2], (DEPTH, DEC_BATCH, PAST_LEN, A_KV_HEADS, A_HEAD_DIM), 1.0),
        'cache_a_v': nrm(ks[3], (DEPTH, DEC_BATCH, PAST_LEN, A_KV_HEADS, A_HEAD_DIM), 1.0),
        'cache_idx_k': nrm(ks[4], (DEPTH, DEC_BATCH, PAST_LEN, IDX_DIM), 1.0),
        'cache_mla_ckv': nrm(ks[5], (DEPTH, DEC_BATCH, PAST_LEN, KV_LORA), 1.0),
        'cache_mla_krope': nrm(ks[6], (DEPTH, DEC_BATCH, PAST_LEN, ROPE_DIM), 1.0),
        'norm_g': 1.0 + nrm(ks[7], (DEPTH, D_MODEL), 0.01),
        'w_in': nrm(ks[8], (DEPTH, D_MODEL, PROJ_WIDTH), D_MODEL ** -0.5),
        'w_uq': nrm(ks[9], (DEPTH, Q_LORA, B_HEADS, NOPE_DIM + ROPE_DIM), Q_LORA ** -0.5),
        'q_norm_g': 1.0 + nrm(ks[10], (DEPTH, Q_LORA), 0.01),
        'kv_norm_g': 1.0 + nrm(ks[11], (DEPTH, KV_LORA), 0.01),
        'w_uk': nrm(ks[12], (DEPTH, KV_LORA, B_HEADS, NOPE_DIM), KV_LORA ** -0.5),
        'w_uv': nrm(ks[13], (DEPTH, KV_LORA, B_HEADS, V_DIM), KV_LORA ** -0.5),
        'w_o_a': nrm(ks[14], (DEPTH, A_WIDTH, D_MODEL), A_WIDTH ** -0.5),
        'w_o_b': nrm(ks[15], (DEPTH, B_WIDTH, D_MODEL), B_WIDTH ** -0.5),
        'w_out': nrm(ks[16], (DEPTH, D_MODEL, D_MODEL), D_MODEL ** -0.5),
        'final_g': 1.0 + nrm(ks[17], (D_MODEL,), 0.01),
    }

def reference(x_prompt, x_sample, cache_a_k, cache_a_v, cache_idx_k, cache_mla_ckv, cache_mla_krope,
              norm_g, w_in, w_uq, q_norm_g, kv_norm_g, w_uk, w_uv, w_o_a, w_o_b, w_out, final_g):
    params = (norm_g, w_in, w_uq, q_norm_g, kv_norm_g, w_uk, w_uv, w_o_a, w_o_b, w_out)
    dt = x_prompt.dtype
    empty = (jnp.zeros((DEPTH, x_prompt.shape[0], 0, A_KV_HEADS, A_HEAD_DIM), dt),
             jnp.zeros((DEPTH, x_prompt.shape[0], 0, A_KV_HEADS, A_HEAD_DIM), dt),
             jnp.zeros((DEPTH, x_prompt.shape[0], 0, IDX_DIM), dt),
             jnp.zeros((DEPTH, x_prompt.shape[0], 0, KV_LORA), dt),
             jnp.zeros((DEPTH, x_prompt.shape[0], 0, ROPE_DIM), dt))
    y_prompt, (pk, pv, pik, pckv, pkr) = trunk(x_prompt, empty, final_g, params)
    caches = (cache_a_k, cache_a_v, cache_idx_k, cache_mla_ckv, cache_mla_krope)
    y_sample, (sk, sv, sik, sckv, skr) = trunk(x_sample, caches, final_g, params)
    return (y_prompt, y_sample, pk, pv, pik, pckv, pkr, sk, sv, sik, sckv, skr)


_drawn_inputs = setup_inputs


def setup_inputs(seed=0):
    import zlib

    import numpy as np

    out = dict(_drawn_inputs(seed))
    spreads = {}
    factors = {'cache_mla_krope': 3.687,
     'norm_g': 5.558,
     'q_norm_g': 8.0,
     'kv_norm_g': 5.511,
     'final_g': 5.651}
    for name, (base, spread) in spreads.items():
        noise = np.random.default_rng([zlib.crc32(name.encode()), seed]).standard_normal(out[name].shape)
        drawn = base * np.exp(spread * noise) if base else spread * noise
        out[name] = __import__('jax').numpy.asarray(drawn.astype(out[name].dtype))
    for name, factor in factors.items():
        out[name] = (out[name] * factor).astype(out[name].dtype)
    return out
```

```python
from contextlib import ExitStack

import numpy as np

import concourse.bass as bass
from concourse import mybir

F32 = mybir.dt.float32
F32R = mybir.dt.float32r
ALU = mybir.AluOpType
ACT = mybir.ActivationFunctionType
AX_X = mybir.AxisListType.X

P = 128
D_MODEL = 2048
SEQ, DEC, PAST = 256, 32, 256
NTOK = DEC + SEQ
NKEY = PAST + NTOK
CHUNK = 64
EPS = 1e-6
ROPE_THETA = 500000.0
A_HEADS, A_KV, A_DIM = 8, 2, 128
GRP = A_HEADS // A_KV
IDX_HEADS, IDX_DIM = 16, 64
B_HEADS, NOPE, ROPE = 8, 128, 64
LORA = 512
KD = D_MODEL // P
KL = LORA // P
KH = KD // 2
TOPK_PROMPT = SEQ // 4
TOPK_SAMPLE = (PAST + DEC) // 4
NEG = -1e30
TAKEN = -3e38
A_SCALE = A_DIM ** -0.5
B_SCALE = (NOPE + ROPE) ** -0.5

COL_AQ, COL_AK, COL_AV, COL_AGATE, COL_IQ, COL_IK, COL_IW, COL_CQ, COL_CKV, COL_KR, COL_BGATE, COL_MG, PROJ = (
    0, 1024, 1280, 1536, 2560, 3584, 3648, 3664, 4176, 4688, 4752, 5776, 9872)

TOK = [(0, DEC), (DEC, P), (DEC + P, P)]
NEW = PAST
PROMPT = PAST + DEC

RAW = 4
G_SMALL, G_IQ, G_AQ, G_AK, G_AV, G_CQ, G_MG, G_GATE, G_END = 0, 1, 5, 9, 10, 11, 15, 31, 39
STEP_CQ = 2 * G_CQ
STEP_UQ = 2 * G_MG
STEP_UK = STEP_UQ + 4
STEP_UV = STEP_UK + 2
STEP_MG = STEP_UV + 2
STEP_GATE = STEP_MG + 32
STEP_Y = STEP_GATE + 16
STEP_OUT = STEP_Y + 16
STEP_END = STEP_OUT + 16
LATE = STEP_MG - STEP_UQ


def steps_of(group):
    return 2 * group + (LATE if group >= G_MG else 0)


class Tally:

    def __init__(self, sem):
        self.sem, self.n, self.it, self.per = sem, 0, None, 0

    def add(self, ins):
        ins.then_inc(self.sem, 1)
        self.n += 1
        return self.now()

    def now(self):
        return self.n if self.it is None else self.it * self.per + self.n

    def enter(self, it, per):
        self.it, self.per, self.start = it, per, self.n

    def leave(self, turns):
        assert self.n - self.start == self.per, (self.n - self.start, self.per)
        self.n, self.it = self.start + self.per * turns, None


def attention_units():
    units = []
    for g in range(A_KV):
        units.append(("A", 0, g))
        units += [("A", kind, h) for h in range(GRP * g, GRP * g + GRP) for kind in (1, 2)]
    for g in range(2):
        units.append(("B", 0, g))
        units += [("B", kind, h) for h in range(4 * g, 4 * g + 4) for kind in (1, 2)]
    return units


UNITS = attention_units()
N_A = sum(u[0] == "A" for u in UNITS)
KEYS = [(0, PAST + DEC), (PROMPT, P), (PROMPT, 2 * P)]
KEY_TILES = [[(0, P, 0), (P, P, 1), (2 * P, DEC, 2)], [(0, P, 3)], [(0, P, 3), (P, P, 4)]]
V_TILES = [0, P, NEW, PROMPT, PROMPT + P]


def indexer_units():
    return [(tt, tuple(range(h, h + n))) for tt, n in ((1, 4), (2, 2), (0, 1)) for h in range(0, IDX_HEADS, n)]


IDX_UNITS = indexer_units()
SWAP_16 = [(i + 16) % 32 for i in range(32)]
SWAP_8 = [(i + 8) % 16 if i < 16 else i for i in range(32)]


def hybrid_layer(nc, d):
    def rows(ap, k):
        return ap.rearrange("(k p) n -> p k n", p=P)

    w_in = rows(d["w_in"], KD)
    w_uq = d["w_uq"].rearrange("(k p) n -> p k n", p=P)
    w_uk = d["w_uk"].rearrange("(k p) n -> p k n", p=P)
    w_uv = d["w_uv"].rearrange("(k p) n -> p k n", p=P)
    w_oa = rows(d["w_o_a"], 8)
    w_ob = rows(d["w_o_b"], 8)
    w_out = rows(d["w_out"], KD)

    ctx = ExitStack()
    with ctx:
        def sem(name):
            return ctx.enter_context(nc.semaphore(name))

        def at(name, shape, offset, dtype=F32):
            t = nc.alloc_sbuf_tensor_at(name, shape, dtype, offset=offset)
            end = offset + 4 * int(np.prod(shape[1:]))
            assert end <= nc.sbuf_usable_end, (name, end)
            return t, end

        def row(start, *parts):
            made = []
            for name, shape, *dtype in parts:
                t, start = at(name, shape, start, *dtype)
                start = -(-start // 32) * 32
                made.append(t)
            return (*made, start)

        (x_hi, x_lo, raw, w_hi, w_lo, ident, ones, rope_tab, norm_g, lora_g, ss, var, root, rstd, newton,
         mx, neg_mx, sum_p, inv_p, o_base) = row(
            -(-nc.sbuf_base // 64) * 64,
            ("x_hi", [P, KD, NTOK], F32R), ("x_lo", [P, KD, NTOK], F32R), ("raw", [P, RAW, 2048]),
            ("w_hi", [P, 2, 2048], F32R), ("w_lo", [P, 2, 2048], F32R), ("ident_sb", [P, P]), ("ones", [P, P]),
            ("rope_sb", [P, 6, NTOK]), ("norm_g_sb", [P, KD]), ("lora_g", [P, 2, KL]), ("ss", [P, 4]),
            ("var", [P, 4]), ("root", [P, 4]), ("rstd", [P, 4]), ("newton", [P, 4]), ("mx", [P, 2]),
            ("neg_mx", [P, 2]), ("sum_p", [P, 2]), ("inv_p", [P, 2]))
        o_t, arena = at("o_t", [P, 16, NTOK], o_base)
        sq_z, lat_var, lat_r, lat_t, _ = row(
            o_base, ("sq_z", [P, 2, KL, NTOK]), ("lat_var", [P, 2, NTOK]), ("lat_r", [P, 2, NTOK]),
            ("lat_t", [P, 2, NTOK]))
        final_g, h_stage, h_sq, h_ss, _ = row(
            o_base, ("final_g_sb", [P, D_MODEL]), ("h_stage", [P, 2, 2, NTOK]), ("h_sq", [P, 256]),
            ("h_ss", [P, 3, 8]))

        kr_t, probs, masked, probs_t, r1 = row(
            arena, ("kr_t", [P, 2, NKEY]), ("probs", [P, 2, PAST + DEC]), ("masked", [P, 2, PAST + DEC]),
            ("probs_t", [P, 2, 3, P]))
        ckv_past, score, s_end = row(arena + 8 * NKEY, ("ckv_past", [P, 2, LORA]), ("score", [P, 3, PAST + DEC]))
        assert s_end <= r1
        (aq_t, ka_t, va_past, kv_tok, work, iw_tok, top8, ik_tok, kr_tok, r4) = row(
            r1, ("aq_t", [P, 8, NTOK]), ("ka_t", [P, A_KV, NKEY]), ("va_past", [P, 2, 256]),
            ("kv_tok", [P, 3, 512]), ("work", [P, 3, PAST + DEC]),
            ("iw_tok", [P, 3, IDX_HEADS]), ("top8", [P, 2, 8]), ("ik_tok", [P, 3, P]), ("kr_tok", [P, 3, ROPE]))
        iq_t, r5 = at("iq_t", [P, 8, NTOK], r4)
        lora_z, _ = at("lora_z", [P, 2, KL, NTOK], r4)
        (z_stage, z_shuf, z_cos, ik_t, ik_z, kr_swap, relu_ring, k_past, idx_past, kr_past, _) = row(
            r5, ("z_stage", [P, 2, 2, NTOK]), ("z_shuf", [P, 2, NTOK]), ("z_cos", [P, 2, NTOK]),
            ("ik_t", [P, 2, NKEY]), ("ik_z", [P, NTOK]), ("kr_swap", [P, NTOK]), ("relu_ring", [P, 4, 512]),
            ("k_past", [P, 2, 256]), ("idx_past", [P, 2, 2 * IDX_DIM]), ("kr_past", [P, 2, 2 * ROPE]))
        cq_hi, cq_lo, ckv_tok, r6 = row(
            r5, ("cq_hi", [P, KL, NTOK], F32R), ("cq_lo", [P, KL, NTOK], F32R), ("ckv_tok", [P, 3, LORA]))
        qr_z, vb, v_end = row(r4, ("qr_z", [P, 4, NTOK]), ("vb", [P, 5, 1024]))
        qr_t = qr_z
        qr_swap, _ = at("qr_swap", [P, 4, NTOK], r4 + 16 * NTOK)
        ckv_hi, ckv_lo, _ = row(
            max(r6, v_end), ("ckv_hi", [P, KL, NKEY], F32R), ("ckv_lo", [P, KL, NKEY], F32R))
        qn_t, kb_t, b1 = row(r1, ("qn_t", [P, 8, NTOK]), ("kb_t", [P, B_HEADS, NKEY]))
        assert b1 <= r4
        merge_g, og_hi, og_lo, gate_e, gate_x, _ = row(
            arena, ("merge_g", [P, 32, NTOK]), ("og_hi", [P, 16, NTOK], F32R), ("og_lo", [P, 16, NTOK], F32R),
            ("gate_e", [P, 2, 2, NTOK]), ("gate_x", [P, 2, 2, NTOK]))
        y_a, _ = at("y_a", [P, 2, NTOK], o_base)
        y_b, _ = at("y_b", [P, 2, NTOK], o_base + 8 * NTOK)
        m_hi, m_lo = x_hi, x_lo
        x_tok, _ = at("x_tok", [P, 3, D_MODEL], r1)
        x_sq, _ = at("x_sq", [P, 2, D_MODEL], r4)
        h_tok, _ = at("h_tok", [P, 3, D_MODEL], arena)

        ps = ctx.enter_context(nc.psum_tensor("ps", [P, 8, 512], F32))

        def pair(n):
            return ps[:, 2 * (n % 2):2 * (n % 2) + 2, 0:NTOK]

        raw_landed = [sem(f"raw_landed{i}") for i in range(RAW)]
        hi_done, lo_done, step_done = sem("hi_done"), sem("lo_done"), sem("step_done")
        pair_read, stage_used = sem("pair_read"), sem("stage_used")
        x_landed = [sem(f"x_landed{i}") for i in range(3)]
        consts_landed, past_landed, va_landed = sem("consts_landed"), sem("past_landed"), sem("va_landed")
        ckv_past_landed, res_landed, fg_landed = sem("ckv_past_landed"), sem("res_landed"), sem("fg_landed")
        ss_done, var_done, root_done, xn_done = (sem(n) for n in ("ss_done", "var_done", "root_done", "xn_done"))
        xt_ready, xhi_done, xlo_done = sem("xt_ready"), sem("xhi_done"), sem("xlo_done")
        small_copied, roped, tr_ready, tr_copied = (sem(n) for n in ("small_copied", "roped", "tr_ready", "tr_copied"))
        iw_scaled = sem("iw_scaled")
        idx_ready, relu_done, idx_added = sem("idx_ready"), sem("relu_done"), sem("idx_added")
        lora_copied, sq_done, sumsq_ready, lat_var_done, lat_root_done, lat_normed = (
            sem(n) for n in ("lora_copied", "sq_done", "sumsq_ready", "lat_var_done", "lat_root_done", "lat_normed"))
        lat_hi, lat_lo, past_lat_ready, past_lat_hi, past_lat_lo, tok_ready, tok_copied = (
            sem(n) for n in ("lat_hi", "lat_lo", "past_lat_ready", "past_lat_hi", "past_lat_lo", "tok_ready",
                             "tok_copied"))
        ones_set, ss_cleared, h_cleared = sem("ones_set"), sem("ss_cleared"), sem("h_cleared")
        scores_ready, scores_read, neg_ready, p_ready, pn_ready = (
            sem(n) for n in ("scores_ready", "scores_read", "neg_ready", "p_ready", "pn_ready"))
        pt_ready, pt_copied, o_ready, o_copied = (sem(n) for n in ("pt_ready", "pt_copied", "o_ready", "o_copied"))
        bias_done = sem("bias_done")
        uq_ready, uq_copied, q_roped = sem("uq_ready"), sem("uq_copied"), sem("q_roped")
        uk_ready, uk_copied, uv_ready, uv_copied = (sem(n) for n in ("uk_ready", "uk_copied", "uv_ready", "uv_copied"))
        gate_copied, gate_used, mg_exp, mg_done = (sem(n) for n in ("gate_copied", "gate_used", "mg_exp", "mg_done"))
        y_ready, y_read, m_done = sem("y_ready"), sem("y_read"), sem("m_done")
        hT_copied, ht_ready, h_added, h_squared, h_ready = (
            sem(n) for n in ("hT_copied", "ht_ready", "h_added", "h_squared", "h_ready"))
        h_var_done, h_root_done = sem("h_var_done"), sem("h_root_done")
        dve_self, act_self = sem("dve_self"), sem("act_self")
        kv_out, ckv_out, y_out = sem("kv_out"), sem("ckv_out"), sem("y_out")

        block = ctx.enter_context(nc.Block())

        def landed(step, it=0):
            return 16 * (step // RAW + 1) + (16 if step % RAW < 2 else 0) + 16 * it

        @block.sync
        def _(sp):
            for tt, (t0, n) in enumerate(TOK):
                src = d["x_sample"] if tt == 0 else d["x_prompt"][t0 - DEC:t0 - DEC + n, :]
                sp.dma_start(x_tok[0:n, tt, :], src).then_inc(x_landed[tt], 16)

            def load(step, src, it=0, part=slice(0, 2048)):
                if step >= RAW:
                    sp.wait_ge(lo_done, step - RAW + 1 + RAW * it)
                dst = raw[:, step % RAW, part].rearrange("p (k n) -> p k n", k=src.shape[1])
                sp.dma_start(dst, src).then_inc(raw_landed[step % RAW], 16)

            def load_w_in(group, turns, col):
                with sp.Fori(0, turns) as it:
                    for j in range(4):
                        load(steps_of(group) + j, w_in[:, KH * (j % 2):KH * (j % 2) + KH,
                                                       bass.ds(it * 512 + (col + 256 * (j // 2)), 256)], it)

            for half in range(2):
                dst = raw[:, half, :].rearrange("p (k n) -> p k n", k=KH)
                for m, col in enumerate((COL_IK, COL_KR)):
                    sp.dma_start(dst[:, :, m * P:(m + 1) * P],
                                 w_in[:, KH * half:KH * half + KH, col:col + P]).then_inc(raw_landed[half], 16)
            for j in range(8):
                col = COL_IQ + 256 * (j // 2)
                load(steps_of(G_IQ) + j, w_in[:, KH * (j % 2):KH * (j % 2) + KH, col:col + 256])
            load_w_in(G_AQ, 3, COL_AQ)
            load_w_in(G_CQ, 2, COL_CQ)
            for j in range(4):
                load(STEP_UQ + j, w_uq[:, :, 384 * j:384 * j + 384], part=slice(0, 4 * 384))
            for j in range(2):
                load(STEP_UK + j, w_uk[:, :, 512 * j:512 * j + 512])
            for j in range(2):
                load(STEP_UV + j, w_uv[:, :, 512 * j:512 * j + 512])
            load_w_in(G_MG, 8, COL_MG)
            load_w_in(G_GATE, 2, COL_AGATE)
            load_w_in(G_GATE + 4, 2, COL_BGATE)
            with sp.Fori(0, 4) as it:
                for j in range(4):
                    w = (w_oa, w_ob)[j % 2]
                    load(STEP_Y + j, w[:, :, bass.ds(it * 512 + 256 * (j // 2), 256)], it)
            with sp.Fori(0, 4) as it:
                for j in range(4):
                    load(STEP_OUT + j, w_out[:, KH * (j % 2):KH * (j % 2) + KH,
                                             bass.ds(it * 512 + 256 * (j // 2), 256)], it)
            for tt, (t0, n) in enumerate(TOK):
                sp.wait_ge(h_ready, tt + 1)
                dst = d["y_sample"] if tt == 0 else d["y_prompt"][t0 - DEC:t0 - DEC + n, :]
                sp.dma_start(dst, h_tok[0:n, tt, :]).then_inc(y_out, 16)
            sp.wait_ge(y_out, 48)

        @block.gpsimd
        def _(pool):
            pool.memset(ones[:], 1.0).then_inc(ones_set, 1)
            pool.dma_start(ident[:], d["ident"]).then_inc(consts_landed, 16)
            pool.dma_start(norm_g[:], d["norm_g"]).then_inc(consts_landed, 16)
            pool.dma_start(rope_tab[:], d["rope_tab"].rearrange("c p t -> p c t")).then_inc(consts_landed, 16)
            for b, name in enumerate(("q_norm_g", "kv_norm_g")):
                pool.dma_start(lora_g[:, b, :], d[name]).then_inc(consts_landed, 16)
            pool.dma_start(k_past[:], rows(d["cache_a_k"], 2)).then_inc(past_landed, 16)
            for dup in range(2):
                pool.dma_start(idx_past[:, :, IDX_DIM * dup:IDX_DIM * dup + IDX_DIM],
                               rows(d["cache_idx_k"], 2)).then_inc(past_landed, 16)
                pool.dma_start(kr_past[:, :, ROPE * dup:ROPE * dup + ROPE],
                               rows(d["cache_mla_krope"], 2)).then_inc(past_landed, 16)
            pool.wait_ge(xt_ready, KD)
            pool.dma_start(va_past[:], rows(d["cache_a_v"], 2)).then_inc(va_landed, 16)
            pool.wait_ge(tr_copied, 7)
            for tt, (t0, n) in enumerate(TOK):
                def out(name):
                    return d[name + "_sample"] if tt == 0 else d[name + "_prompt"][t0 - DEC:t0 - DEC + n, :]
                pool.dma_start(out("new_a_k"), kv_tok[0:n, tt, 0:256]).then_inc(kv_out, 16)
                pool.dma_start(out("new_a_v"), kv_tok[0:n, tt, 256:512]).then_inc(kv_out, 16)
                pool.dma_start(out("new_idx_k"), ik_tok[0:n, tt, 0:IDX_DIM]).then_inc(kv_out, 16)
                pool.dma_start(out("new_krope"), kr_tok[0:n, tt, :]).then_inc(kv_out, 16)
            pool.dma_start(ckv_past[:], rows(d["cache_mla_ckv"], 2)).then_inc(ckv_past_landed, 16)
            pool.wait_ge(tok_copied, 3)
            for tt, (t0, n) in enumerate(TOK):
                dst = d["new_ckv_sample"] if tt == 0 else d["new_ckv_prompt"][t0 - DEC:t0 - DEC + n, :]
                pool.dma_start(dst, ckv_tok[0:n, tt, :]).then_inc(ckv_out, 16)
            pool.wait_ge(m_done, 8)
            for tt, (t0, n) in enumerate(TOK):
                src = d["x_sample"] if tt == 0 else d["x_prompt"][t0 - DEC:t0 - DEC + n, :]
                pool.dma_start(h_tok[0:n, tt, :], src).then_inc(res_landed, 16)
            pool.dma_start(final_g[:], d["final_g"].rearrange("(a n) -> a n", a=1).partition_broadcast(P))\
                .then_inc(fg_landed, 16)
            pool.wait_ge(kv_out, 12 * 16)
            pool.wait_ge(ckv_out, 48)

        @block.tensor
        def _(pe):
            def three(out, hi, lo, x_h, x_l, first, last):
                nc.tensor.matmul(out, hi, x_h, start=first, stop=False)
                nc.tensor.matmul(out, hi, x_l, start=False, stop=False)
                return nc.tensor.matmul(out, lo, x_h, start=False, stop=last)

            def weights(step, k):
                cols = 1536 if STEP_UQ <= step < STEP_UK else 2048
                return [w[:, step % 2, 0:cols].rearrange("p (k n) -> p k n", k=k) for w in (w_hi, w_lo)]

            def half_group(step, group, half, x_h, x_l, it=0):
                pe.wait_ge(lo_done, step + 1 + RAW * it)
                hi, lo = weights(step, KH)
                for m in range(2):
                    for k in range(KH):
                        cols = slice(m * P, (m + 1) * P)
                        last = three(pair(group)[:, m, :], hi[:, k, cols], lo[:, k, cols], x_h[:, KH * half + k, :],
                                     x_l[:, KH * half + k, :], half == 0 and k == 0, half == 1 and k == KH - 1)
                last.then_inc(step_done, 1)

            def w_in_group(group, it=0):
                if group >= 2:
                    pe.wait_ge(pair_read, group - 1 + 2 * it)
                for half in range(2):
                    half_group(steps_of(group) + half, group, half, x_hi, x_lo, it)

            def w_in_groups(group, turns):
                with pe.Fori(0, turns) as it:
                    for j in range(2):
                        w_in_group(group + j, it)

            pe.wait_ge(consts_landed, 80)
            pe.wait_ge(xn_done, 3)
            for k in range(KD):
                if k >= 8:
                    pe.wait_ge(xlo_done, k - 7)
                for tt, (t0, n) in enumerate(TOK):
                    last = nc.tensor.transpose(ps[:, k % 8, t0:t0 + n], x_tok[0:n, tt, k * P:(k + 1) * P],
                                               ident[0:n, 0:n])
                last.then_inc(xt_ready, 1)
            pe.wait_ge(xlo_done, KD)
            w_in_group(G_SMALL)
            w_in_groups(G_IQ, 5)

            pe.wait_ge(past_landed, 80)
            for g in range(A_KV):
                for t in range(2):
                    last = nc.tensor.transpose(ps[:, 4, (2 * g + t) * P:(2 * g + t + 1) * P],
                                               k_past[:, t, g * P:(g + 1) * P], ident[:])
            last.then_inc(tr_ready, 1)
            for i, past in enumerate((idx_past, kr_past)):
                for t in range(2):
                    last = nc.tensor.transpose(ps[:, 5, (2 * i + t) * P:(2 * i + t + 1) * P], past[:, t, :], ident[:])
            last.then_inc(tr_ready, 1)
            pe.wait_ge(roped, 2)
            for tt, (t0, n) in enumerate(TOK):
                last = nc.tensor.transpose(ps[0:n, 6, tt * P:(tt + 1) * P], ik_z[:, t0:t0 + n], ident[:])
            last.then_inc(tr_ready, 1)
            for tt, (t0, n) in enumerate(TOK):
                last = nc.tensor.transpose(ps[0:n, 7, tt * ROPE:(tt + 1) * ROPE], kr_t[0:ROPE, 0, NEW + t0:NEW + t0 + n],
                                           ident[0:ROPE, 0:ROPE])
            last.then_inc(tr_ready, 1)
            pe.wait_ge(roped, 2 + G_AK)
            pe.wait_ge(pair_read, G_AV + 1)
            for tt, (t0, n) in enumerate(TOK):
                pe.wait_ge(tr_copied, tt + 1)
                for g in range(A_KV):
                    nc.tensor.transpose(ps[0:n, 4 + tt, g * P:(g + 1) * P], ka_t[:, g, NEW + t0:NEW + t0 + n], ident[:])
                    last = nc.tensor.transpose(ps[0:n, 4 + tt, (2 + g) * P:(3 + g) * P],
                                               z_stage[:, G_AV % 2, g, t0:t0 + n], ident[:])
                last.then_inc(tr_ready, 1)

            pe.wait_ge(tr_copied, 7)
            for u, (tt, heads) in enumerate(IDX_UNITS):
                if u >= 4:
                    pe.wait_ge(relu_done, u - 3)
                (t0, n), (k0, nk) = TOK[tt], KEYS[tt]
                for i, h in enumerate(heads):
                    last = nc.tensor.matmul(ps[0:n, 4 + u % 4, i * nk:(i + 1) * nk], iq_t[:, h // 2, t0:t0 + n],
                                            ik_t[:, h % 2, k0:k0 + nk], start=True, stop=True)
                last.then_inc(idx_ready, 1)

            w_in_groups(G_CQ, 2)

            pe.wait_ge(ones_set, 1)
            pe.wait_ge(relu_done, len(IDX_UNITS))
            for b in range(2):
                pe.wait_ge(sq_done, b + 1)
                for k in range(KL):
                    last = nc.tensor.matmul(ps[:, 4 + b, 0:NTOK], ones[:], sq_z[:, b, k, :],
                                            start=k == 0, stop=k == KL - 1)
                last.then_inc(sumsq_ready, 1)
            pe.wait_ge(ckv_past_landed, 16)
            for b in range(2):
                for k in range(2):
                    for t in range(2):
                        last = nc.tensor.transpose(ps[:, 6 + b, (2 * k + t) * P:(2 * k + t + 1) * P],
                                                   ckv_past[:, t, (2 * b + k) * P:(2 * b + k + 1) * P], ident[:])
                last.then_inc(past_lat_ready, 1)
            pe.wait_ge(lat_normed, 2 * KL)
            pe.wait_ge(past_lat_lo, 1)
            for tt, (t0, n) in enumerate(TOK):
                for k in range(KL):
                    last = nc.tensor.transpose(ps[0:n, 4 + tt, k * P:(k + 1) * P], lora_z[:, 1, k, t0:t0 + n], ident[:])
                last.then_inc(tok_ready, 1)

            def scores(u):
                branch, kind, h = UNITS[u]
                (t0, n), (k0, nk), bank = TOK[kind], KEYS[kind], 4 + u % 2
                if u >= 2:
                    pe.wait_ge(scores_read if UNITS[u - 2][0] == "A" else p_ready, u - 1)
                for i, hh in enumerate(range(4 * h, 4 * h + 4) if kind == 0 else [h]):
                    out = ps[n * i:n * i + n, bank, 0:nk]
                    if branch == "A":
                        last = nc.tensor.matmul(out, aq_t[:, hh, t0:t0 + n], ka_t[:, hh // GRP, k0:k0 + nk],
                                                start=True, stop=True)
                    else:
                        nc.tensor.matmul(out, qn_t[:, hh, t0:t0 + n], kb_t[:, hh, k0:k0 + nk], start=True, stop=False)
                        last = nc.tensor.matmul(out, qr_t[:, hh // 2, t0:t0 + n], kr_t[:, hh % 2, k0:k0 + nk],
                                                start=False, stop=True)
                last.then_inc(scores_ready, 1)

            def turn_probs(u):
                pe.wait_ge(pn_ready, u + 1)
                if u >= 1:
                    pe.wait_ge(pt_copied, u)
                for j, (off, nk, _) in enumerate(KEY_TILES[UNITS[u][1]]):
                    last = nc.tensor.transpose(ps[0:nk, 6, j * P:(j + 1) * P], probs[:, u % 2, off:off + nk], ident[:])
                last.then_inc(pt_ready, 1)

            def values(u):
                branch, kind, h = UNITS[u]
                pe.wait_ge(pt_copied, u + 1)
                if u >= 1:
                    pe.wait_ge(o_copied, u)
                tiles = KEY_TILES[kind]
                heads = range(4 * h, 4 * h + 4) if branch == "B" and kind == 0 else [h]
                width = P // len(heads)
                for i, hh in enumerate(heads):
                    for j, (_, nk, t) in enumerate(tiles):
                        if branch == "B":
                            v = vb[0:nk, t, hh * P:(hh + 1) * P]
                        else:
                            g = h if kind == 0 else h // GRP
                            v = va_past[:, t, g * P:(g + 1) * P] if t < 2 else \
                                kv_tok[0:nk, t - 2, (2 + g) * P:(3 + g) * P]
                        last = nc.tensor.matmul(ps[:, 7, width * i:width * (i + 1)], v,
                                                probs_t[0:nk, u % 2, j, width * i:width * (i + 1)],
                                                start=j == 0, stop=j == len(tiles) - 1)
                last.then_inc(o_ready, 1)

            def attention(first, end):
                scores(first)
                for u in range(first, end):
                    if u + 1 < end:
                        scores(u + 1)
                    turn_probs(u)
                    if u > first:
                        values(u - 1)
                values(end - 1)

            pe.wait_ge(tok_copied, 3)
            pe.wait_ge(past_lat_lo, 2)
            pe.wait_ge(va_landed, 16)
            attention(0, N_A)

            pe.wait_ge(pair_read, G_MG)
            for j in range(4):
                step = STEP_UQ + j
                pe.wait_ge(lo_done, step + 1)
                hi, lo = weights(step, KL)
                for i in range(3):
                    n = 3 * j + i
                    if n >= 4:
                        pe.wait_ge(uq_copied, n - 3)
                    for k in range(KL):
                        cols = slice(i * P, (i + 1) * P)
                        last = three(ps[:, n % 4, 0:NTOK], hi[:, k, cols], lo[:, k, cols], cq_hi[:, k, :], cq_lo[:, k, :], k == 0, k == KL - 1)
                    last.then_inc(uq_ready, 1)
                pe.wait_ge(uq_ready, 3 * j + 3)
                pe.sem_inc(step_done, 1)
            for h in range(B_HEADS):
                step = STEP_UK + h // 4
                if h % 4 == 0:
                    pe.wait_ge(lo_done, step + 1)
                if h < 2:
                    pe.wait_ge(uq_copied, 12)
                else:
                    pe.wait_ge(uk_copied, h - 1)
                hi, lo = weights(step, KL)
                cols = slice((h % 4) * P, (h % 4 + 1) * P)
                for k in range(KL):
                    for half in range(2):
                        keys = slice(half * NKEY // 2, (half + 1) * NKEY // 2)
                        last = three(ps[:, 2 * (h % 2) + half, 0:NKEY // 2], hi[:, k, cols], lo[:, k, cols],
                                     ckv_hi[:, k, keys], ckv_lo[:, k, keys], k == 0, k == KL - 1)
                last.then_inc(uk_ready, 1)
                if h % 4 == 3:
                    pe.wait_ge(uk_ready, h + 1)
                    pe.sem_inc(step_done, 1)
            for n in range(10):
                step, w = STEP_UV + n // 5, n % 5
                if w == 0:
                    pe.wait_ge(lo_done, step + 1)
                if n < 4:
                    pe.wait_ge(uk_copied, B_HEADS)
                else:
                    pe.wait_ge(uv_copied, n - 3)
                hi, lo = weights(step, KL)
                keys = slice(V_TILES[w], V_TILES[w] + P)
                for k in range(KL):
                    nc.tensor.matmul(ps[:, n % 4, :], ckv_hi[:, k, keys], hi[:, k, :], start=k == 0, stop=False)
                    nc.tensor.matmul(ps[:, n % 4, :], ckv_hi[:, k, keys], lo[:, k, :], start=False, stop=False)
                    last = nc.tensor.matmul(ps[:, n % 4, :], ckv_lo[:, k, keys], hi[:, k, :],
                                            start=False, stop=k == KL - 1)
                last.then_inc(uv_ready, 1)
                if w == 4:
                    pe.wait_ge(uv_ready, n + 1)
                    pe.sem_inc(step_done, 1)

            pe.wait_ge(q_roped, 1)
            pe.wait_ge(uk_copied, B_HEADS)
            pe.wait_ge(uv_copied, 10)
            attention(N_A, len(UNITS))

            w_in_groups(G_MG, 8)
            w_in_groups(G_GATE, 4)

            def branch_out(step, group, b, it=0):
                pe.wait_ge(lo_done, step + 1 + RAW * it)
                if isinstance(it, int) and group == 0:
                    pe.wait_ge(pair_read, G_END)
                else:
                    pe.wait_ge(y_read, 2 * group + b - 1 + 4 * it)
                hi, lo = weights(step, KH)
                for m in range(2):
                    for k in range(KH):
                        cols = slice(m * P, (m + 1) * P)
                        last = three(ps[:, 2 * b + m, 0:NTOK], hi[:, k, cols], lo[:, k, cols], og_hi[:, 8 * b + k, :],
                                     og_lo[:, 8 * b + k, :], k == 0, k == KH - 1)
                last.then_inc(step_done, 1)

            pe.wait_ge(gate_used, G_END - G_MG)
            for j in range(4):
                branch_out(STEP_Y + j, j // 2, j % 2)
            with pe.Fori(0, 3) as it:
                for j in range(4, 8):
                    branch_out(STEP_Y + j, j // 2, j % 2, it)

            def out_group(j, it=0):
                for half in range(2):
                    step = STEP_OUT + 2 * j + half
                    if isinstance(it, int) and j == 0:
                        pe.wait_ge(m_done, 4 + 4 * half)
                        pe.wait_ge(y_read, 16)
                    elif half == 0 and not (isinstance(it, int) and j == 1):
                        pe.wait_ge(hT_copied, j - 1 + 2 * it)
                    half_group(step, j, half, m_hi, m_lo, it)

            def turn_out(j, it=0):
                pe.wait_ge(hT_copied, j + 1 + 2 * it)
                if not (isinstance(it, int) and j == 0):
                    pe.wait_ge(h_added, j + 2 * it)
                for tt, (t0, n) in enumerate(TOK):
                    for m in range(2):
                        last = nc.tensor.transpose(ps[0:n, 4 + tt, m * P:(m + 1) * P], h_stage[:, j % 2, m, t0:t0 + n],
                                                   ident[:])
                last.then_inc(ht_ready, 1)

            out_group(0)
            out_group(1)
            turn_out(0)
            with pe.Fori(0, 3) as it:
                for j in range(2, 4):
                    out_group(j, it)
                    turn_out(j - 1, it)
            turn_out(7)

        @block.scalar
        def _(act):
            def split_hi(step, it=0):
                act.wait_ge(raw_landed[step % RAW], landed(step, it))
                if step >= 2:
                    act.wait_ge(step_done, step - 1 + RAW * it)
                n = 1536 if STEP_UQ <= step < STEP_UK else 2048
                nc.scalar.copy(w_hi[:, step % 2, 0:n], raw[:, step % RAW, 0:n]).then_inc(hi_done, 1)

            def group_ready(group, it=0):
                act.wait_ge(step_done, steps_of(group) + 2 + RAW * it)

            for tt, (_, n) in enumerate(TOK):
                act.wait_ge(x_landed[tt], 16)
                if tt == 0:
                    act.wait_ge(ss_cleared, 1)
                if tt == 2:
                    act.wait_ge(ss_done, 1)
                nc.scalar.activation(x_sq[0:n, tt % 2, :], x_tok[0:n, tt, :], ACT.Square,
                                     accum_out=ss[0:n, tt:tt + 1]).then_inc(ss_done, 1)
            act.wait_ge(var_done, 1)
            nc.scalar.activation(root[:, 0:3], var[:, 0:3], ACT.Sqrt).then_inc(root_done, 1)
            split_hi(0)
            act.wait_ge(consts_landed, 80)
            for k in range(KD):
                act.wait_ge(xt_ready, k + 1)
                nc.scalar.activation(x_hi[:, k, :], ps[:, k % 8, 0:NTOK], ACT.Copy,
                                     scale=norm_g[:, k:k + 1]).then_inc(xhi_done, 1)
            split_hi(1)

            def to_stage(group, it=0):
                group_ready(group, it)
                if group >= 2:
                    act.wait_ge(stage_used, group - 1 + 2 * it)
                nc.scalar.copy(z_stage[:, group % 2, :, :], pair(group)).then_inc(pair_read, 1)

            for half in range(2):
                split_hi(2 + half)
            group_ready(G_SMALL)
            for a, b in ((0, 32), (32, 0)):
                nc.scalar.copy(kr_swap[a:a + 32, :], ps[b:b + 32, 1, 0:NTOK]).then_inc(small_copied, 1)
            to_stage(G_SMALL)
            for half in range(2):
                split_hi(4 + half)
            to_stage(1)
            with act.Fori(0, 4) as it:
                for j in range(3, 5):
                    for half in range(2):
                        split_hi(2 * j + half, it)
                    to_stage(j - 1, it)
            for half in range(2):
                split_hi(STEP_CQ + half)
            to_stage(G_AV)

            act.wait_ge(tr_ready, 1)
            nc.scalar.copy(ka_t[:, :, 0:PAST], ps[:, 4, :].rearrange("p (g t) -> p g t", g=2)).then_inc(tr_copied, 1)
            act.wait_ge(tr_ready, 2)
            for i, dst in enumerate((ik_t, kr_t)):
                for half in range(2):
                    rows64 = slice(64 * half, 64 * half + 64)
                    last = nc.scalar.copy(dst[rows64, half, 0:PAST], ps[rows64, 5, i * PAST:(i + 1) * PAST])
            last.then_inc(tr_copied, 1)
            for i, dst in enumerate((ik_tok, kr_tok)):
                act.wait_ge(tr_ready, 3 + i)
                width = dst.shape[2]
                nc.scalar.copy(dst[0:DEC, 0, :], ps[0:DEC, 6 + i, 0:width])
                nc.scalar.copy(dst[:, 1:3, :], ps[:, 6 + i, width:3 * width].rearrange("p (t n) -> p t n", t=2))\
                    .then_inc(tr_copied, 1)
            for tt, (_, n) in enumerate(TOK):
                act.wait_ge(tr_ready, 5 + tt)
                nc.scalar.copy(kv_tok[0:n, tt, :], ps[0:n, 4 + tt, :]).then_inc(tr_copied, 1)

            for u, (tt, heads) in enumerate(IDX_UNITS):
                act.wait_ge(idx_ready, u + 1)
                if u >= 4:
                    act.wait_ge(idx_added, u - 3)
                n, width = TOK[tt][1], KEYS[tt][1] * len(heads)
                nc.scalar.activation(relu_ring[0:n, u % 4, 0:width], ps[0:n, 4 + u % 4, 0:width], ACT.Relu,
                                     scale=IDX_DIM ** -0.5).then_inc(relu_done, 1)

            lat_tiles = lora_z[:].rearrange("p b k t -> p (b k) t")
            for g in range(G_CQ, G_MG):
                for half in range(2):
                    split_hi(2 * g + 2 + half)
                group_ready(g)
                nc.scalar.copy(lat_tiles[:, 2 * (g - G_CQ):2 * (g - G_CQ) + 2, :], pair(g)).then_inc(pair_read, 1)
                if g % 2 == 0:
                    b = (g - G_CQ) // 2
                    act.wait_ge(pair_read, g + 1)
                    nc.scalar.activation(sq_z[:, b, :, :], lora_z[:, b, :, :], ACT.Square).then_inc(sq_done, 1)
            for b in range(2):
                act.wait_ge(past_lat_ready, b + 1)
                if b == 0:
                    act.wait_ge(idx_added, len(IDX_UNITS))
                nc.scalar.copy(ckv_hi[:, 2 * b:2 * b + 2, 0:PAST],
                               ps[:, 6 + b, :].rearrange("p (k t) -> p k t", k=2)).then_inc(past_lat_hi, 1)
            act.wait_ge(lat_var_done, 1)
            nc.scalar.activation(lat_t[:], lat_var[:], ACT.Sqrt).then_inc(lat_root_done, 1)
            act.wait_ge(lat_normed, KL)
            nc.scalar.copy(cq_hi[:], lora_z[:, 0, :, :]).then_inc(lat_hi, 1)
            act.wait_ge(lat_normed, 2 * KL)
            nc.scalar.copy(ckv_hi[:, :, NEW:NKEY], lora_z[:, 1, :, :]).then_inc(lat_hi, 1)
            for tt, (_, n) in enumerate(TOK):
                act.wait_ge(tok_ready, tt + 1)
                nc.scalar.copy(ckv_tok[0:n, tt, :], ps[0:n, 4 + tt, :]).then_inc(tok_copied, 1)

            def exponentials(u):
                branch, kind, _ = UNITS[u]
                nk = KEYS[kind][1]
                act.wait_ge(neg_ready, u + 1)
                if u >= 2:
                    act.wait_ge(pt_ready, u - 1)
                src = masked[:, u % 2, 0:nk] if branch == "A" else ps[:, 4 + u % 2, 0:nk]
                nc.scalar.activation(probs[:, u % 2, 0:nk], src, ACT.Exp, bias=neg_mx[:, u % 2:u % 2 + 1],
                                     scale=A_SCALE if branch == "A" else B_SCALE,
                                     accum_out=sum_p[:, u % 2:u % 2 + 1]).then_inc(p_ready, 1)

            def copy_turned(u):
                act.wait_ge(pt_ready, u + 1)
                if u >= 2:
                    act.wait_ge(o_ready, u - 1)
                tiles = KEY_TILES[UNITS[u][1]]
                full = sum(nk == P for _, nk, _ in tiles)
                last = nc.scalar.copy(probs_t[:, u % 2, 0:full, :],
                                      ps[:, 6, 0:full * P].rearrange("p (j q) -> p j q", j=full))
                if full < len(tiles):
                    nk = tiles[full][1]
                    last = nc.scalar.copy(probs_t[0:nk, u % 2, full, :], ps[0:nk, 6, full * P:(full + 1) * P])
                last.then_inc(pt_copied, 1)

            def attention(first, end):
                exponentials(first)
                for u in range(first, end):
                    if u + 1 < end:
                        exponentials(u + 1)
                    copy_turned(u)

            attention(0, N_A)

            act.wait_ge(kv_out, 12 * 16)
            act.wait_ge(o_ready, N_A)
            for j in range(4):
                split_hi(STEP_UQ + 2 + j)
                for i in range(3):
                    n = 3 * j + i
                    act.wait_ge(uq_ready, n + 1)
                    if i < 2:
                        nc.scalar.copy(qn_t[:, 2 * j + i, :], ps[:, n % 4, 0:NTOK]).then_inc(uq_copied, 1)
                    else:
                        nc.scalar.copy(qr_z[:, j, :], ps[:, n % 4, 0:NTOK])
                        for a, b in ((0, 32), (32, 0), (64, 96), (96, 64)):
                            last = nc.scalar.copy(qr_swap[a:a + 32, j, :], ps[b:b + 32, n % 4, 0:NTOK])
                        last.then_inc(uq_copied, 1)
            for h in range(B_HEADS):
                act.wait_ge(uk_ready, h + 1)
                nc.scalar.copy(kb_t[:, h, :].rearrange("p (a t) -> p a t", a=2),
                               ps[:, 2 * (h % 2):2 * (h % 2) + 2, 0:NKEY // 2]).then_inc(uk_copied, 1)
                if h % 4 == 3:
                    split_hi(STEP_UV + h // 4)
            for half in range(2):
                split_hi(STEP_MG + half)
            attention(N_A, len(UNITS))

            def gate_stage_free(group, it):
                if not (isinstance(it, int) and group < G_MG + 2):
                    act.wait_ge(gate_used, group - G_MG - 1 + 2 * it)

            def merge_exp(group, it=0):
                group_ready(group, it)
                gate_stage_free(group, it)
                nc.scalar.activation(gate_e[:, group % 2, :, :], pair(group), ACT.Exp,
                                     scale=-1.0).then_inc(pair_read, 1)

            for half in range(2):
                split_hi(STEP_MG + 2 + half)
            act.wait_ge(o_copied, len(UNITS))
            merge_exp(G_MG)
            with act.Fori(0, 7) as it:
                for j in range(2, 4):
                    for half in range(2):
                        split_hi(STEP_MG + 2 * j + half, it)
                    merge_exp(G_MG + j - 1, it)
            for half in range(2):
                split_hi(STEP_GATE + half)
            merge_exp(G_GATE - 1)

            def gate_exp(group, it=0):
                group_ready(group, it)
                gate_stage_free(group, it)
                nc.scalar.copy(gate_x[:, group % 2, :, :], pair(group))
                nc.scalar.activation(gate_e[:, group % 2, :, :], pair(group), ACT.Exp,
                                     scale=-1.0).then_inc(pair_read, 1)

            for half in range(2):
                split_hi(STEP_GATE + 2 + half)
            gate_exp(G_GATE)
            with act.Fori(0, 3) as it:
                for j in range(2, 4):
                    for half in range(2):
                        split_hi(STEP_GATE + 2 * j + half, it)
                    gate_exp(G_GATE + j - 1, it)
            for half in range(2):
                split_hi(STEP_Y + half)
            gate_exp(G_END - 1)
            for half in range(2):
                split_hi(STEP_Y + 2 + half)
            with act.Fori(0, 3) as it:
                for j in range(4):
                    split_hi(STEP_Y + 4 + j, it)

            def to_h_stage(j):
                act.wait_ge(step_done, STEP_OUT + 2 * j + 2)
                if j >= 2:
                    act.wait_ge(ht_ready, j - 1)
                nc.scalar.copy(h_stage[:, j % 2, :, :], pair(j)).then_inc(hT_copied, 1)

            def squares(j):
                act.wait_ge(h_added, j + 1)
                for tt, (_, n) in enumerate(TOK):
                    if j + tt:
                        act.wait_ge(h_squared, 3 * j + tt)
                    nc.scalar.activation(h_sq[0:n, :], h_tok[0:n, tt, 256 * j:256 * j + 256], ACT.Square,
                                         accum_out=h_ss[0:n, tt, j:j + 1]).then_inc(h_squared, 1)

            for half in range(2):
                split_hi(STEP_OUT + half)
            act.wait_ge(m_done, 8)
            for j in range(1, 8):
                for half in range(2):
                    split_hi(STEP_OUT + 2 * j + half)
                to_h_stage(j - 1)
                if j >= 3:
                    squares(j - 3)
            squares(5)
            to_h_stage(7)
            squares(6)
            squares(7)
            act.wait_ge(h_var_done, 1)
            nc.scalar.activation(root[:, 0:3], var[:, 0:3], ACT.Sqrt).then_inc(h_root_done, 1)

        @block.vector
        def _(dve):
            own = Tally(dve_self)

            def settled(ins):
                dve.wait_ge(dve_self, own.add(ins))

            def split_lo(step, it=0):
                dve.wait_ge(hi_done, step + 1 + RAW * it)
                n = 1536 if STEP_UQ <= step < STEP_UK else 2048
                nc.vector.tensor_tensor(w_lo[:, step % 2, 0:n], raw[:, step % RAW, 0:n],
                                        w_hi[:, step % 2, 0:n].bitcast(F32), ALU.subtract).then_inc(lo_done, 1)

            def refine(r, v, t):
                settled(nc.vector.tensor_tensor(t, r, r, ALU.mult))
                settled(nc.vector.tensor_tensor(t, t, v, ALU.mult))
                settled(nc.vector.tensor_scalar(t, t, -0.5, 1.5, ALU.mult, ALU.add))
                settled(nc.vector.tensor_tensor(r, r, t, ALU.mult))

            nc.vector.memset(ss[:], 1.0).then_inc(ss_cleared, 1)
            dve.wait_ge(ss_done, 3)
            nc.vector.tensor_scalar(var[:, 0:3], ss[:, 0:3], 1.0 / D_MODEL, EPS, ALU.mult, ALU.add).then_inc(var_done, 1)
            dve.wait_ge(root_done, 1)
            settled(nc.vector.reciprocal(rstd[:, 0:3], root[:, 0:3]))
            refine(rstd[:, 0:3], var[:, 0:3], newton[:, 0:3])
            for tt, (_, n) in enumerate(TOK):
                nc.vector.tensor_scalar(x_tok[0:n, tt, :], x_tok[0:n, tt, :], rstd[0:n, tt:tt + 1], None,
                                        ALU.mult).then_inc(xn_done, 1)
            split_lo(0)
            for k in range(KD):
                dve.wait_ge(xhi_done, k + 1)
                nc.vector.scalar_tensor_tensor(out=x_lo[:, k, :], in0=ps[:, k % 8, 0:NTOK], scalar=norm_g[:, k:k + 1],
                                               in1=x_hi[:, k, :].bitcast(F32), op0=ALU.mult,
                                               op1=ALU.subtract).then_inc(xlo_done, 1)
            split_lo(1)

            def table(i, like):
                return rope_tab[:, i:i + 1, :].broadcast_to(like)

            def rotate(group, dst, kind, mask):
                shape = [P, 2, NTOK]
                dve.wait_ge(pair_read, group + 1)
                z = z_stage[:, group % 2, :, :]
                settled(nc.vector.stream_shuffle(z_shuf[:], z, mask))
                nc.vector.tensor_tensor(z_cos[:], z, table(2 * kind, shape), ALU.mult).then_inc(stage_used, 1)
                settled(nc.vector.tensor_tensor(z_shuf[:], z_shuf[:], table(2 * kind + 1, shape), ALU.mult))
                dve.wait_ge(stage_used, group + 1)
                nc.vector.tensor_tensor(dst, z_cos[:], z_shuf[:], ALU.add).then_inc(roped, 1)
                dve.wait_ge(roped, group + 2)

            for half in range(2):
                split_lo(2 + half)
            dve.wait_ge(xt_ready, KD)
            for t in (ik_t, kr_t):
                for half in range(2):
                    nc.vector.memset(t[64 * (1 - half):64 * (1 - half) + 64, half, :], 0.0)
            dve.wait_ge(pair_read, 1)
            z, zk = z_stage[:, 0, 0, :], z_stage[0:ROPE, 0, 1, :]
            settled(nc.vector.stream_shuffle(z_shuf[0:64, 0, :], z[0:64, :], SWAP_8))
            settled(nc.vector.tensor_copy(ik_z[64:P, :], z[64:P, :]))
            settled(nc.vector.tensor_tensor(z_cos[0:64, 0, :], z[0:64, :], rope_tab[0:64, 2, :], ALU.mult))
            settled(nc.vector.tensor_tensor(z_shuf[0:64, 0, :], z_shuf[0:64, 0, :], rope_tab[0:64, 3, :], ALU.mult))
            settled(nc.vector.tensor_tensor(ik_z[0:64, :], z_cos[0:64, 0, :], z_shuf[0:64, 0, :], ALU.add))
            for half in range(2):
                settled(nc.vector.tensor_copy(ik_t[64 * half:64 * half + 64, half, NEW:NKEY], ik_z[0:64, :]))
            settled(nc.vector.tensor_tensor(z_cos[0:ROPE, 1, :], zk, rope_tab[0:ROPE, 4, :], ALU.mult))
            dve.wait_ge(small_copied, 2)
            settled(nc.vector.tensor_tensor(z_shuf[0:ROPE, 1, :], kr_swap[0:ROPE, :], rope_tab[0:ROPE, 5, :], ALU.mult))
            for half in range(2):
                if half == 1:
                    nc.vector.sem_inc(stage_used, 1)
                settled(nc.vector.tensor_tensor(kr_t[64 * half:64 * half + 64, half, NEW:NKEY], z_cos[0:ROPE, 1, :],
                                                z_shuf[0:ROPE, 1, :], ALU.add))
            nc.vector.sem_inc(roped, 2)
            for g in range(G_IQ, G_AV):
                for half in range(2):
                    split_lo(2 * g + 2 + half)
                if g < G_AQ:
                    rotate(g, iq_t[:, 2 * (g - G_IQ):2 * (g - G_IQ) + 2, :], 1, SWAP_8)
                elif g < G_AK:
                    rotate(g, aq_t[:, 2 * (g - G_AQ):2 * (g - G_AQ) + 2, :], 0, SWAP_16)
                else:
                    rotate(g, ka_t[:, :, NEW:NKEY], 0, SWAP_16)
            for half in range(2):
                split_lo(STEP_CQ + half)

            dve.wait_ge(tr_copied, 3)
            settled(nc.vector.tensor_scalar(iw_tok[0:DEC, 0, :], ik_tok[0:DEC, 0, IDX_DIM:IDX_DIM + IDX_HEADS],
                                            IDX_HEADS ** -0.5, None, ALU.mult))
            settled(nc.vector.tensor_scalar(iw_tok[:, 1:3, :], ik_tok[:, 1:3, IDX_DIM:IDX_DIM + IDX_HEADS],
                                            IDX_HEADS ** -0.5, None, ALU.mult))
            begun = set()
            for u, (tt, heads) in enumerate(IDX_UNITS):
                dve.wait_ge(relu_done, u + 1)
                n, nk = TOK[tt][1], KEYS[tt][1]
                for i, h in enumerate(heads):
                    r, s = relu_ring[0:n, u % 4, i * nk:(i + 1) * nk], score[0:n, tt, 0:nk]
                    w = iw_tok[0:n, tt, h:h + 1]
                    if tt not in begun:
                        ins = nc.vector.tensor_scalar(s, r, w, None, ALU.mult)
                        begun.add(tt)
                    else:
                        ins = nc.vector.scalar_tensor_tensor(out=s, in0=r, scalar=w, in1=s, op0=ALU.mult, op1=ALU.add)
                    if i < len(heads) - 1:
                        settled(ins)
                ins.then_inc(idx_added, 1)
                dve.wait_ge(idx_added, u + 1)
            for tt in (1, 2):
                settled(nc.vector.memset(score[0:CHUNK, tt, KEYS[tt][1] - CHUNK:KEYS[tt][1]], TAKEN))

            def take_eight(tt, r):
                n, nk = TOK[tt][1], KEYS[tt][1]
                src = score if r == 0 else work
                settled(nc.vector.max(top8[0:n, 0, :], src[0:n, tt, 0:nk]))
                settled(nc.vector.match_replace(work[0:n, tt, 0:nk], top8[0:n, 0, :], src[0:n, tt, 0:nk], TAKEN))

            def selection(tt):
                n, nk = TOK[tt][1], KEYS[tt][1]
                w = work[0:n, tt, 0:nk]
                settled(nc.vector.tensor_tensor(w, w, score[0:n, tt, 0:nk], ALU.not_equal))
                settled(nc.vector.tensor_scalar(w, w, -1.0, -NEG, ALU.add, ALU.mult))

            rounds = [(1, r) for r in range(TOPK_PROMPT // 8)] + [(2, r) for r in range(TOPK_PROMPT // 8)] \
                + [(0, r) for r in range(TOPK_SAMPLE // 8)]
            n_steps = STEP_UQ - STEP_CQ
            for i in range(n_steps):
                split_lo(STEP_CQ + 2 + i)
                for tt, r in rounds[i * len(rounds) // n_steps:(i + 1) * len(rounds) // n_steps]:
                    take_eight(tt, r)
            for tt in range(3):
                selection(tt)
            for q in range(1, 4):
                settled(nc.vector.tensor_copy(work[DEC * q:DEC * q + DEC, 0, :], work[0:DEC, 0, :]))

            for b in range(2):
                dve.wait_ge(sumsq_ready, b + 1)
                last = nc.vector.tensor_scalar(lat_var[:, b, :], ps[:, 4 + b, 0:NTOK], 1.0 / LORA, EPS, ALU.mult, ALU.add)
            last.then_inc(lat_var_done, 1)
            for b in range(2):
                dve.wait_ge(past_lat_hi, b + 1)
                cols = slice(2 * b, 2 * b + 2)
                nc.vector.tensor_tensor(ckv_lo[:, cols, 0:PAST], ps[:, 6 + b, :].rearrange("p (k t) -> p k t", k=2),
                                        ckv_hi[:, cols, 0:PAST].bitcast(F32), ALU.subtract).then_inc(past_lat_lo, 1)
            dve.wait_ge(lat_root_done, 1)
            settled(nc.vector.reciprocal(lat_r[:], lat_t[:]))
            refine(lat_r[:], lat_var[:], lat_t[:])
            for b in range(2):
                for k in range(KL):
                    nc.vector.scalar_tensor_tensor(out=lora_z[:, b, k, :], in0=lora_z[:, b, k, :],
                                                   scalar=lora_g[:, b, k:k + 1], in1=lat_r[:, b, :], op0=ALU.mult,
                                                   op1=ALU.mult).then_inc(lat_normed, 1)
            dve.wait_ge(lat_normed, 2 * KL)
            dve.wait_ge(lat_hi, 1)
            nc.vector.tensor_tensor(cq_lo[:], lora_z[:, 0, :, :], cq_hi[:].bitcast(F32), ALU.subtract).then_inc(lat_lo, 1)
            dve.wait_ge(lat_hi, 2)
            nc.vector.tensor_tensor(ckv_lo[:, :, NEW:NKEY], lora_z[:, 1, :, :], ckv_hi[:, :, NEW:NKEY].bitcast(F32),
                                    ALU.subtract).then_inc(lat_lo, 1)

            def row_max(u):
                branch, kind, _ = UNITS[u]
                nk, bank, i = KEYS[kind][1], 4 + u % 2, u % 2
                dve.wait_ge(scores_ready, u + 1)
                if branch == "A":
                    nc.vector.tensor_tensor_reduce(out=masked[:, i, 0:nk], in0=ps[:, bank, 0:nk], in1=work[:, kind, 0:nk],
                                                   scale=1.0, scalar=TAKEN, op0=ALU.add, op1=ALU.max,
                                                   accum_out=mx[:, i:i + 1]).then_inc(scores_read, 1)
                    dve.wait_ge(scores_read, u + 1)
                else:
                    if kind:
                        settled(nc.vector.memset(ps[0:CHUNK, bank, nk - CHUNK:nk], NEG))
                    settled(nc.vector.tensor_reduce(mx[:, i:i + 1], ps[:, bank, 0:nk], AX_X, ALU.max))
                nc.vector.tensor_scalar(neg_mx[:, i:i + 1], mx[:, i:i + 1], -(A_SCALE if branch == "A" else B_SCALE),
                                        None, ALU.mult).then_inc(neg_ready, 1)

            def normalise(u):
                nk, i = KEYS[UNITS[u][1]][1], u % 2
                dve.wait_ge(p_ready, u + 1)
                settled(nc.vector.reciprocal(inv_p[:, i:i + 1], sum_p[:, i:i + 1]))
                nc.vector.tensor_scalar(probs[:, i, 0:nk], probs[:, i, 0:nk], inv_p[:, i:i + 1], None,
                                        ALU.mult).then_inc(pn_ready, 1)

            def copy_out(u):
                branch, kind, h = UNITS[u]
                t0, n = TOK[kind]
                base = 0 if branch == "A" else 8
                dve.wait_ge(o_ready, u + 1)
                if kind == 0:
                    ins = nc.vector.tensor_copy(o_t[:, base + 4 * h:base + 4 * h + 4, 0:DEC],
                                                ps[:, 7, 0:P].rearrange("p (h t) -> p h t", h=4))
                else:
                    ins = nc.vector.tensor_copy(o_t[:, base + h, t0:t0 + n], ps[:, 7, 0:P])
                ins.then_inc(o_copied, 1)

            def attention(first, end):
                row_max(first)
                for u in range(first, end):
                    if u + 1 < end:
                        row_max(u + 1)
                    normalise(u)
                    if u > first:
                        copy_out(u - 1)
                copy_out(end - 1)

            attention(0, N_A)
            for j in range(2, 5):
                split_lo(STEP_UQ + j)
            dve.wait_ge(uq_copied, 12)
            shape = [P, 4, NTOK]
            settled(nc.vector.tensor_tensor(qr_z[:], qr_z[:], table(4, shape), ALU.mult))
            settled(nc.vector.tensor_tensor(qr_swap[:], qr_swap[:], table(5, shape), ALU.mult))
            nc.vector.tensor_tensor(qr_t[:], qr_z[:], qr_swap[:], ALU.add).then_inc(q_roped, 1)
            for j in range(3):
                split_lo(STEP_UK + 1 + j)
            dve.wait_ge(q_roped, 1)
            dve.wait_ge(ckv_out, 48)
            for n in range(10):
                dve.wait_ge(uv_ready, n + 1)
                nc.vector.tensor_copy(vb[:, n % 5, 512 * (n // 5):512 * (n // 5) + 512], ps[:, n % 4, :])\
                    .then_inc(uv_copied, 1)
            for half in range(2):
                split_lo(STEP_MG + half)
            attention(N_A, len(UNITS))

            def merge_sigmoid(group, it=0):
                dve.wait_ge(pair_read, group + 1 + 2 * it)
                e = gate_e[:, group % 2, :, :]
                settled(nc.vector.tensor_scalar(e, e, 1.0, None, ALU.add))
                settled(nc.vector.reciprocal(e, e))
                nc.vector.tensor_copy(merge_g[:, bass.ds(it * 4 + 2 * (group - G_MG), 2), :], e)\
                    .then_inc(gate_used, 1)

            for half in range(2):
                split_lo(STEP_MG + 2 + half)
            merge_sigmoid(G_MG)
            with dve.Fori(0, 7) as it:
                own.enter(it, 4)
                for j in range(2, 4):
                    for half in range(2):
                        split_lo(STEP_MG + 2 * j + half, it)
                    merge_sigmoid(G_MG + j - 1, it)
            own.leave(7)
            for half in range(2):
                split_lo(STEP_GATE + half)
            merge_sigmoid(G_GATE - 1)

            def gated(group, it=0):
                dve.wait_ge(pair_read, group + 1 + 2 * it)
                e, x = gate_e[:, group % 2, :, :], gate_x[:, group % 2, :, :]
                tiles = bass.ds(it * 4 + 2 * (group - G_GATE), 2)
                settled(nc.vector.tensor_scalar(e, e, 1.0, None, ALU.add))
                settled(nc.vector.reciprocal(e, e))
                settled(nc.vector.tensor_tensor(x, x, e, ALU.mult))
                settled(nc.vector.tensor_tensor(x, x, o_t[:, tiles, :], ALU.mult))
                settled(nc.vector.tensor_copy(og_hi[:, tiles, :], x))
                nc.vector.tensor_tensor(og_lo[:, tiles, :], x, og_hi[:, tiles, :].bitcast(F32),
                                        ALU.subtract).then_inc(gate_used, 1)

            for half in range(2):
                split_lo(STEP_GATE + 2 + half)
            gated(G_GATE)
            with dve.Fori(0, 3) as it:
                own.enter(it, 10)
                for j in range(2, 4):
                    for half in range(2):
                        split_lo(STEP_GATE + 2 * j + half, it)
                    gated(G_GATE + j - 1, it)
            own.leave(3)
            for half in range(2):
                split_lo(STEP_Y + half)
            gated(G_END - 1)

            def merge_a(j, it=0):
                dve.wait_ge(step_done, STEP_Y + 2 * j + 1 + RAW * it)
                settled(nc.vector.tensor_tensor(y_a[:], ps[:, 0:2, 0:NTOK], merge_g[:, bass.ds(it * 4 + 2 * j, 2), :],
                                                ALU.mult))
                nc.vector.sem_inc(y_read, 1)

            def merge_b(j, it=0):
                dve.wait_ge(step_done, STEP_Y + 2 * j + 2 + RAW * it)
                tiles = bass.ds(it * 4 + 2 * j, 2)
                nc.vector.tensor_tensor(y_b[:], ps[:, 2:4, 0:NTOK], merge_g[:, bass.ds(it * 4 + 16 + 2 * j, 2), :],
                                        ALU.mult).then_inc(y_read, 1)
                dve.wait_ge(y_read, 2 * j + 2 + 4 * it)
                settled(nc.vector.tensor_tensor(y_a[:], y_a[:], y_b[:], ALU.add))
                settled(nc.vector.tensor_copy(m_hi[:, tiles, :], y_a[:]))
                nc.vector.tensor_tensor(m_lo[:, tiles, :], y_a[:], m_hi[:, tiles, :].bitcast(F32),
                                        ALU.subtract).then_inc(m_done, 1)
                dve.wait_ge(m_done, j + 1 + 2 * it)

            merge_a(0)
            split_lo(STEP_Y + 2)
            merge_b(0)
            split_lo(STEP_Y + 3)
            merge_a(1)
            with dve.Fori(0, 3) as it:
                own.enter(it, 6)
                for j in range(2, 4):
                    split_lo(STEP_Y + 2 * j, it)
                    merge_b(j - 1, it)
                    split_lo(STEP_Y + 2 * j + 1, it)
                    merge_a(j, it)
            own.leave(3)
            split_lo(STEP_OUT)
            merge_b(7)
            split_lo(STEP_OUT + 1)

            def add_residual(j):
                dve.wait_ge(ht_ready, j + 1)
                for tt, (_, n) in enumerate(TOK):
                    h = h_tok[0:n, tt, 256 * j:256 * j + 256]
                    last = nc.vector.tensor_tensor(h, h, ps[0:n, 4 + tt, 0:256], ALU.add)
                last.then_inc(h_added, 1)

            for half in range(2):
                split_lo(STEP_OUT + 2 + half)
            nc.vector.memset(h_ss[:], 1.0).then_inc(h_cleared, 1)
            dve.wait_ge(res_landed, 48)
            for j in range(2, 8):
                for half in range(2):
                    split_lo(STEP_OUT + 2 * j + half)
                add_residual(j - 2)
            add_residual(6)
            add_residual(7)

            dve.wait_ge(h_squared, 24)
            settled(nc.vector.tensor_reduce(ss[:, 0:3], h_ss[:], AX_X, ALU.add))
            nc.vector.tensor_scalar(var[:, 0:3], ss[:, 0:3], 1.0 / D_MODEL, EPS, ALU.mult, ALU.add)\
                .then_inc(h_var_done, 1)
            dve.wait_ge(h_root_done, 1)
            settled(nc.vector.reciprocal(rstd[:, 0:3], root[:, 0:3]))
            refine(rstd[:, 0:3], var[:, 0:3], newton[:, 0:3])
            dve.wait_ge(fg_landed, 16)
            for tt, (_, n) in enumerate(TOK):
                nc.vector.scalar_tensor_tensor(out=h_tok[0:n, tt, :], in0=h_tok[0:n, tt, :], scalar=rstd[0:n, tt:tt + 1],
                                               in1=final_g[0:n, :], op0=ALU.mult, op1=ALU.mult).then_inc(h_ready, 1)


def rope_tables():
    pos = np.concatenate([PAST + np.arange(DEC), np.arange(SEQ)]).astype(np.float32)
    tables = np.zeros((6, P, NTOK), np.float32)
    for kind, (width, rot) in enumerate(((A_DIM, A_DIM // 4), (IDX_DIM, IDX_DIM // 4), (ROPE, ROPE))):
        half = rot // 2
        freq = (np.float32(ROPE_THETA) ** (-np.arange(half, dtype=np.float32) * np.float32(2.0 / rot))).astype(np.float32)
        angle = (freq[:, None] * pos[None, :]).astype(np.float32)
        tables[2 * kind] = 1.0
        for start in range(0, P, width):
            tables[2 * kind, start:start + half] = np.cos(angle)
            tables[2 * kind, start + half:start + rot] = np.cos(angle)
            tables[2 * kind + 1, start:start + half] = -np.sin(angle)
            tables[2 * kind + 1, start + half:start + rot] = np.sin(angle)
    return tables


OUTPUTS = [("y_prompt", (SEQ, D_MODEL)), ("y_sample", (DEC, D_MODEL))] + [
    (f"{name}_{part}", (n, width)) for part, n in (("prompt", SEQ), ("sample", DEC))
    for name, width in (("new_a_k", 256), ("new_a_v", 256), ("new_idx_k", IDX_DIM), ("new_ckv", LORA),
                        ("new_krope", ROPE))]
SHAPES = [(1, SEQ, D_MODEL), (1, DEC, D_MODEL)] + [
    (1, 1, n, *width) for n in (SEQ, DEC)
    for width in ((A_KV, A_DIM), (A_KV, A_DIM), (IDX_DIM,), (LORA,), (ROPE,))]


def kernel(**inputs):
    import concourse.bacc as bacc
    from concourse.bass_utils import run_bass_kernel_spmd

    flat = {
        "x_prompt": (SEQ, D_MODEL), "x_sample": (DEC, D_MODEL), "cache_a_k": (PAST, 256), "cache_a_v": (PAST, 256),
        "cache_idx_k": (PAST, IDX_DIM), "cache_mla_ckv": (PAST, LORA), "cache_mla_krope": (PAST, ROPE),
        "norm_g": (D_MODEL,), "w_in": (D_MODEL, PROJ), "w_uq": (LORA, 1536), "q_norm_g": (LORA,),
        "kv_norm_g": (LORA,), "w_uk": (LORA, 1024), "w_uv": (LORA, 1024), "w_o_a": (1024, D_MODEL),
        "w_o_b": (1024, D_MODEL), "w_out": (D_MODEL, D_MODEL), "final_g": (D_MODEL,)}
    arrays = {f"in_{k}": np.ascontiguousarray(np.asarray(inputs[k]).reshape(s)) for k, s in flat.items()}
    uq = arrays["in_w_uq"].reshape(LORA, 4, 2, NOPE + ROPE)
    arrays["in_w_uq"] = np.concatenate([uq[..., :NOPE].reshape(LORA, 4, -1), uq[..., NOPE:].reshape(LORA, 4, -1)],
                                       axis=2).reshape(LORA, -1)
    for name in ("norm_g", "q_norm_g", "kv_norm_g"):
        arrays[f"in_{name}"] = np.ascontiguousarray(arrays[f"in_{name}"].reshape(-1, P).T)
    arrays["in_ident"] = np.eye(P, dtype=np.float32)
    arrays["in_rope_tab"] = rope_tables()

    nc = bacc.Bacc("TRN2", target_bir_lowering=False, num_devices=1)
    d = {k[3:]: nc.dram_tensor(k, a.shape, F32, kind="ExternalInput").ap() for k, a in arrays.items()}
    for name, shape in OUTPUTS:
        d[name] = nc.dram_tensor(f"out_{name}", shape, F32, kind="ExternalOutput").ap()
    hybrid_layer(nc, d)
    got = run_bass_kernel_spmd(nc, [arrays], core_ids=[0]).results[0]
    return tuple(got[f"out_{name}"].reshape(shape) for (name, _), shape in zip(OUTPUTS, SHAPES))
```

```python
from contextlib import ExitStack

import numpy as np

import concourse.bass as bass
from concourse import mybir

F32 = mybir.dt.float32
F32R = mybir.dt.float32r
ALU = mybir.AluOpType
ACT = mybir.ActivationFunctionType
AX_X = mybir.AxisListType.X

P = 128
D_MODEL = 2048
SEQ, DEC, PAST = 256, 32, 256
NTOK = DEC + SEQ
NKEY = PAST + NTOK
CHUNK = 64
EPS = 1e-6
ROPE_THETA = 500000.0
A_HEADS, A_KV, A_DIM = 8, 2, 128
GRP = A_HEADS // A_KV
IDX_HEADS, IDX_DIM = 16, 64
B_HEADS, NOPE, ROPE = 8, 128, 64
LORA = 512
KD = D_MODEL // P
KL = LORA // P
KH = KD // 2
TOPK_PROMPT = SEQ // 4
TOPK_SAMPLE = (PAST + DEC) // 4
NEG = -1e30
TAKEN = -3e38
A_SCALE = A_DIM ** -0.5
B_SCALE = (NOPE + ROPE) ** -0.5

COL_AQ, COL_AK, COL_AV, COL_AGATE, COL_IQ, COL_IK, COL_IW, COL_CQ, COL_CKV, COL_KR, COL_BGATE, COL_MG, PROJ = (
    0, 1024, 1280, 1536, 2560, 3584, 3648, 3664, 4176, 4688, 4752, 5776, 9872)

TOK = [(0, DEC), (DEC, P), (DEC + P, P)]
NEW = PAST
PROMPT = PAST + DEC

LAG_SPLIT = 3

DVE_LAST, ACT_LAST = (1, 0), 2

RAW = 4
G_SMALL, G_IQ, G_AK, G_AV, G_CQ, G_AQ, G_FILL_A, G_FILL_B, G_MG, G_GATE, G_END = 0, 1, 5, 6, 7, 11, 15, 19, 23, 31, 39
STEP_AK = 2 * G_AK
STEP_CQ = 2 * G_CQ
STEP_FILL_A = 2 * G_FILL_A
STEP_UQ = 2 * G_FILL_B
STEP_UK = STEP_UQ + 4
STEP_UV = STEP_UK + 2
STEP_FILL_B = STEP_UV + 2
LATE = STEP_FILL_B - STEP_UQ
STEP_MG = STEP_FILL_B + 8
STEP_GATE = STEP_MG + 16
STEP_Y = STEP_GATE + 16
STEP_OUT = STEP_Y + 16


def steps_of(group):
    return 2 * group + (LATE if group >= G_FILL_B else 0)


def merge_tile(group):
    return {G_FILL_A: 8, G_FILL_B: 0, G_MG: 16}[max(g for g in (G_FILL_A, G_FILL_B, G_MG) if g <= group)] \
        + 2 * (group - max(g for g in (G_FILL_A, G_FILL_B, G_MG) if g <= group))


class Tally:

    def __init__(self, sem):
        self.sem, self.n, self.it, self.per = sem, 0, None, 0

    def add(self, ins):
        ins.then_inc(self.sem, 1)
        self.n += 1
        return self.now()

    def now(self):
        return self.n if self.it is None else self.it * self.per + self.n

    def enter(self, it, per):
        self.it, self.per, self.start = it, per, self.n

    def leave(self, turns):
        assert self.n - self.start == self.per, (self.n - self.start, self.per)
        self.n, self.it = self.start + self.per * turns, None


def attention_units():
    units = []
    for g in range(A_KV):
        units.append(("A", 0, g))
        units += [("A", kind, h) for h in range(GRP * g, GRP * g + GRP) for kind in (1, 2)]
    for g in range(2):
        units.append(("B", 0, g))
        units += [("B", kind, h) for h in range(4 * g, 4 * g + 4) for kind in (1, 2)]
    return units


PIECES = 16


def pieces(turn, turns, filled):
    left = PIECES - filled
    return range(filled + turn * left // turns, filled + (turn + 1) * left // turns) if turn >= 0 else ()


UNITS = attention_units()
N_A = sum(u[0] == "A" for u in UNITS)
KEYS = [(0, PAST + DEC), (PROMPT, P), (PROMPT, 2 * P)]
KEY_TILES = [[(0, P, 0), (P, P, 1), (2 * P, DEC, 2)], [(0, P, 3)], [(0, P, 3), (P, P, 4)]]
V_TILES = [0, P, NEW, PROMPT, PROMPT + P]


def indexer_units():
    return [(tt, tuple(range(h, h + n))) for tt, n in ((1, 4), (2, 2), (0, 1)) for h in range(0, IDX_HEADS, n)]


IDX_UNITS = indexer_units()
IDX_PIECES = 8
FILLED_A = 2


def units_after(piece):
    turns = IDX_PIECES - 1
    return range((piece - 1) * len(IDX_UNITS) // turns, piece * len(IDX_UNITS) // turns) if piece else ()


def rotated_before(group):
    return group - (G_AQ - G_AV if group >= G_AQ else 0)


def roped_by(group):
    return rotated_before(group) + 2


SWAP_16 = [(i + 16) % 32 for i in range(32)]
SWAP_8 = [(i + 8) % 16 if i < 16 else i for i in range(32)]


def hybrid_layer(nc, d):
    def rows(ap, k):
        return ap.rearrange("(k p) n -> p k n", p=P)

    w_in = rows(d["w_in"], KD)
    w_uq = d["w_uq"].rearrange("(k p) n -> p k n", p=P)
    w_uk = d["w_uk"].rearrange("(k p) n -> p k n", p=P)
    w_uv = d["w_uv"].rearrange("(k p) n -> p k n", p=P)
    w_oa = rows(d["w_o_a"], 8)
    w_ob = rows(d["w_o_b"], 8)
    w_out = rows(d["w_out"], KD)

    ctx = ExitStack()
    with ctx:
        def sem(name):
            return ctx.enter_context(nc.semaphore(name))

        def at(name, shape, offset, dtype=F32):
            t = nc.alloc_sbuf_tensor_at(name, shape, dtype, offset=offset)
            end = offset + 4 * int(np.prod(shape[1:]))
            assert end <= nc.sbuf_usable_end, (name, end)
            return t, end

        def row(start, *parts):
            made = []
            for name, shape, *dtype in parts:
                t, start = at(name, shape, start, *dtype)
                start = -(-start // 32) * 32
                made.append(t)
            return (*made, start)

        (x_hi, x_lo, raw, w_hi, w_lo, ident, ones, rope_tab, norm_g, lora_g, ss, var, root, rstd,
         mx, neg_mx, sum_p, inv_p, o_base) = row(
            -(-nc.sbuf_base // 64) * 64,
            ("x_hi", [P, KD, NTOK], F32R), ("x_lo", [P, KD, NTOK], F32R), ("raw", [P, RAW, 2048]),
            ("w_hi", [P, 2, 2048], F32R), ("w_lo", [P, 2, 2048], F32R), ("ident_sb", [P, P]), ("ones", [P, P]),
            ("rope_sb", [P, 6, NTOK]), ("norm_g_sb", [P, KD]), ("lora_g", [P, 2, KL]), ("ss", [P, 4]), ("var", [P, 4]), ("root", [P, 4]), ("rstd", [P, 4]), ("mx", [P, 2]),
            ("neg_mx", [P, 2]), ("sum_p", [P, 2]), ("inv_p", [P, 2]))
        o_t, arena = at("o_t", [P, 16, NTOK], o_base)
        z_stage, z_shuf, z_cos, sq_z, lat_var, lat_r, _ = row(
            o_base, ("z_stage", [P, 2, 2, NTOK]), ("z_shuf", [P, 2, NTOK]), ("z_cos", [P, 2, NTOK]),
            ("sq_z", [P, KL, NTOK]), ("lat_var", [P, 2, NTOK]), ("lat_r", [P, 2, NTOK]))
        og_lo, _ = at("og_lo", [P, 16, NTOK], o_base, F32R)

        at_x = arena + 8 * NKEY
        at_f = at_x + 18432
        at_y = at_f + 32 * NTOK
        at_v = at_y + 32 * NTOK + 32 * NKEY + 16 * NTOK

        kr_t, _ = at("kr_t", [P, 2, NKEY], arena)
        x_tok, _ = at("x_tok", [P, 3, D_MODEL], at_y)
        x_sq, dve_sq, diag, d_end = row(at_x, ("x_sq", [P, 2, D_MODEL]), ("dve_sq", [P, D_MODEL]), ("diag", [P, 3, P]))
        assert d_end <= at_y
        probs_a, masked, probs_ta, aq_t, ka_t, va_past, kv_tok, work, at_l = row(
            at_y, ("probs_a", [P, 2, PAST + DEC]), ("masked", [P, 2, PAST + DEC]), ("probs_ta", [P, 2, 3, P]),
            ("aq_t", [P, 8, NTOK]), ("ka_t", [P, A_KV, NKEY]), ("va_past", [P, 2, 256]), ("kv_tok", [P, 3, 512]),
            ("work", [P, 3, PAST + DEC]))
        cq_hi, cq_lo, ckv_tok, iw_tok, top8, ik_tok, kr_tok, _ = row(
            at_l, ("cq_hi", [P, KL, NTOK], F32R), ("cq_lo", [P, KL, NTOK], F32R), ("ckv_tok", [P, 3, LORA]),
            ("iw_tok", [P, 3, IDX_HEADS]), ("top8", [P, 2, 8]), ("ik_tok", [P, 3, P]), ("kr_tok", [P, 3, ROPE]))
        ckv_past, score, s_end = row(at_y, ("ckv_past", [P, 2, LORA]), ("score", [P, 3, PAST + DEC]))
        relu_ring, _ = at("relu_ring", [P, 4, 512], at_l)
        k_past, idx_past, kr_past, _ = row(
            at_l + 32 * NTOK, ("k_past", [P, 2, 256]), ("idx_past", [P, 2, 2 * IDX_DIM]), ("kr_past", [P, 2, 2 * ROPE]))
        iq_t, _ = at("iq_t", [P, 8, NTOK], at_f)
        lora_z, _ = at("lora_z", [P, 2, KL, NTOK], at_f)
        ik_t, ik_z, kr_swap, _ = row(at_x, ("ik_t", [P, 2, NKEY]), ("ik_z", [P, NTOK]), ("kr_swap", [P, NTOK]))
        ckv_hi, ckv_lo, _ = row(at_x, ("ckv_hi", [P, KL, NKEY], F32R), ("ckv_lo", [P, KL, NKEY], F32R))
        probs_b, probs_tb, p_end = row(at_x, ("probs_b", [P, 2, PAST + DEC]), ("probs_tb", [P, 2, 3, P]))
        assert p_end <= at_f - 32 * NTOK
        qn_t, kb_t, qr_z, v_start = row(
            at_y, ("qn_t", [P, 8, NTOK]), ("kb_t", [P, B_HEADS, NKEY]), ("qr_z", [P, 4, NTOK]))
        assert v_start == at_v
        qr_t = qr_z
        vb, _ = at("vb", [P, 5, 1024], at_v)
        qr_swap, _ = at("qr_swap", [P, 4, NTOK], at_l + 32 * NTOK)
        merge_g, _ = at("merge_g", [P, 32, NTOK], at_f - 32 * NTOK)
        og_hi, gate_t, gate_x, y_a, y_b, _ = row(
            at_y + 64 * NTOK, ("og_hi", [P, 16, NTOK], F32R), ("gate_t", [P, 2, 2, NTOK]),
            ("gate_x", [P, 2, 2, NTOK]), ("y_a", [P, 2, NTOK]), ("y_b", [P, 2, NTOK]))
        m_hi, m_lo = x_hi, x_lo
        h_tok, _ = at("h_tok", [P, 3, D_MODEL], at_f - 32 * NTOK)
        final_g, h_stage, h_sum, h_sq, h_ss, _ = row(
            at_y + 64 * NTOK, ("final_g_sb", [P, D_MODEL]), ("h_stage", [P, 2, 2, NTOK]),
            ("h_sum", [P, 2, 3, 256]), ("h_sq", [P, 256]), ("h_ss", [P, 3, 8]))

        ps = ctx.enter_context(nc.psum_tensor("ps", [P, 8, 512], F32))

        def pair(n):
            return ps[:, 2 * (n % 2):2 * (n % 2) + 2, 0:NTOK]

        raw_landed = [sem(f"raw_landed{i}") for i in range(RAW)]
        hi_done, lo_done, step_done = sem("hi_done"), sem("lo_done"), sem("step_done")
        pair_read, stage_used = sem("pair_read"), sem("stage_used")
        x_landed = [sem(f"x_landed{i}") for i in range(3)]
        rope_landed, lora_g_landed = sem("rope_landed"), sem("lora_g_landed")
        consts_landed, past_landed, va_landed = sem("consts_landed"), sem("past_landed"), sem("va_landed")
        ckv_past_landed, res_landed, fg_landed = sem("ckv_past_landed"), sem("res_landed"), sem("fg_landed")
        ss_done, var_done, root_done, diag_done = (sem(n) for n in ("ss_done", "var_done", "root_done", "diag_done"))
        xt_ready, xhi_done, xlo_done = sem("xt_ready"), sem("xhi_done"), sem("xlo_done")
        small_copied, roped, tr_ready, tr_copied = (sem(n) for n in ("small_copied", "roped", "tr_ready", "tr_copied"))
        iw_scaled = sem("iw_scaled")
        idx_ready, relu_done, idx_added = sem("idx_ready"), sem("relu_done"), sem("idx_added")
        lora_copied, sq_done, sumsq_ready, lat_var_done, lat_root_done, lat_normed = (
            sem(n) for n in ("lora_copied", "sq_done", "sumsq_ready", "lat_var_done", "lat_root_done", "lat_normed"))
        lat_hi, lat_lo, past_lat_ready, past_lat_hi, past_lat_lo, tok_ready, tok_copied = (
            sem(n) for n in ("lat_hi", "lat_lo", "past_lat_ready", "past_lat_hi", "past_lat_lo", "tok_ready",
                             "tok_copied"))
        h_weighted, h_rstd, h_ready_act = sem("h_weighted"), sem("h_rstd"), sem("h_ready_act")
        ones_set, ss_cleared, h_cleared = sem("ones_set"), sem("ss_cleared"), sem("h_cleared")
        scores_ready, scores_read, neg_ready, p_ready, pn_ready = (
            sem(n) for n in ("scores_ready", "scores_read", "neg_ready", "p_ready", "pn_ready"))
        pt_ready, pt_copied, o_ready, o_copied = (sem(n) for n in ("pt_ready", "pt_copied", "o_ready", "o_copied"))
        bias_done = sem("bias_done")
        uq_ready, uq_copied, q_roped = sem("uq_ready"), sem("uq_copied"), sem("q_roped")
        uk_ready, uk_copied, uv_ready, uv_copied = (sem(n) for n in ("uk_ready", "uk_copied", "uv_ready", "uv_copied"))
        gate_ready, gate_used, gated_hi_done, gated_lo_done = (
            sem(n) for n in ("gate_ready", "gate_used", "gated_hi_done", "gated_lo_done"))
        y_ready, y_read, m_done = sem("y_ready"), sem("y_read"), sem("m_done")
        hT_copied, ht_ready, h_added, h_squared, h_ready = (
            sem(n) for n in ("hT_copied", "ht_ready", "h_added", "h_squared", "h_ready"))
        h_var_done, h_root_done = sem("h_var_done"), sem("h_root_done")
        dve_self, act_self = sem("dve_self"), sem("act_self")
        kv_out, ckv_out, y_out = sem("kv_out"), sem("ckv_out"), sem("y_out")

        block = ctx.enter_context(nc.Block())

        def landed(step, it=0):
            return 16 * (step // RAW + 1) + (16 if step % RAW < 2 else 0) + 16 * it

        @block.sync
        def _(sp):
            for tt, (t0, n) in enumerate(TOK):
                src = d["x_sample"] if tt == 0 else d["x_prompt"][t0 - DEC:t0 - DEC + n, :]
                sp.dma_start(x_tok[0:n, tt, :], src).then_inc(x_landed[tt], 16)

            def load(step, src, it=0, part=slice(0, 2048)):
                if step >= RAW:
                    sp.wait_ge(lo_done, step - RAW + 1 + RAW * it)
                dst = raw[:, step % RAW, part].rearrange("p (k n) -> p k n", k=src.shape[1])
                sp.dma_start(dst, src).then_inc(raw_landed[step % RAW], 16)

            def load_w_in(group, turns, col):
                with sp.Fori(0, turns) as it:
                    for j in range(4):
                        load(steps_of(group) + j, w_in[:, KH * (j % 2):KH * (j % 2) + KH,
                                                       bass.ds(it * 512 + (col + 256 * (j // 2)), 256)], it)

            for half in range(2):
                dst = raw[:, half, :].rearrange("p (k n) -> p k n", k=KH)
                for m, col in enumerate((COL_IK, COL_KR)):
                    sp.dma_start(dst[:, :, m * P:(m + 1) * P],
                                 w_in[:, KH * half:KH * half + KH, col:col + P]).then_inc(raw_landed[half], 16)
            for j in range(8):
                col = COL_IQ + 256 * (j // 2)
                load(steps_of(G_IQ) + j, w_in[:, KH * (j % 2):KH * (j % 2) + KH, col:col + 256])
            for j in range(4):
                col = COL_AK + 256 * (j // 2)
                load(STEP_AK + j, w_in[:, KH * (j % 2):KH * (j % 2) + KH, col:col + 256])
            load_w_in(G_CQ, 2, COL_CQ)
            load_w_in(G_AQ, 2, COL_AQ)
            load_w_in(G_FILL_A, 2, COL_MG + P * merge_tile(G_FILL_A))
            for j in range(4):
                load(STEP_UQ + j, w_uq[:, :, 384 * j:384 * j + 384], part=slice(0, 4 * 384))
            for j in range(2):
                load(STEP_UK + j, w_uk[:, :, 512 * j:512 * j + 512])
            for j in range(2):
                load(STEP_UV + j, w_uv[:, :, 512 * j:512 * j + 512])
            load_w_in(G_FILL_B, 2, COL_MG + P * merge_tile(G_FILL_B))
            load_w_in(G_MG, 4, COL_MG + P * merge_tile(G_MG))
            load_w_in(G_GATE, 2, COL_AGATE)
            load_w_in(G_GATE + 4, 2, COL_BGATE)
            with sp.Fori(0, 4) as it:
                for j in range(4):
                    w = (w_oa, w_ob)[j % 2]
                    load(STEP_Y + j, w[:, :, bass.ds(it * 512 + 256 * (j // 2), 256)], it)
            with sp.Fori(0, 4) as it:
                for j in range(4):
                    load(STEP_OUT + j, w_out[:, KH * (j % 2):KH * (j % 2) + KH,
                                             bass.ds(it * 512 + 256 * (j // 2), 256)], it)
            for i, tt in enumerate((*DVE_LAST, ACT_LAST)):
                (t0, n) = TOK[tt]
                if tt == ACT_LAST:
                    sp.wait_ge(h_ready_act, 1)
                else:
                    sp.wait_ge(h_ready, i + 1)
                dst = d["y_sample"] if tt == 0 else d["y_prompt"][t0 - DEC:t0 - DEC + n, :]
                sp.dma_start(dst, h_tok[0:n, tt, :]).then_inc(y_out, 16)
            sp.wait_ge(y_out, 48)

        @block.gpsimd
        def _(pool):
            pool.memset(ones[:], 1.0).then_inc(ones_set, 1)
            pool.dma_start(ident[:], d["ident"]).then_inc(consts_landed, 16)
            pool.dma_start(norm_g[:], d["norm_g"]).then_inc(consts_landed, 16)
            pool.wait_ge(x_landed[2], 16)
            pool.dma_start(rope_tab[:], d["rope_tab"].rearrange("c p t -> p c t")).then_inc(rope_landed, 16)
            for b, name in enumerate(("q_norm_g", "kv_norm_g")):
                pool.dma_start(lora_g[:, b, :], d[name]).then_inc(lora_g_landed, 16)
            pool.dma_start(k_past[:], rows(d["cache_a_k"], 2)).then_inc(past_landed, 16)
            for dup in range(2):
                pool.dma_start(idx_past[:, :, IDX_DIM * dup:IDX_DIM * dup + IDX_DIM],
                               rows(d["cache_idx_k"], 2)).then_inc(past_landed, 16)
                pool.dma_start(kr_past[:, :, ROPE * dup:ROPE * dup + ROPE],
                               rows(d["cache_mla_krope"], 2)).then_inc(past_landed, 16)
            pool.wait_ge(xt_ready, KD)
            pool.dma_start(va_past[:], rows(d["cache_a_v"], 2)).then_inc(va_landed, 16)
            pool.dma_start(ckv_past[:], rows(d["cache_mla_ckv"], 2)).then_inc(ckv_past_landed, 16)
            pool.wait_ge(tr_copied, 7)
            for tt, (t0, n) in enumerate(TOK):
                def out(name):
                    return d[name + "_sample"] if tt == 0 else d[name + "_prompt"][t0 - DEC:t0 - DEC + n, :]
                pool.dma_start(out("new_a_k"), kv_tok[0:n, tt, 0:256]).then_inc(kv_out, 16)
                pool.dma_start(out("new_a_v"), kv_tok[0:n, tt, 256:512]).then_inc(kv_out, 16)
                pool.dma_start(out("new_idx_k"), ik_tok[0:n, tt, 0:IDX_DIM]).then_inc(kv_out, 16)
                pool.dma_start(out("new_krope"), kr_tok[0:n, tt, :]).then_inc(kv_out, 16)
            pool.wait_ge(tok_copied, 3)
            for tt, (t0, n) in enumerate(TOK):
                dst = d["new_ckv_sample"] if tt == 0 else d["new_ckv_prompt"][t0 - DEC:t0 - DEC + n, :]
                pool.dma_start(dst, ckv_tok[0:n, tt, :]).then_inc(ckv_out, 16)
            pool.wait_ge(m_done, 8)
            for tt, (t0, n) in enumerate(TOK):
                src = d["x_sample"] if tt == 0 else d["x_prompt"][t0 - DEC:t0 - DEC + n, :]
                pool.dma_start(h_tok[0:n, tt, :], src).then_inc(res_landed, 16)
            pool.dma_start(final_g[:], d["final_g"].rearrange("(a n) -> a n", a=1).partition_broadcast(P))\
                .then_inc(fg_landed, 16)
            pool.wait_ge(kv_out, 12 * 16)
            pool.wait_ge(ckv_out, 48)

        @block.tensor
        def _(pe):
            def three(out, hi, lo, x_h, x_l, first, last):
                nc.tensor.matmul(out, hi, x_h, start=first, stop=False)
                nc.tensor.matmul(out, hi, x_l, start=False, stop=False)
                return nc.tensor.matmul(out, lo, x_h, start=False, stop=last)

            def weights(step, k):
                cols = 1536 if STEP_UQ <= step < STEP_UK else 2048
                return [w[:, step % 2, 0:cols].rearrange("p (k n) -> p k n", k=k) for w in (w_hi, w_lo)]

            def half_tile(step, group, half, m, x_h, x_l):
                hi, lo = weights(step, KH)
                cols = slice(m * P, (m + 1) * P)
                for k in range(KH):
                    last = three(pair(group)[:, m, :], hi[:, k, cols], lo[:, k, cols], x_h[:, KH * half + k, :],
                                 x_l[:, KH * half + k, :], half == 0 and k == 0, half == 1 and k == KH - 1)
                return last

            def half_group(step, group, half, x_h, x_l, it=0):
                pe.wait_ge(lo_done, step + 1 + RAW * it)
                half_tile(step, group, half, 0, x_h, x_l)
                half_tile(step, group, half, 1, x_h, x_l).then_inc(step_done, 1)

            def fill(first_group, i):
                group, half, m = first_group + i // 4, i // 2 % 2, i % 2
                if i % 4 == 0:
                    pe.wait_ge(pair_read, group - 1)
                if m == 0:
                    pe.wait_ge(lo_done, steps_of(group) + half + 1)
                last = half_tile(steps_of(group) + half, group, half, m, x_hi, x_lo)
                if m == 1:
                    last.then_inc(step_done, 1)

            def w_in_group(group, it=0):
                if group >= 2:
                    pe.wait_ge(pair_read, group - 1 + 2 * it)
                for half in range(2):
                    half_group(steps_of(group) + half, group, half, x_hi, x_lo, it)

            def w_in_groups(group, turns):
                with pe.Fori(0, turns) as it:
                    for j in range(2):
                        w_in_group(group + j, it)

            LAG = 4
            small = pair(G_SMALL)
            pe.wait_ge(diag_done, 1)
            for k in range(KD + LAG):
                if k < KD:
                    if k >= 6:
                        pe.wait_ge(xlo_done, k - 5)
                    for tt, (t0, n) in enumerate(TOK):
                        last = nc.tensor.matmul(ps[:, 2 + k % 6, t0:t0 + n], x_tok[0:n, tt, k * P:(k + 1) * P],
                                                diag[0:n, tt, 0:n], start=True, stop=True)
                    last.then_inc(xt_ready, 1)
                if k >= LAG:
                    kk = k - LAG
                    half, row_tile = kk // KH, kk % KH
                    if row_tile == 0:
                        pe.wait_ge(lo_done, half + 1)
                    pe.wait_ge(xlo_done, kk + 1)
                    hi, lo = weights(half, KH)
                    for m in range(2):
                        cols = slice(m * P, (m + 1) * P)
                        last = three(small[:, m, :], hi[:, row_tile, cols], lo[:, row_tile, cols], x_hi[:, kk, :],
                                     x_lo[:, kk, :], kk == 0, kk == KD - 1)
                    if row_tile == KH - 1:
                        last.then_inc(step_done, 1)
            w_in_groups(G_IQ, 2)

            pe.wait_ge(past_landed, 80)
            for g in range(A_KV):
                for t in range(2):
                    last = nc.tensor.transpose(ps[:, 4, (2 * g + t) * P:(2 * g + t + 1) * P],
                                               k_past[:, t, g * P:(g + 1) * P], ident[:])
            last.then_inc(tr_ready, 1)
            for i, past in enumerate((idx_past, kr_past)):
                for t in range(2):
                    last = nc.tensor.transpose(ps[:, 5, (2 * i + t) * P:(2 * i + t + 1) * P], past[:, t, :], ident[:])
            last.then_inc(tr_ready, 1)
            pe.wait_ge(roped, 2)
            for tt, (t0, n) in enumerate(TOK):
                last = nc.tensor.transpose(ps[0:n, 6, tt * P:(tt + 1) * P], ik_z[:, t0:t0 + n], ident[:])
            last.then_inc(tr_ready, 1)
            for tt, (t0, n) in enumerate(TOK):
                last = nc.tensor.transpose(ps[0:n, 7, tt * ROPE:(tt + 1) * ROPE], kr_t[0:ROPE, 0, NEW + t0:NEW + t0 + n],
                                           ident[0:ROPE, 0:ROPE])
            last.then_inc(tr_ready, 1)

            for i in range(IDX_PIECES):
                fill(G_AK, i)
                if i == 1:
                    pe.wait_ge(tr_copied, 4)
                    pe.wait_ge(roped, 2 + G_AK - G_IQ)
                for u in units_after(i):
                    tt, heads = IDX_UNITS[u]
                    if u >= 4:
                        pe.wait_ge(relu_done, u - 3)
                    (t0, n), (k0, nk) = TOK[tt], KEYS[tt]
                    for j, h in enumerate(heads):
                        last = nc.tensor.matmul(ps[0:n, 4 + u % 4, j * nk:(j + 1) * nk], iq_t[:, h // 2, t0:t0 + n],
                                                ik_t[:, h % 2, k0:k0 + nk], start=True, stop=True)
                    last.then_inc(idx_ready, 1)

            w_in_group(G_CQ)
            pe.wait_ge(relu_done, len(IDX_UNITS))
            pe.wait_ge(roped, roped_by(G_AK))
            pe.wait_ge(pair_read, G_AV + 1)
            for tt, (t0, n) in enumerate(TOK):
                for g in range(A_KV):
                    nc.tensor.transpose(ps[0:n, 4 + tt, g * P:(g + 1) * P], ka_t[:, g, NEW + t0:NEW + t0 + n], ident[:])
                    last = nc.tensor.transpose(ps[0:n, 4 + tt, (2 + g) * P:(3 + g) * P],
                                               z_stage[:, G_AV % 2, g, t0:t0 + n], ident[:])
                last.then_inc(tr_ready, 1)

            def sums_of_squares(b):
                pe.wait_ge(sq_done, b + 1)
                for k in range(KL):
                    last = nc.tensor.matmul(ps[:, 4 + b, 0:NTOK], ones[:], sq_z[:, k, :], start=k == 0, stop=k == KL - 1)
                last.then_inc(sumsq_ready, 1)

            w_in_group(G_CQ + 1)
            w_in_group(G_CQ + 2)
            pe.wait_ge(ones_set, 1)
            pe.wait_ge(tr_copied, 7)
            sums_of_squares(0)
            pe.wait_ge(ckv_past_landed, 16)
            for b in range(2):
                for k in range(2):
                    for t in range(2):
                        last = nc.tensor.transpose(ps[:, 6 + b, (2 * k + t) * P:(2 * k + t + 1) * P],
                                                   ckv_past[:, t, (2 * b + k) * P:(2 * b + k + 1) * P], ident[:])
                last.then_inc(past_lat_ready, 1)
            w_in_group(G_CQ + 3)
            w_in_group(G_AQ)
            sums_of_squares(1)
            for g in range(1, 4):
                w_in_group(G_AQ + g)
            pe.wait_ge(lat_normed, 2 * KL)
            pe.wait_ge(past_lat_lo, 2)
            for tt, (t0, n) in enumerate(TOK):
                for k in range(KL):
                    last = nc.tensor.transpose(ps[0:n, 4 + tt, k * P:(k + 1) * P], lora_z[:, 1, k, t0:t0 + n], ident[:])
                last.then_inc(tok_ready, 1)

            def scores(u):
                branch, kind, h = UNITS[u]
                (t0, n), (k0, nk), bank = TOK[kind], KEYS[kind], 4 + u % 2
                if u >= 2:
                    pe.wait_ge(scores_read if UNITS[u - 2][0] == "A" else p_ready, u - 1)
                for i, hh in enumerate(range(4 * h, 4 * h + 4) if kind == 0 else [h]):
                    out = ps[n * i:n * i + n, bank, 0:nk]
                    if branch == "A":
                        last = nc.tensor.matmul(out, aq_t[:, hh, t0:t0 + n], ka_t[:, hh // GRP, k0:k0 + nk],
                                                start=True, stop=True)
                    else:
                        nc.tensor.matmul(out, qn_t[:, hh, t0:t0 + n], kb_t[:, hh, k0:k0 + nk], start=True, stop=False)
                        last = nc.tensor.matmul(out, qr_t[:, hh // 2, t0:t0 + n], kr_t[:, hh % 2, k0:k0 + nk],
                                                start=False, stop=True)
                last.then_inc(scores_ready, 1)

            def turn_probs(u):
                pe.wait_ge(pn_ready, u + 1)
                if u >= 1:
                    pe.wait_ge(pt_copied, u)
                probs = (probs_a, probs_b)[u >= N_A]
                for j, (off, nk, _) in enumerate(KEY_TILES[UNITS[u][1]]):
                    last = nc.tensor.transpose(ps[0:nk, 6, j * P:(j + 1) * P], probs[:, u % 2, off:off + nk], ident[:])
                last.then_inc(pt_ready, 1)

            def values(u):
                branch, kind, h = UNITS[u]
                pe.wait_ge(pt_copied, u + 1)
                if u >= 1:
                    pe.wait_ge(o_copied, u)
                tiles = KEY_TILES[kind]
                heads = range(4 * h, 4 * h + 4) if branch == "B" and kind == 0 else [h]
                width = P // len(heads)
                probs_t = (probs_ta, probs_tb)[u >= N_A]
                for i, hh in enumerate(heads):
                    for j, (_, nk, t) in enumerate(tiles):
                        if branch == "B":
                            v = vb[0:nk, t, hh * P:(hh + 1) * P]
                        else:
                            g = h if kind == 0 else h // GRP
                            v = va_past[:, t, g * P:(g + 1) * P] if t < 2 else \
                                kv_tok[0:nk, t - 2, (2 + g) * P:(3 + g) * P]
                        last = nc.tensor.matmul(ps[:, 7, width * i:width * (i + 1)], v,
                                                probs_t[0:nk, u % 2, j, width * i:width * (i + 1)],
                                                start=j == 0, stop=j == len(tiles) - 1)
                last.then_inc(o_ready, 1)

            def attention(first, end, group, filled):
                scores(first)
                for u in range(first, end):
                    for i in pieces(u - first, end - first, filled):
                        fill(group, i)
                    if u + 1 < end:
                        scores(u + 1)
                    turn_probs(u)
                    if u > first:
                        values(u - 1)
                values(end - 1)

            for i in range(FILLED_A):
                fill(G_FILL_A, i)
            pe.wait_ge(tok_copied, 3)
            pe.wait_ge(roped, roped_by(G_AQ + 3))
            pe.wait_ge(va_landed, 16)
            attention(0, N_A, G_FILL_A, FILLED_A)

            pe.wait_ge(lat_lo, 2)
            pe.wait_ge(pair_read, G_FILL_B)
            for j in range(4):
                step = STEP_UQ + j
                pe.wait_ge(lo_done, step + 1)
                hi, lo = weights(step, KL)
                for i in range(3):
                    n = 3 * j + i
                    if n >= 4:
                        pe.wait_ge(uq_copied, n - 3)
                    for k in range(KL):
                        cols = slice(i * P, (i + 1) * P)
                        last = three(ps[:, n % 4, 0:NTOK], hi[:, k, cols], lo[:, k, cols], cq_hi[:, k, :], cq_lo[:, k, :], k == 0, k == KL - 1)
                    last.then_inc(uq_ready, 1)
                pe.wait_ge(uq_ready, 3 * j + 3)
                pe.sem_inc(step_done, 1)
            for h in range(B_HEADS):
                step = STEP_UK + h // 4
                if h % 4 == 0:
                    pe.wait_ge(lo_done, step + 1)
                if h < 2:
                    pe.wait_ge(uq_copied, 12)
                else:
                    pe.wait_ge(uk_copied, h - 1)
                hi, lo = weights(step, KL)
                cols = slice((h % 4) * P, (h % 4 + 1) * P)
                for k in range(KL):
                    for half in range(2):
                        keys = slice(half * NKEY // 2, (half + 1) * NKEY // 2)
                        last = three(ps[:, 2 * (h % 2) + half, 0:NKEY // 2], hi[:, k, cols], lo[:, k, cols],
                                     ckv_hi[:, k, keys], ckv_lo[:, k, keys], k == 0, k == KL - 1)
                last.then_inc(uk_ready, 1)
                if h % 4 == 3:
                    pe.wait_ge(uk_ready, h + 1)
                    pe.sem_inc(step_done, 1)
            for n in range(10):
                step, w = STEP_UV + n // 5, n % 5
                if w == 0:
                    pe.wait_ge(lo_done, step + 1)
                if n < 4:
                    pe.wait_ge(uk_copied, B_HEADS)
                else:
                    pe.wait_ge(uv_copied, n - 3)
                hi, lo = weights(step, KL)
                keys = slice(V_TILES[w], V_TILES[w] + P)
                for k in range(KL):
                    nc.tensor.matmul(ps[:, n % 4, :], ckv_hi[:, k, keys], hi[:, k, :], start=k == 0, stop=False)
                    nc.tensor.matmul(ps[:, n % 4, :], ckv_hi[:, k, keys], lo[:, k, :], start=False, stop=False)
                    last = nc.tensor.matmul(ps[:, n % 4, :], ckv_lo[:, k, keys], hi[:, k, :],
                                            start=False, stop=k == KL - 1)
                last.then_inc(uv_ready, 1)
                if w == 4:
                    pe.wait_ge(uv_ready, n + 1)
                    pe.sem_inc(step_done, 1)

            pe.wait_ge(q_roped, 1)
            pe.wait_ge(uk_copied, B_HEADS)
            pe.wait_ge(uv_copied, 10)
            attention(N_A, len(UNITS), G_FILL_B, 0)

            w_in_groups(G_MG, 4)
            w_in_groups(G_GATE, 4)

            def branch_out(step, group, b, it=0):
                pe.wait_ge(lo_done, step + 1 + RAW * it)
                if isinstance(it, int) and group == 0:
                    pe.wait_ge(pair_read, G_END)
                else:
                    pe.wait_ge(y_read, 2 * group + b - 1 + 4 * it)
                hi, lo = weights(step, KH)
                for m in range(2):
                    for k in range(KH):
                        cols = slice(m * P, (m + 1) * P)
                        last = three(ps[:, 2 * b + m, 0:NTOK], hi[:, k, cols], lo[:, k, cols], og_hi[:, 8 * b + k, :],
                                     og_lo[:, 8 * b + k, :], k == 0, k == KH - 1)
                last.then_inc(step_done, 1)

            for j in range(4):
                if j < 2:
                    pe.wait_ge(gated_lo_done, 4 + 4 * j)
                branch_out(STEP_Y + j, j // 2, j % 2)
            with pe.Fori(0, 3) as it:
                for j in range(4, 8):
                    branch_out(STEP_Y + j, j // 2, j % 2, it)

            def out_group(j, it=0):
                for half in range(2):
                    step = STEP_OUT + 2 * j + half
                    if isinstance(it, int) and j == 0:
                        pe.wait_ge(m_done, 4 + 4 * half)
                        pe.wait_ge(y_read, 16)
                    elif half == 0 and not (isinstance(it, int) and j == 1):
                        pe.wait_ge(hT_copied, j - 1 + 2 * it)
                    half_group(step, j, half, m_hi, m_lo, it)

            def turn_out(j, it=0):
                pe.wait_ge(hT_copied, j + 1 + 2 * it)
                if not (isinstance(it, int) and j == 0):
                    pe.wait_ge(h_added, j + 2 * it)
                for tt, (t0, n) in enumerate(TOK):
                    for m in range(2):
                        last = nc.tensor.transpose(ps[0:n, 4 + tt, m * P:(m + 1) * P], h_stage[:, j % 2, m, t0:t0 + n],
                                                   ident[:])
                last.then_inc(ht_ready, 1)

            out_group(0)
            out_group(1)
            turn_out(0)
            with pe.Fori(0, 3) as it:
                for j in range(2, 4):
                    out_group(j, it)
                    turn_out(j - 1, it)
            turn_out(7)

        @block.scalar
        def _(act):
            def split_hi(step, it=0):
                act.wait_ge(raw_landed[step % RAW], landed(step, it))
                if step >= 2:
                    act.wait_ge(step_done, step - 1 + RAW * it)
                n = 1536 if STEP_UQ <= step < STEP_UK else 2048
                nc.scalar.copy(w_hi[:, step % 2, 0:n], raw[:, step % RAW, 0:n]).then_inc(hi_done, 1)

            def group_ready(group, it=0):
                act.wait_ge(step_done, steps_of(group) + 2 + RAW * it)

            act.wait_ge(ss_cleared, 1)
            n = TOK[1][1]
            act.wait_ge(x_landed[1], 16)
            nc.scalar.activation(x_sq[0:n, 0, :], x_tok[0:n, 1, :], ACT.Square, accum_out=ss[0:n, 1:2])
            act.wait_ge(x_landed[2], 16)
            nc.scalar.activation(x_sq[0:n, 1, 0:D_MODEL // 2], x_tok[0:n, 2, 0:D_MODEL // 2], ACT.Square,
                                 accum_out=ss[0:n, 2:3]).then_inc(ss_done, 1)
            act.wait_ge(var_done, 1)
            nc.scalar.activation(root[:, 0:3], var[:, 0:3], ACT.Sqrt).then_inc(root_done, 1)
            split_hi(0)
            act.wait_ge(consts_landed, 32)
            for k in range(KD):
                act.wait_ge(xt_ready, k + 1)
                nc.scalar.activation(x_hi[:, k, :], ps[:, 2 + k % 6, 0:NTOK], ACT.Copy,
                                     scale=norm_g[:, k:k + 1]).then_inc(xhi_done, 1)
                if k == LAG_SPLIT:
                    split_hi(1)

            def to_stage(group):
                group_ready(group)
                if group >= G_AQ:
                    act.wait_ge(stage_used, max(rotated_before(group) - 1, G_AK + 1))
                elif group >= 2:
                    act.wait_ge(stage_used, group - 1)
                nc.scalar.copy(z_stage[:, group % 2, :, :], pair(group)).then_inc(pair_read, 1)

            for half in range(2):
                split_hi(2 + half)
            group_ready(G_SMALL)
            for a, b in ((0, 32), (32, 0)):
                nc.scalar.copy(kr_swap[a:a + 32, :], ps[b:b + 32, 1, 0:NTOK]).then_inc(small_copied, 1)
            to_stage(G_SMALL)
            for g in range(G_IQ, G_AK):
                for half in range(2):
                    split_hi(2 * g + 2 + half)
                to_stage(g)

            act.wait_ge(tr_ready, 1)
            nc.scalar.copy(ka_t[:, :, 0:PAST], ps[:, 4, :].rearrange("p (g t) -> p g t", g=2)).then_inc(tr_copied, 1)
            act.wait_ge(tr_ready, 2)
            for i, dst in enumerate((ik_t, kr_t)):
                for half in range(2):
                    rows64 = slice(64 * half, 64 * half + 64)
                    last = nc.scalar.copy(dst[rows64, half, 0:PAST], ps[rows64, 5, i * PAST:(i + 1) * PAST])
            last.then_inc(tr_copied, 1)
            for i, dst in enumerate((ik_tok, kr_tok)):
                act.wait_ge(tr_ready, 3 + i)
                width = dst.shape[2]
                nc.scalar.copy(dst[0:DEC, 0, :], ps[0:DEC, 6 + i, 0:width])
                nc.scalar.copy(dst[:, 1:3, :], ps[:, 6 + i, width:3 * width].rearrange("p (t n) -> p t n", t=2))\
                    .then_inc(tr_copied, 1)

            for i in range(IDX_PIECES):
                if i % 2 == 1:
                    split_hi(STEP_AK + 2 + i // 2)
                if i % 4 == 3:
                    to_stage(G_AK + i // 4)
                for u in units_after(i):
                    tt, heads = IDX_UNITS[u]
                    act.wait_ge(idx_ready, u + 1)
                    if u >= 4:
                        act.wait_ge(idx_added, u - 3)
                    n, width = TOK[tt][1], KEYS[tt][1] * len(heads)
                    nc.scalar.activation(relu_ring[0:n, u % 4, 0:width], ps[0:n, 4 + u % 4, 0:width], ACT.Relu,
                                         scale=IDX_DIM ** -0.5).then_inc(relu_done, 1)

            lat_tiles = lora_z[:].rearrange("p b k t -> p (b k) t")
            for g in range(G_CQ, G_AQ):
                for half in range(2):
                    split_hi(2 * g + 2 + half)
                group_ready(g)
                nc.scalar.copy(lat_tiles[:, 2 * (g - G_CQ):2 * (g - G_CQ) + 2, :], pair(g)).then_inc(pair_read, 1)
                b = (g - G_CQ) // 2
                if g == G_CQ:
                    for tt, (_, n) in enumerate(TOK):
                        act.wait_ge(tr_ready, 5 + tt)
                        nc.scalar.copy(kv_tok[0:n, tt, :], ps[0:n, 4 + tt, :]).then_inc(tr_copied, 1)
                if g == G_CQ + 2:
                    act.wait_ge(idx_added, len(IDX_UNITS))
                    for c in range(2):
                        act.wait_ge(past_lat_ready, c + 1)
                        nc.scalar.copy(ckv_hi[:, 2 * c:2 * c + 2, 0:PAST],
                                       ps[:, 6 + c, :].rearrange("p (k t) -> p k t", k=2)).then_inc(past_lat_hi, 1)
                if g in (G_CQ + 1, G_CQ + 3):
                    act.wait_ge(pair_read, g + 1)
                    if b == 1:
                        act.wait_ge(sumsq_ready, 1)
                    nc.scalar.activation(sq_z[:], lora_z[:, b, :, :], ACT.Square).then_inc(sq_done, 1)

            for g in range(G_AQ, G_FILL_A):
                for half in range(2):
                    split_hi(2 * g + 2 + half)
                    if g == G_AQ + 2 and half == 1:
                        act.wait_ge(lat_normed, KL)
                        nc.scalar.copy(cq_hi[:], lora_z[:, 0, :, :]).then_inc(lat_hi, 1)
                    if g == G_AQ + 3 and half == 0:
                        act.wait_ge(lat_normed, 2 * KL)
                        nc.scalar.copy(ckv_hi[:, :, NEW:NKEY], lora_z[:, 1, :, :]).then_inc(lat_hi, 1)
                to_stage(g)
                if g == G_AQ:
                    act.wait_ge(lat_var_done, 1)
                    nc.scalar.activation(lat_r[:], lat_var[:], ACT.Sqrt).then_inc(lat_root_done, 1)
            for tt, (_, n) in enumerate(TOK):
                act.wait_ge(tok_ready, tt + 1)
                nc.scalar.copy(ckv_tok[0:n, tt, :], ps[0:n, 4 + tt, :]).then_inc(tok_copied, 1)

            def exponentials(u):
                branch, kind, _ = UNITS[u]
                nk = KEYS[kind][1]
                act.wait_ge(neg_ready, u + 1)
                if u >= 2:
                    act.wait_ge(pt_ready, u - 1)
                probs = (probs_a, probs_b)[u >= N_A]
                src = masked[:, u % 2, 0:nk] if branch == "A" else ps[:, 4 + u % 2, 0:nk]
                nc.scalar.activation(probs[:, u % 2, 0:nk], src, ACT.Exp, bias=neg_mx[:, u % 2:u % 2 + 1],
                                     scale=A_SCALE if branch == "A" else B_SCALE,
                                     accum_out=sum_p[:, u % 2:u % 2 + 1]).then_inc(p_ready, 1)

            def copy_turned(u):
                act.wait_ge(pt_ready, u + 1)
                if u >= 2:
                    act.wait_ge(o_ready, u - 1)
                tiles = KEY_TILES[UNITS[u][1]]
                probs_t = (probs_ta, probs_tb)[u >= N_A]
                full = sum(nk == P for _, nk, _ in tiles)
                last = nc.scalar.copy(probs_t[:, u % 2, 0:full, :],
                                      ps[:, 6, 0:full * P].rearrange("p (j q) -> p j q", j=full))
                if full < len(tiles):
                    nk = tiles[full][1]
                    last = nc.scalar.copy(probs_t[0:nk, u % 2, full, :], ps[0:nk, 6, full * P:(full + 1) * P])
                last.then_inc(pt_copied, 1)

            def merge_tanh(group, it=0):
                group_ready(group, it)
                nc.scalar.activation(merge_g[:, bass.ds(it * 4 + merge_tile(group), 2), :], pair(group), ACT.Tanh,
                                     scale=0.5).then_inc(pair_read, 1)

            def after(group, i):
                if i % 2 == 1:
                    split_hi(steps_of(group) + i // 2 + 2)
                if i % 4 == 3:
                    merge_tanh(group + i // 4)

            def attention(first, end, group, filled):
                exponentials(first)
                for u in range(first, end):
                    for i in pieces(u - first - 1, end - first, filled):
                        after(group, i)
                    copy_turned(u)
                    if u + 1 < end:
                        exponentials(u + 1)
                for i in pieces(end - first - 1, end - first, filled):
                    after(group, i)

            act.wait_ge(lat_lo, 2)
            for i in range(FILLED_A):
                after(G_FILL_A, i)
            attention(0, N_A, G_FILL_A, FILLED_A)

            act.wait_ge(kv_out, 12 * 16)
            act.wait_ge(ckv_out, 48)
            act.wait_ge(o_ready, N_A)
            for j in range(4):
                split_hi(STEP_UQ + 2 + j)
                for i in range(3):
                    n = 3 * j + i
                    act.wait_ge(uq_ready, n + 1)
                    if i < 2:
                        nc.scalar.copy(qn_t[:, 2 * j + i, :], ps[:, n % 4, 0:NTOK]).then_inc(uq_copied, 1)
                    else:
                        nc.scalar.copy(qr_z[:, j, :], ps[:, n % 4, 0:NTOK])
                        for a, b in ((0, 32), (32, 0), (64, 96), (96, 64)):
                            last = nc.scalar.copy(qr_swap[a:a + 32, j, :], ps[b:b + 32, n % 4, 0:NTOK])
                        last.then_inc(uq_copied, 1)
            for h in range(B_HEADS):
                act.wait_ge(uk_ready, h + 1)
                nc.scalar.copy(kb_t[:, h, :].rearrange("p (a t) -> p a t", a=2),
                               ps[:, 2 * (h % 2):2 * (h % 2) + 2, 0:NKEY // 2]).then_inc(uk_copied, 1)
                if h % 4 == 3:
                    split_hi(STEP_UV + h // 4)
            for half in range(2):
                split_hi(STEP_FILL_B + half)
            act.wait_ge(uv_ready, 10)
            attention(N_A, len(UNITS), G_FILL_B, 0)

            for half in range(2):
                split_hi(STEP_MG + 2 + half)
            act.wait_ge(o_copied, len(UNITS))
            merge_tanh(G_MG)
            with act.Fori(0, 3) as it:
                for j in range(2, 4):
                    for half in range(2):
                        split_hi(STEP_MG + 2 * j + half, it)
                    merge_tanh(G_MG + j - 1, it)
            for half in range(2):
                split_hi(STEP_GATE + half)
            merge_tanh(G_GATE - 1)

            def gate_tanh(group, it=0):
                group_ready(group, it)
                if not (isinstance(it, int) and group < G_GATE + 2):
                    act.wait_ge(gate_used, group - G_GATE - 1 + 2 * it)
                nc.scalar.activation(gate_t[:, group % 2, :, :], pair(group), ACT.Tanh, scale=0.5).then_inc(gate_ready, 1)

            def gated_hi(group, it=0):
                act.wait_ge(gate_used, group - G_GATE + 1 + 2 * it)
                nc.scalar.copy(og_hi[:, bass.ds(it * 4 + 2 * (group - G_GATE), 2), :], gate_x[:, group % 2, :, :])\
                    .then_inc(gated_hi_done, 1)

            for half in range(2):
                split_hi(STEP_GATE + 2 + half)
            gate_tanh(G_GATE)
            with act.Fori(0, 3) as it:
                for j in range(2, 4):
                    split_hi(STEP_GATE + 2 * j, it)
                    gated_hi(G_GATE + j - 2, it)
                    split_hi(STEP_GATE + 2 * j + 1, it)
                    gate_tanh(G_GATE + j - 1, it)
            split_hi(STEP_Y)
            gated_hi(G_END - 2)
            split_hi(STEP_Y + 1)
            gate_tanh(G_END - 1)
            gated_hi(G_END - 1)
            for half in range(2):
                split_hi(STEP_Y + 2 + half)
            with act.Fori(0, 3) as it:
                for j in range(4):
                    split_hi(STEP_Y + 4 + j, it)

            def to_h_stage(j):
                act.wait_ge(step_done, STEP_OUT + 2 * j + 2)
                if j >= 2:
                    act.wait_ge(ht_ready, j - 1)
                nc.scalar.activation(h_stage[:, j % 2, :, :], pair(j), ACT.Copy, scale=0.25).then_inc(hT_copied, 1)

            def squares(j):
                act.wait_ge(h_added, j + 1)
                for tt, (_, n) in enumerate(TOK):
                    if j + tt:
                        act.wait_ge(h_squared, 3 * j + tt)
                    nc.scalar.activation(h_sq[0:n, :], h_sum[0:n, j % 2, tt, :], ACT.Square,
                                         accum_out=h_ss[0:n, tt, j:j + 1]).then_inc(h_squared, 1)

            for half in range(2):
                split_hi(STEP_OUT + half)
            act.wait_ge(m_done, 8)
            for j in range(1, 8):
                for half in range(2):
                    split_hi(STEP_OUT + 2 * j + half)
                to_h_stage(j - 1)
                if j >= 3:
                    squares(j - 3)
            squares(5)
            to_h_stage(7)
            squares(6)
            squares(7)
            act.wait_ge(h_var_done, 1)
            nc.scalar.activation(root[:, 0:3], var[:, 0:3], ACT.Sqrt).then_inc(h_root_done, 1)
            act.wait_ge(h_rstd, 1)
            act.wait_ge(h_weighted, 1)
            n = TOK[ACT_LAST][1]
            nc.scalar.activation(h_tok[0:n, ACT_LAST, :], h_tok[0:n, ACT_LAST, :], ACT.Copy,
                                 scale=rstd[0:n, ACT_LAST:ACT_LAST + 1]).then_inc(h_ready_act, 1)

        @block.vector
        def _(dve):
            own = Tally(dve_self)

            def settled(ins):
                dve.wait_ge(dve_self, own.add(ins))

            def split_lo(step, it=0):
                dve.wait_ge(hi_done, step + 1 + RAW * it)
                n = 1536 if STEP_UQ <= step < STEP_UK else 2048
                nc.vector.tensor_tensor(w_lo[:, step % 2, 0:n], raw[:, step % RAW, 0:n],
                                        w_hi[:, step % 2, 0:n].bitcast(F32), ALU.subtract).then_inc(lo_done, 1)

            def refine(r, v, t):
                settled(nc.vector.tensor_tensor(t, r, r, ALU.mult))
                settled(nc.vector.tensor_tensor(t, t, v, ALU.mult))
                settled(nc.vector.tensor_scalar(t, t, -0.5, 1.5, ALU.mult, ALU.add))
                settled(nc.vector.tensor_tensor(r, r, t, ALU.mult))

            nc.vector.memset(ss[:], 1.0).then_inc(ss_cleared, 1)
            dve.wait_ge(ss_cleared, 1)
            for i, (tt, part) in enumerate(((0, slice(0, D_MODEL)), (2, slice(D_MODEL // 2, D_MODEL)))):
                n = TOK[tt][1]
                dve.wait_ge(x_landed[tt], 16)
                col = (0, 3)[i]
                settled(nc.vector.tensor_tensor_reduce(
                    out=dve_sq[0:n, part], in0=x_tok[0:n, tt, part], in1=x_tok[0:n, tt, part], scale=1.0, scalar=0.0,
                    op0=ALU.mult, op1=ALU.add, accum_out=ss[0:n, col:col + 1]))
            dve.wait_ge(ss_done, 1)
            settled(nc.vector.tensor_tensor(ss[:, 2:3], ss[:, 2:3], ss[:, 3:4], ALU.add))
            nc.vector.tensor_scalar(var[:, 0:3], ss[:, 0:3], 1.0 / D_MODEL, EPS, ALU.mult, ALU.add).then_inc(var_done, 1)
            dve.wait_ge(root_done, 1)
            settled(nc.vector.reciprocal(rstd[:, 0:3], root[:, 0:3]))
            refine(rstd[:, 0:3], var[:, 0:3], root[:, 0:3])
            dve.wait_ge(consts_landed, 32)
            for tt in range(3):
                last = nc.vector.tensor_scalar(diag[:, tt, :], ident[:], rstd[:, tt:tt + 1], None, ALU.mult)
            last.then_inc(diag_done, 1)
            split_lo(0)
            for k in range(KD):
                dve.wait_ge(xhi_done, k + 1)
                nc.vector.scalar_tensor_tensor(out=x_lo[:, k, :], in0=ps[:, 2 + k % 6, 0:NTOK], scalar=norm_g[:, k:k + 1],
                                               in1=x_hi[:, k, :].bitcast(F32), op0=ALU.mult,
                                               op1=ALU.subtract).then_inc(xlo_done, 1)
                if k == LAG_SPLIT:
                    split_lo(1)
            dve.wait_ge(rope_landed, 16)

            def table(i, like):
                return rope_tab[:, i:i + 1, :].broadcast_to(like)

            def rotate(group, dst, kind, mask):
                shape = [P, 2, NTOK]
                dve.wait_ge(pair_read, group + 1)
                z = z_stage[:, group % 2, :, :]
                settled(nc.vector.stream_shuffle(z_shuf[:], z, mask))
                nc.vector.tensor_tensor(z_cos[:], z, table(2 * kind, shape), ALU.mult).then_inc(stage_used, 1)
                settled(nc.vector.tensor_tensor(z_shuf[:], z_shuf[:], table(2 * kind + 1, shape), ALU.mult))
                dve.wait_ge(stage_used, rotated_before(group) + 1)
                nc.vector.tensor_tensor(dst, z_cos[:], z_shuf[:], ALU.add).then_inc(roped, 1)
                dve.wait_ge(roped, roped_by(group))

            for half in range(2):
                split_lo(2 + half)
            dve.wait_ge(xt_ready, KD)
            for t in (ik_t, kr_t):
                for half in range(2):
                    nc.vector.memset(t[64 * (1 - half):64 * (1 - half) + 64, half, :], 0.0)
            dve.wait_ge(pair_read, 1)
            z, zk = z_stage[:, 0, 0, :], z_stage[0:ROPE, 0, 1, :]
            settled(nc.vector.stream_shuffle(z_shuf[0:64, 0, :], z[0:64, :], SWAP_8))
            settled(nc.vector.tensor_copy(ik_z[64:P, :], z[64:P, :]))
            settled(nc.vector.tensor_tensor(z_cos[0:64, 0, :], z[0:64, :], rope_tab[0:64, 2, :], ALU.mult))
            settled(nc.vector.tensor_tensor(z_shuf[0:64, 0, :], z_shuf[0:64, 0, :], rope_tab[0:64, 3, :], ALU.mult))
            settled(nc.vector.tensor_tensor(ik_z[0:64, :], z_cos[0:64, 0, :], z_shuf[0:64, 0, :], ALU.add))
            for half in range(2):
                settled(nc.vector.tensor_copy(ik_t[64 * half:64 * half + 64, half, NEW:NKEY], ik_z[0:64, :]))
            settled(nc.vector.tensor_tensor(z_cos[0:ROPE, 1, :], zk, rope_tab[0:ROPE, 4, :], ALU.mult))
            dve.wait_ge(small_copied, 2)
            settled(nc.vector.tensor_tensor(z_shuf[0:ROPE, 1, :], kr_swap[0:ROPE, :], rope_tab[0:ROPE, 5, :], ALU.mult))
            for half in range(2):
                if half == 1:
                    nc.vector.sem_inc(stage_used, 1)
                settled(nc.vector.tensor_tensor(kr_t[64 * half:64 * half + 64, half, NEW:NKEY], z_cos[0:ROPE, 1, :],
                                                z_shuf[0:ROPE, 1, :], ALU.add))
            nc.vector.sem_inc(roped, 2)
            for g in range(G_IQ, G_AK):
                for half in range(2):
                    split_lo(2 * g + 2 + half)
                rotate(g, iq_t[:, 2 * (g - G_IQ):2 * (g - G_IQ) + 2, :], 1, SWAP_8)

            dve.wait_ge(tr_copied, 3)
            settled(nc.vector.tensor_scalar(iw_tok[0:DEC, 0, :], ik_tok[0:DEC, 0, IDX_DIM:IDX_DIM + IDX_HEADS],
                                            IDX_HEADS ** -0.5, None, ALU.mult))
            settled(nc.vector.tensor_scalar(iw_tok[:, 1:3, :], ik_tok[:, 1:3, IDX_DIM:IDX_DIM + IDX_HEADS],
                                            IDX_HEADS ** -0.5, None, ALU.mult))
            begun = set()
            for i in range(IDX_PIECES):
                if i % 2 == 1:
                    split_lo(STEP_AK + 2 + i // 2)
                if i == 3:
                    rotate(G_AK, ka_t[:, :, NEW:NKEY], 0, SWAP_16)
                for u in units_after(i):
                    tt, heads = IDX_UNITS[u]
                    dve.wait_ge(relu_done, u + 1)
                    n, nk = TOK[tt][1], KEYS[tt][1]
                    for j, h in enumerate(heads):
                        r, s = relu_ring[0:n, u % 4, j * nk:(j + 1) * nk], score[0:n, tt, 0:nk]
                        w = iw_tok[0:n, tt, h:h + 1]
                        if tt not in begun:
                            ins = nc.vector.tensor_scalar(s, r, w, None, ALU.mult)
                            begun.add(tt)
                        else:
                            ins = nc.vector.scalar_tensor_tensor(out=s, in0=r, scalar=w, in1=s, op0=ALU.mult,
                                                                 op1=ALU.add)
                        if j < len(heads) - 1:
                            settled(ins)
                    ins.then_inc(idx_added, 1)
                    dve.wait_ge(idx_added, u + 1)
            for tt in (1, 2):
                settled(nc.vector.memset(score[0:CHUNK, tt, KEYS[tt][1] - CHUNK:KEYS[tt][1]], TAKEN))

            def take_eight(tt, r):
                n, nk = TOK[tt][1], KEYS[tt][1]
                src = score if r == 0 else work
                settled(nc.vector.max(top8[0:n, 0, :], src[0:n, tt, 0:nk]))
                settled(nc.vector.match_replace(work[0:n, tt, 0:nk], top8[0:n, 0, :], src[0:n, tt, 0:nk], TAKEN))

            def selection(tt):
                n, nk = TOK[tt][1], KEYS[tt][1]
                w = work[0:n, tt, 0:nk]
                settled(nc.vector.tensor_tensor(w, w, score[0:n, tt, 0:nk], ALU.not_equal))
                settled(nc.vector.tensor_scalar(w, w, -1.0, -NEG, ALU.add, ALU.mult))

            rounds = [(1, r) for r in range(TOPK_PROMPT // 8)] + [(2, r) for r in range(TOPK_PROMPT // 8)] \
                + [(0, r) for r in range(TOPK_SAMPLE // 8)]
            def take_rounds(i):
                n_steps = 9
                for tt, r in rounds[i * len(rounds) // n_steps:(i + 1) * len(rounds) // n_steps]:
                    take_eight(tt, r)
                if 9 <= i < 12:
                    selection(i - 9)

            for i in range(STEP_FILL_A - STEP_CQ):
                g, half = G_CQ + i // 2, i % 2
                split_lo(STEP_CQ + 2 + i)
                take_rounds(i)
                if g >= G_AQ and half == 1:
                    rotate(g, aq_t[:, 2 * (g - G_AQ):2 * (g - G_AQ) + 2, :], 0, SWAP_16)
                if g == G_AQ and half == 1:
                    for b in range(2):
                        dve.wait_ge(sumsq_ready, b + 1)
                        last = nc.vector.tensor_scalar(lat_var[:, b, :], ps[:, 4 + b, 0:NTOK], 1.0 / LORA, EPS, ALU.mult,
                                                       ALU.add)
                    last.then_inc(lat_var_done, 1)
                if g == G_AQ + 1 and half == 0:
                    dve.wait_ge(lat_root_done, 1)
                    settled(nc.vector.reciprocal(lat_r[:], lat_r[:]))
                    refine(lat_r[:], lat_var[:], z_cos[:])
                if (g, half) in ((G_AQ + 1, 1), (G_AQ + 2, 0)):
                    b = 1 - half
                    for k in range(KL):
                        nc.vector.scalar_tensor_tensor(
                            out=lora_z[:, b, k, :], in0=lora_z[:, b, k, :], scalar=lora_g[:, b, k:k + 1],
                            in1=lat_r[:, b, :], op0=ALU.mult, op1=ALU.mult).then_inc(lat_normed, 1)
                if g == G_CQ + 3 and half == 0:
                    for b in range(2):
                        dve.wait_ge(past_lat_hi, b + 1)
                        cols = slice(2 * b, 2 * b + 2)
                        nc.vector.tensor_tensor(ckv_lo[:, cols, 0:PAST], ps[:, 6 + b, :].rearrange("p (k t) -> p k t", k=2),
                                                ckv_hi[:, cols, 0:PAST].bitcast(F32), ALU.subtract).then_inc(past_lat_lo, 1)
                if g == G_AQ + 2 and half == 1:
                    dve.wait_ge(lat_normed, 2 * KL)
                    dve.wait_ge(lat_hi, 1)
                    nc.vector.tensor_tensor(cq_lo[:], lora_z[:, 0, :, :], cq_hi[:].bitcast(F32), ALU.subtract)\
                        .then_inc(lat_lo, 1)
                if g == G_AQ + 3 and half == 0:
                    dve.wait_ge(lat_hi, 2)
                    nc.vector.tensor_tensor(ckv_lo[:, :, NEW:NKEY], lora_z[:, 1, :, :], ckv_hi[:, :, NEW:NKEY].bitcast(F32),
                                            ALU.subtract).then_inc(lat_lo, 1)
            for q in range(1, 4):
                settled(nc.vector.tensor_copy(work[DEC * q:DEC * q + DEC, 0, :], work[0:DEC, 0, :]))

            def row_max(u):
                branch, kind, _ = UNITS[u]
                nk, bank, i = KEYS[kind][1], 4 + u % 2, u % 2
                dve.wait_ge(scores_ready, u + 1)
                if branch == "A":
                    nc.vector.tensor_tensor_reduce(out=masked[:, i, 0:nk], in0=ps[:, bank, 0:nk], in1=work[:, kind, 0:nk],
                                                   scale=1.0, scalar=TAKEN, op0=ALU.add, op1=ALU.max,
                                                   accum_out=mx[:, i:i + 1]).then_inc(scores_read, 1)
                    dve.wait_ge(scores_read, u + 1)
                else:
                    if kind:
                        settled(nc.vector.memset(ps[0:CHUNK, bank, nk - CHUNK:nk], NEG))
                    settled(nc.vector.tensor_reduce(mx[:, i:i + 1], ps[:, bank, 0:nk], AX_X, ALU.max))
                nc.vector.tensor_scalar(neg_mx[:, i:i + 1], mx[:, i:i + 1], -(A_SCALE if branch == "A" else B_SCALE),
                                        None, ALU.mult).then_inc(neg_ready, 1)

            def normalise(u):
                nk, i = KEYS[UNITS[u][1]][1], u % 2
                probs = (probs_a, probs_b)[u >= N_A]
                dve.wait_ge(p_ready, u + 1)
                settled(nc.vector.reciprocal(inv_p[:, i:i + 1], sum_p[:, i:i + 1]))
                nc.vector.tensor_scalar(probs[:, i, 0:nk], probs[:, i, 0:nk], inv_p[:, i:i + 1], None,
                                        ALU.mult).then_inc(pn_ready, 1)

            def copy_out(u):
                branch, kind, h = UNITS[u]
                t0, n = TOK[kind]
                base = 0 if branch == "A" else 8
                dve.wait_ge(o_ready, u + 1)
                if kind == 0:
                    ins = nc.vector.tensor_copy(o_t[:, base + 4 * h:base + 4 * h + 4, 0:DEC],
                                                ps[:, 7, 0:P].rearrange("p (h t) -> p h t", h=4))
                else:
                    ins = nc.vector.tensor_copy(o_t[:, base + h, t0:t0 + n], ps[:, 7, 0:P])
                ins.then_inc(o_copied, 1)

            def attention(first, end, group, filled):
                row_max(first)
                for u in range(first, end):
                    normalise(u)
                    before = [i for i in pieces(u - first - 1, end - first, filled)]
                    for i in before:
                        if i % 2 == 1:
                            split_lo(steps_of(group) + i // 2 + 2)
                    if u + 1 < end:
                        row_max(u + 1)
                    if u > first:
                        copy_out(u - 1)
                copy_out(end - 1)
                for i in pieces(end - first - 1, end - first, filled):
                    if i % 2 == 1:
                        split_lo(steps_of(group) + i // 2 + 2)

            split_lo(STEP_FILL_A + 2)
            attention(0, N_A, G_FILL_A, FILLED_A)
            for j in range(2, 5):
                split_lo(STEP_UQ + j)
            dve.wait_ge(uq_copied, 12)
            shape = [P, 4, NTOK]
            settled(nc.vector.tensor_tensor(qr_z[:], qr_z[:], table(4, shape), ALU.mult))
            settled(nc.vector.tensor_tensor(qr_swap[:], qr_swap[:], table(5, shape), ALU.mult))
            nc.vector.tensor_tensor(qr_t[:], qr_z[:], qr_swap[:], ALU.add).then_inc(q_roped, 1)
            for j in range(3):
                split_lo(STEP_UK + 1 + j)
            dve.wait_ge(q_roped, 1)
            dve.wait_ge(ckv_out, 48)
            for n in range(10):
                dve.wait_ge(uv_ready, n + 1)
                nc.vector.tensor_copy(vb[:, n % 5, 512 * (n // 5):512 * (n // 5) + 512], ps[:, n % 4, :])\
                    .then_inc(uv_copied, 1)
            for half in range(2):
                split_lo(STEP_FILL_B + half)
            attention(N_A, len(UNITS), G_FILL_B, 0)

            for half in range(2):
                split_lo(STEP_MG + 2 + half)
            with dve.Fori(0, 3) as it:
                for j in range(4):
                    split_lo(STEP_MG + 4 + j, it)
            for half in range(2):
                split_lo(STEP_GATE + half)

            def gated(group, it=0):
                dve.wait_ge(gate_ready, group - G_GATE + 1 + 2 * it)
                t, x = gate_t[:, group % 2, :, :], gate_x[:, group % 2, :, :]
                nc.vector.scalar_tensor_tensor(out=t, in0=t, scalar=1.0, in1=pair(group), op0=ALU.add, op1=ALU.mult)\
                    .then_inc(pair_read, 1)
                dve.wait_ge(pair_read, group + 1 + 2 * it)
                nc.vector.tensor_tensor(x, t, o_t[:, bass.ds(it * 4 + 2 * (group - G_GATE), 2), :], ALU.mult)\
                    .then_inc(gate_used, 1)

            def gated_lo(group, it=0):
                dve.wait_ge(gated_hi_done, group - G_GATE + 1 + 2 * it)
                tiles = bass.ds(it * 4 + 2 * (group - G_GATE), 2)
                nc.vector.tensor_tensor(og_lo[:, tiles, :], gate_x[:, group % 2, :, :], og_hi[:, tiles, :].bitcast(F32),
                                        ALU.subtract).then_inc(gated_lo_done, 1)

            for half in range(2):
                split_lo(STEP_GATE + 2 + half)
            gated(G_GATE)
            with dve.Fori(0, 3) as it:
                for j in range(2, 4):
                    split_lo(STEP_GATE + 2 * j, it)
                    gated_lo(G_GATE + j - 2, it)
                    split_lo(STEP_GATE + 2 * j + 1, it)
                    gated(G_GATE + j - 1, it)
            split_lo(STEP_Y)
            gated_lo(G_END - 2)
            split_lo(STEP_Y + 1)
            gated(G_END - 1)
            gated_lo(G_END - 1)

            def merge_a(j, it=0):
                dve.wait_ge(step_done, STEP_Y + 2 * j + 1 + RAW * it)
                settled(nc.vector.scalar_tensor_tensor(out=y_a[:], in0=merge_g[:, bass.ds(it * 4 + 2 * j, 2), :],
                                                       scalar=1.0, in1=ps[:, 0:2, 0:NTOK], op0=ALU.add, op1=ALU.mult))
                nc.vector.sem_inc(y_read, 1)

            def merge_b(j, it=0):
                dve.wait_ge(step_done, STEP_Y + 2 * j + 2 + RAW * it)
                tiles = bass.ds(it * 4 + 2 * j, 2)
                nc.vector.scalar_tensor_tensor(out=y_b[:], in0=merge_g[:, bass.ds(it * 4 + 16 + 2 * j, 2), :],
                                               scalar=1.0, in1=ps[:, 2:4, 0:NTOK], op0=ALU.add, op1=ALU.mult)\
                    .then_inc(y_read, 1)
                dve.wait_ge(y_read, 2 * j + 2 + 4 * it)
                settled(nc.vector.tensor_tensor(y_a[:], y_a[:], y_b[:], ALU.add))
                settled(nc.vector.tensor_copy(m_hi[:, tiles, :], y_a[:]))
                nc.vector.tensor_tensor(m_lo[:, tiles, :], y_a[:], m_hi[:, tiles, :].bitcast(F32),
                                        ALU.subtract).then_inc(m_done, 1)
                dve.wait_ge(m_done, j + 1 + 2 * it)

            merge_a(0)
            split_lo(STEP_Y + 2)
            merge_b(0)
            split_lo(STEP_Y + 3)
            merge_a(1)
            with dve.Fori(0, 3) as it:
                own.enter(it, 6)
                for j in range(2, 4):
                    split_lo(STEP_Y + 2 * j, it)
                    merge_b(j - 1, it)
                    split_lo(STEP_Y + 2 * j + 1, it)
                    merge_a(j, it)
            own.leave(3)
            split_lo(STEP_OUT)
            merge_b(7)
            split_lo(STEP_OUT + 1)

            def add_residual(j):
                dve.wait_ge(ht_ready, j + 1)
                if j >= 2:
                    dve.wait_ge(h_squared, 3 * (j - 1))
                cols = slice(256 * j, 256 * j + 256)
                for tt, (_, n) in enumerate(TOK):
                    last = nc.vector.tensor_tensor(h_sum[0:n, j % 2, tt, :], h_tok[0:n, tt, cols],
                                                   ps[0:n, 4 + tt, 0:256], ALU.add)
                last.then_inc(h_added, 1)
                dve.wait_ge(h_added, j + 1)
                for tt, (_, n) in enumerate(TOK):
                    last = nc.vector.tensor_tensor(h_tok[0:n, tt, cols], h_sum[0:n, j % 2, tt, :],
                                                   final_g[0:n, cols], ALU.mult)
                return last

            for half in range(2):
                split_lo(STEP_OUT + 2 + half)
            nc.vector.memset(h_ss[:], 1.0).then_inc(h_cleared, 1)
            dve.wait_ge(res_landed, 48)
            dve.wait_ge(fg_landed, 16)
            for j in range(2, 8):
                for half in range(2):
                    split_lo(STEP_OUT + 2 * j + half)
                add_residual(j - 2)
            add_residual(6)
            add_residual(7).then_inc(h_weighted, 1)

            dve.wait_ge(h_squared, 24)
            settled(nc.vector.tensor_reduce(ss[:, 0:3], h_ss[:], AX_X, ALU.add))
            nc.vector.tensor_scalar(var[:, 0:3], ss[:, 0:3], 1.0 / D_MODEL, EPS, ALU.mult, ALU.add)\
                .then_inc(h_var_done, 1)
            dve.wait_ge(h_root_done, 1)
            settled(nc.vector.reciprocal(rstd[:, 0:3], root[:, 0:3]))
            refine(rstd[:, 0:3], var[:, 0:3], root[:, 0:3])
            nc.vector.sem_inc(h_rstd, 1)
            dve.wait_ge(h_weighted, 1)
            for i, tt in enumerate(DVE_LAST):
                n = TOK[tt][1]
                nc.vector.tensor_scalar(h_tok[0:n, tt, :], h_tok[0:n, tt, :], rstd[0:n, tt:tt + 1], None, ALU.mult)\
                    .then_inc(h_ready, 1)


def rope_tables():
    pos = np.concatenate([PAST + np.arange(DEC), np.arange(SEQ)]).astype(np.float32)
    tables = np.zeros((6, P, NTOK), np.float32)
    for kind, (width, rot) in enumerate(((A_DIM, A_DIM // 4), (IDX_DIM, IDX_DIM // 4), (ROPE, ROPE))):
        half = rot // 2
        freq = (np.float32(ROPE_THETA) ** (-np.arange(half, dtype=np.float32) * np.float32(2.0 / rot))).astype(np.float32)
        angle = (freq[:, None] * pos[None, :]).astype(np.float32)
        tables[2 * kind] = 1.0
        for start in range(0, P, width):
            tables[2 * kind, start:start + half] = np.cos(angle)
            tables[2 * kind, start + half:start + rot] = np.cos(angle)
            tables[2 * kind + 1, start:start + half] = -np.sin(angle)
            tables[2 * kind + 1, start + half:start + rot] = np.sin(angle)
    return tables


OUTPUTS = [("y_prompt", (SEQ, D_MODEL)), ("y_sample", (DEC, D_MODEL))] + [
    (f"{name}_{part}", (n, width)) for part, n in (("prompt", SEQ), ("sample", DEC))
    for name, width in (("new_a_k", 256), ("new_a_v", 256), ("new_idx_k", IDX_DIM), ("new_ckv", LORA),
                        ("new_krope", ROPE))]
SHAPES = [(1, SEQ, D_MODEL), (1, DEC, D_MODEL)] + [
    (1, 1, n, *width) for n in (SEQ, DEC)
    for width in ((A_KV, A_DIM), (A_KV, A_DIM), (IDX_DIM,), (LORA,), (ROPE,))]


def kernel(**inputs):
    import concourse.bacc as bacc
    from concourse.bass_utils import run_bass_kernel_spmd

    flat = {
        "x_prompt": (SEQ, D_MODEL), "x_sample": (DEC, D_MODEL), "cache_a_k": (PAST, 256), "cache_a_v": (PAST, 256),
        "cache_idx_k": (PAST, IDX_DIM), "cache_mla_ckv": (PAST, LORA), "cache_mla_krope": (PAST, ROPE),
        "norm_g": (D_MODEL,), "w_in": (D_MODEL, PROJ), "w_uq": (LORA, 1536), "q_norm_g": (LORA,),
        "kv_norm_g": (LORA,), "w_uk": (LORA, 1024), "w_uv": (LORA, 1024), "w_o_a": (1024, D_MODEL),
        "w_o_b": (1024, D_MODEL), "w_out": (D_MODEL, D_MODEL), "final_g": (D_MODEL,)}
    arrays = {f"in_{k}": np.ascontiguousarray(np.asarray(inputs[k]).reshape(s)) for k, s in flat.items()}
    uq = arrays["in_w_uq"].reshape(LORA, 4, 2, NOPE + ROPE)
    arrays["in_w_uq"] = np.concatenate([uq[..., :NOPE].reshape(LORA, 4, -1), uq[..., NOPE:].reshape(LORA, 4, -1)],
                                       axis=2).reshape(LORA, -1)
    for name in ("norm_g", "q_norm_g", "kv_norm_g"):
        arrays[f"in_{name}"] = np.ascontiguousarray(arrays[f"in_{name}"].reshape(-1, P).T)
    arrays["in_ident"] = np.eye(P, dtype=np.float32)
    arrays["in_rope_tab"] = rope_tables()

    nc = bacc.Bacc("TRN2", target_bir_lowering=False, num_devices=1)
    d = {k[3:]: nc.dram_tensor(k, a.shape, F32, kind="ExternalInput").ap() for k, a in arrays.items()}
    for name, shape in OUTPUTS:
        d[name] = nc.dram_tensor(f"out_{name}", shape, F32, kind="ExternalOutput").ap()
    hybrid_layer(nc, d)
    got = run_bass_kernel_spmd(nc, [arrays], core_ids=[0]).results[0]
    return tuple(got[f"out_{name}"].reshape(shape) for (name, _), shape in zip(OUTPUTS, SHAPES))
```

```python
from contextlib import ExitStack

import numpy as np

import concourse.bass as bass
from concourse import mybir

F32 = mybir.dt.float32
F32R = mybir.dt.float32r
ALU = mybir.AluOpType
ACT = mybir.ActivationFunctionType
AX_X = mybir.AxisListType.X

P = 128
D_MODEL = 2048
SEQ, DEC, PAST = 256, 32, 256
NTOK = DEC + SEQ
NKEY = PAST + NTOK
CHUNK = 64
EPS = 1e-6
ROPE_THETA = 500000.0
A_HEADS, A_KV, A_DIM = 8, 2, 128
GRP = A_HEADS // A_KV
IDX_HEADS, IDX_DIM = 16, 64
B_HEADS, NOPE, ROPE = 8, 128, 64
LORA = 512
KD = D_MODEL // P
KL = LORA // P
KH = KD // 2
TOPK_PROMPT = SEQ // 4
TOPK_SAMPLE = (PAST + DEC) // 4
NEG = -1e30
TAKEN = -3e38
A_SCALE = A_DIM ** -0.5
B_SCALE = (NOPE + ROPE) ** -0.5

COL_AQ, COL_AK, COL_AV, COL_AGATE, COL_IQ, COL_IK, COL_IW, COL_CQ, COL_CKV, COL_KR, COL_BGATE, COL_MG, PROJ = (
    0, 1024, 1280, 1536, 2560, 3584, 3648, 3664, 4176, 4688, 4752, 5776, 9872)

TOK = [(0, DEC), (DEC, P), (DEC + P, P)]
NEW = PAST
PROMPT = PAST + DEC

LAG = 4
SPLIT_AT = {3: 1, KD // 2 + LAG: 2}

DVE_LAST, ACT_LAST = (1, 0), 2

RAW = 4
G_SMALL, G_IQ, G_AK, G_AV, G_CQ, G_AQ, G_FILL_A, G_FILL_B, G_MG, G_GATE, G_END = 0, 1, 5, 6, 7, 11, 15, 19, 23, 31, 39
STEP_AK = 2 * G_AK
STEP_CQ = 2 * G_CQ
STEP_FILL_A = 2 * G_FILL_A
STEP_UQ = 2 * G_FILL_B
STEP_UK = STEP_UQ + 4
STEP_UV = STEP_UK + 2
STEP_FILL_B = STEP_UV + 2
LATE = STEP_FILL_B - STEP_UQ
STEP_MG = STEP_FILL_B + 8
STEP_GATE = STEP_MG + 16
STEP_Y = STEP_GATE + 16
STEP_OUT = STEP_Y + 16


def steps_of(group):
    return 2 * group + (LATE if group >= G_FILL_B else 0)


def merge_tile(group):
    return {G_FILL_A: 8, G_FILL_B: 0, G_MG: 16}[max(g for g in (G_FILL_A, G_FILL_B, G_MG) if g <= group)] \
        + 2 * (group - max(g for g in (G_FILL_A, G_FILL_B, G_MG) if g <= group))


class Tally:

    def __init__(self, sem):
        self.sem, self.n, self.it, self.per = sem, 0, None, 0

    def add(self, ins):
        ins.then_inc(self.sem, 1)
        self.n += 1
        return self.now()

    def now(self):
        return self.n if self.it is None else self.it * self.per + self.n

    def enter(self, it, per):
        self.it, self.per, self.start = it, per, self.n

    def leave(self, turns):
        assert self.n - self.start == self.per, (self.n - self.start, self.per)
        self.n, self.it = self.start + self.per * turns, None


def attention_units():
    units = []
    for g in range(A_KV):
        units.append(("A", 0, g))
        units += [("A", kind, h) for h in range(GRP * g, GRP * g + GRP) for kind in (1, 2)]
    for g in range(2):
        units.append(("B", 0, g))
        units += [("B", kind, h) for h in range(4 * g, 4 * g + 4) for kind in (1, 2)]
    return units


HALF_TILE = KH
FILLING = 4 * 4 * HALF_TILE


def filling(turn, units, filled):
    left = FILLING - filled
    return range(filled + turn * left // (units + 1), filled + (turn + 1) * left // (units + 1)) if turn >= 0 else ()


UNITS = attention_units()
N_A = sum(u[0] == "A" for u in UNITS)
KEYS = [(0, PAST + DEC), (PROMPT, P), (PROMPT, 2 * P)]
KEY_TILES = [[(0, P, 0), (P, P, 1), (2 * P, DEC, 2)], [(0, P, 3)], [(0, P, 3), (P, P, 4)]]
V_TILES = [0, P, NEW, PROMPT, PROMPT + P]


def indexer_units():
    return [(tt, tuple(range(h, h + n))) for tt, n in ((1, 4), (2, 2), (0, 1)) for h in range(0, IDX_HEADS, n)]


IDX_UNITS = indexer_units()
IDX_PIECES = 8
FILLED_A = 14


def units_after(piece):
    turns = IDX_PIECES - 1
    return range((piece - 1) * len(IDX_UNITS) // turns, piece * len(IDX_UNITS) // turns) if piece else ()


def rotated_before(group):
    return group - (G_AQ - G_AV if group >= G_AQ else 0)


def roped_by(group):
    return rotated_before(group) + 2


SWAP_16 = [(i + 16) % 32 for i in range(32)]
SWAP_8 = [(i + 8) % 16 if i < 16 else i for i in range(32)]


def hybrid_layer(nc, d):
    def rows(ap, k):
        return ap.rearrange("(k p) n -> p k n", p=P)

    w_in = rows(d["w_in"], KD)
    w_uq = d["w_uq"].rearrange("(k p) n -> p k n", p=P)
    w_uk = d["w_uk"].rearrange("(k p) n -> p k n", p=P)
    w_uv = d["w_uv"].rearrange("(k p) n -> p k n", p=P)
    w_oa = rows(d["w_o_a"], 8)
    w_ob = rows(d["w_o_b"], 8)
    w_out = rows(d["w_out"], KD)

    ctx = ExitStack()
    with ctx:
        def sem(name):
            return ctx.enter_context(nc.semaphore(name))

        def at(name, shape, offset, dtype=F32):
            t = nc.alloc_sbuf_tensor_at(name, shape, dtype, offset=offset)
            end = offset + 4 * int(np.prod(shape[1:]))
            assert end <= nc.sbuf_usable_end, (name, end)
            return t, end

        def row(start, *parts):
            made = []
            for name, shape, *dtype in parts:
                t, start = at(name, shape, start, *dtype)
                start = -(-start // 32) * 32
                made.append(t)
            return (*made, start)

        (x_hi, x_lo, raw, w_hi, w_lo, ident, ones, rope_tab, norm_g, lora_g, ss, var, root, rstd,
         mx, neg_mx, sum_p, inv_p, o_base) = row(
            -(-nc.sbuf_base // 64) * 64,
            ("x_hi", [P, KD, NTOK], F32R), ("x_lo", [P, KD, NTOK], F32R), ("raw", [P, RAW, 2048]),
            ("w_hi", [P, 2, 2048], F32R), ("w_lo", [P, 2, 2048], F32R), ("ident_sb", [P, P]), ("ones", [P, P]),
            ("rope_sb", [P, 6, NTOK]), ("norm_g_sb", [P, KD]), ("lora_g", [P, 2, KL]), ("ss", [P, 4]),
            ("var", [P, 4]), ("root", [P, 4]), ("rstd", [P, 4]), ("mx", [P, 2]),
            ("neg_mx", [P, 2]), ("sum_p", [P, 2]), ("inv_p", [P, 2]))
        o_t, arena = at("o_t", [P, 16, NTOK], o_base)
        z_stage, z_shuf, z_cos, sq_z, lat_var, lat_r, _ = row(
            o_base, ("z_stage", [P, 2, 2, NTOK]), ("z_shuf", [P, 2, NTOK]), ("z_cos", [P, 2, NTOK]),
            ("sq_z", [P, KL, NTOK]), ("lat_var", [P, 2, NTOK]), ("lat_r", [P, 2, NTOK]))
        og_lo, _ = at("og_lo", [P, 16, NTOK], o_base, F32R)

        at_x = arena + 8 * NKEY
        at_f = at_x + 18432
        at_y = at_f + 32 * NTOK
        at_v = at_y + 32 * NTOK + 32 * NKEY + 16 * NTOK

        kr_t, _ = at("kr_t", [P, 2, NKEY], arena)
        x_tok, _ = at("x_tok", [P, 3, D_MODEL], at_y)
        x_sq, dve_sq, diag, d_end = row(at_x, ("x_sq", [P, 2, D_MODEL]), ("dve_sq", [P, D_MODEL]), ("diag", [P, 3, P]))
        assert d_end <= at_y
        probs_a, masked, probs_ta, aq_t, ka_t, va_past, kv_tok, work, at_l = row(
            at_y, ("probs_a", [P, 2, PAST + DEC]), ("masked", [P, 2, PAST + DEC]), ("probs_ta", [P, 2, 3, P]),
            ("aq_t", [P, 8, NTOK]), ("ka_t", [P, A_KV, NKEY]), ("va_past", [P, 2, 256]), ("kv_tok", [P, 3, 512]),
            ("work", [P, 3, PAST + DEC]))
        cq_hi, cq_lo, ckv_tok, iw_tok, top8, ik_tok, kr_tok, _ = row(
            at_l, ("cq_hi", [P, KL, NTOK], F32R), ("cq_lo", [P, KL, NTOK], F32R), ("ckv_tok", [P, 3, LORA]),
            ("iw_tok", [P, 3, IDX_HEADS]), ("top8", [P, 2, 8]), ("ik_tok", [P, 3, P]), ("kr_tok", [P, 3, ROPE]))
        ckv_past, score, s_end = row(at_y, ("ckv_past", [P, 2, LORA]), ("score", [P, 3, PAST + DEC]))
        relu_ring, _ = at("relu_ring", [P, 4, 512], at_l)
        k_past, idx_past, kr_past, _ = row(
            at_l + 32 * NTOK, ("k_past", [P, 2, 256]), ("idx_past", [P, 2, 2 * IDX_DIM]), ("kr_past", [P, 2, 2 * ROPE]))
        iq_t, _ = at("iq_t", [P, 8, NTOK], at_f)
        lora_z, _ = at("lora_z", [P, 2, KL, NTOK], at_f)
        ik_t, ik_z, kr_swap, _ = row(at_x, ("ik_t", [P, 2, NKEY]), ("ik_z", [P, NTOK]), ("kr_swap", [P, NTOK]))
        ckv_hi, ckv_lo, _ = row(at_x, ("ckv_hi", [P, KL, NKEY], F32R), ("ckv_lo", [P, KL, NKEY], F32R))
        probs_b, probs_tb, p_end = row(at_x, ("probs_b", [P, 2, PAST + DEC]), ("probs_tb", [P, 2, 3, P]))
        assert p_end <= at_f - 32 * NTOK
        qn_t, kb_t, qr_z, v_start = row(
            at_y, ("qn_t", [P, 8, NTOK]), ("kb_t", [P, B_HEADS, NKEY]), ("qr_z", [P, 4, NTOK]))
        assert v_start == at_v
        qr_t = qr_z
        vb, _ = at("vb", [P, 5, 1024], at_v)
        qr_swap, _ = at("qr_swap", [P, 4, NTOK], at_l + 32 * NTOK)
        merge_g, _ = at("merge_g", [P, 32, NTOK], at_f - 32 * NTOK)
        og_hi, gate_t, gate_x, y_a, y_b, _ = row(
            at_y + 64 * NTOK, ("og_hi", [P, 16, NTOK], F32R), ("gate_t", [P, 2, 2, NTOK]),
            ("gate_x", [P, 2, 2, NTOK]), ("y_a", [P, 2, NTOK]), ("y_b", [P, 2, NTOK]))
        m_hi, m_lo = x_hi, x_lo
        h_tok, _ = at("h_tok", [P, 3, D_MODEL], at_f - 32 * NTOK)
        final_g, h_stage, h_sum, h_sq, h_ss, _ = row(
            at_y + 64 * NTOK, ("final_g_sb", [P, D_MODEL]), ("h_stage", [P, 2, 2, NTOK]),
            ("h_sum", [P, 2, 3, 256]), ("h_sq", [P, 256]), ("h_ss", [P, 3, 8]))

        ps = ctx.enter_context(nc.psum_tensor("ps", [P, 8, 512], F32))

        def pair(n):
            return ps[:, 2 * (n % 2):2 * (n % 2) + 2, 0:NTOK]

        raw_landed = [sem(f"raw_landed{i}") for i in range(RAW)]
        hi_done, lo_done, step_done = sem("hi_done"), sem("lo_done"), sem("step_done")
        pair_read, stage_used = sem("pair_read"), sem("stage_used")
        x_landed = [sem(f"x_landed{i}") for i in range(3)]
        halves_cleared = sem("halves_cleared")
        rope_landed, lora_g_landed = sem("rope_landed"), sem("lora_g_landed")
        consts_landed, past_landed, va_landed = sem("consts_landed"), sem("past_landed"), sem("va_landed")
        ckv_past_landed, res_landed, fg_landed = sem("ckv_past_landed"), sem("res_landed"), sem("fg_landed")
        ss_done, var_done, root_done, diag_done = (sem(n) for n in ("ss_done", "var_done", "root_done", "diag_done"))
        xt_ready, xhi_done, xlo_done = sem("xt_ready"), sem("xhi_done"), sem("xlo_done")
        small_copied, roped, tr_ready, tr_copied = (sem(n) for n in ("small_copied", "roped", "tr_ready", "tr_copied"))
        idx_ready, relu_done, idx_added = sem("idx_ready"), sem("relu_done"), sem("idx_added")
        sq_done, sumsq_ready, lat_var_done, lat_root_done, lat_normed = (
            sem(n) for n in ("sq_done", "sumsq_ready", "lat_var_done", "lat_root_done", "lat_normed"))
        lat_hi, lat_lo, past_lat_ready, past_lat_hi, past_lat_lo, tok_ready, tok_copied = (
            sem(n) for n in ("lat_hi", "lat_lo", "past_lat_ready", "past_lat_hi", "past_lat_lo", "tok_ready",
                             "tok_copied"))
        h_weighted, h_rstd, h_ready_act = sem("h_weighted"), sem("h_rstd"), sem("h_ready_act")
        ones_set, ss_cleared, h_cleared = sem("ones_set"), sem("ss_cleared"), sem("h_cleared")
        scores_ready, scores_read, neg_ready, p_ready, pn_ready = (
            sem(n) for n in ("scores_ready", "scores_read", "neg_ready", "p_ready", "pn_ready"))
        pt_ready, pt_copied, o_ready, o_copied = (sem(n) for n in ("pt_ready", "pt_copied", "o_ready", "o_copied"))
        uq_ready, uq_copied, q_roped = sem("uq_ready"), sem("uq_copied"), sem("q_roped")
        uk_ready, uk_copied, uv_ready, uv_copied = (sem(n) for n in ("uk_ready", "uk_copied", "uv_ready", "uv_copied"))
        gate_ready, gate_used, gated_hi_done, gated_lo_done = (
            sem(n) for n in ("gate_ready", "gate_used", "gated_hi_done", "gated_lo_done"))
        y_read, m_done = sem("y_read"), sem("m_done")
        hT_copied, ht_ready, h_added, h_squared, h_ready = (
            sem(n) for n in ("hT_copied", "ht_ready", "h_added", "h_squared", "h_ready"))
        h_var_done, h_root_done = sem("h_var_done"), sem("h_root_done")
        dve_self = sem("dve_self")
        kv_out, ckv_out, y_out = sem("kv_out"), sem("ckv_out"), sem("y_out")

        block = ctx.enter_context(nc.Block())

        def landed(step, it=0):
            return 16 * (step // RAW + 1) + (16 if step % RAW < 2 else 0) + 16 * it

        @block.sync
        def _(sp):
            for tt, (t0, n) in enumerate(TOK):
                src = d["x_sample"] if tt == 0 else d["x_prompt"][t0 - DEC:t0 - DEC + n, :]
                sp.dma_start(x_tok[0:n, tt, :], src).then_inc(x_landed[tt], 16)

            def load(step, src, it=0, part=slice(0, 2048)):
                if step >= RAW:
                    sp.wait_ge(lo_done, step - RAW + 1 + RAW * it)
                dst = raw[:, step % RAW, part].rearrange("p (k n) -> p k n", k=src.shape[1])
                sp.dma_start(dst, src).then_inc(raw_landed[step % RAW], 16)

            def load_w_in(group, turns, col):
                with sp.Fori(0, turns) as it:
                    for j in range(4):
                        load(steps_of(group) + j, w_in[:, KH * (j % 2):KH * (j % 2) + KH,
                                                       bass.ds(it * 512 + (col + 256 * (j // 2)), 256)], it)

            for half in range(2):
                dst = raw[:, half, :].rearrange("p (k n) -> p k n", k=KH)
                for m, col in enumerate((COL_IK, COL_KR)):
                    sp.dma_start(dst[:, :, m * P:(m + 1) * P],
                                 w_in[:, KH * half:KH * half + KH, col:col + P]).then_inc(raw_landed[half], 16)
            for j in range(8):
                col = COL_IQ + 256 * (j // 2)
                load(steps_of(G_IQ) + j, w_in[:, KH * (j % 2):KH * (j % 2) + KH, col:col + 256])
            for j in range(4):
                col = COL_AK + 256 * (j // 2)
                load(STEP_AK + j, w_in[:, KH * (j % 2):KH * (j % 2) + KH, col:col + 256])
            load_w_in(G_CQ, 2, COL_CQ)
            load_w_in(G_AQ, 2, COL_AQ)
            load_w_in(G_FILL_A, 2, COL_MG + P * merge_tile(G_FILL_A))
            for j in range(4):
                load(STEP_UQ + j, w_uq[:, :, 384 * j:384 * j + 384], part=slice(0, 4 * 384))
            for j in range(2):
                load(STEP_UK + j, w_uk[:, :, 512 * j:512 * j + 512])
            for j in range(2):
                load(STEP_UV + j, w_uv[:, :, 512 * j:512 * j + 512])
            load_w_in(G_FILL_B, 2, COL_MG + P * merge_tile(G_FILL_B))
            load_w_in(G_MG, 4, COL_MG + P * merge_tile(G_MG))
            load_w_in(G_GATE, 2, COL_AGATE)
            load_w_in(G_GATE + 4, 2, COL_BGATE)
            with sp.Fori(0, 4) as it:
                for j in range(4):
                    w = (w_oa, w_ob)[j % 2]
                    load(STEP_Y + j, w[:, :, bass.ds(it * 512 + 256 * (j // 2), 256)], it)
            with sp.Fori(0, 4) as it:
                for j in range(4):
                    load(STEP_OUT + j, w_out[:, KH * (j % 2):KH * (j % 2) + KH,
                                             bass.ds(it * 512 + 256 * (j // 2), 256)], it)
            for tt, half, by_act, count in ((1, 0, False, 1), (2, 0, True, 1), (1, 1, False, 2), (2, 1, True, 2),
                                            (0, 0, False, 3), (0, 1, False, 4)):
                (t0, n) = TOK[tt]
                if by_act:
                    sp.wait_ge(h_ready_act, count)
                else:
                    sp.wait_ge(h_ready, count)
                cols = slice(half * D_MODEL // 2, (half + 1) * D_MODEL // 2)
                dst = d["y_sample"] if tt == 0 else d["y_prompt"][t0 - DEC:t0 - DEC + n, :]
                sp.dma_start(dst[:, cols], h_tok[0:n, tt, cols]).then_inc(y_out, 16)
            sp.wait_ge(y_out, 6 * 16)

        @block.gpsimd
        def _(pool):
            pool.memset(ones[:], 1.0).then_inc(ones_set, 1)
            pool.dma_start(ident[:], d["ident"]).then_inc(consts_landed, 16)
            pool.dma_start(norm_g[:], d["norm_g"]).then_inc(consts_landed, 16)
            pool.wait_ge(x_landed[2], 16)
            pool.dma_start(rope_tab[:], d["rope_tab"].rearrange("c p t -> p c t")).then_inc(rope_landed, 16)
            for b, name in enumerate(("q_norm_g", "kv_norm_g")):
                pool.dma_start(lora_g[:, b, :], d[name]).then_inc(lora_g_landed, 16)
            pool.dma_start(k_past[:], rows(d["cache_a_k"], 2)).then_inc(past_landed, 16)
            for dup in range(2):
                pool.dma_start(idx_past[:, :, IDX_DIM * dup:IDX_DIM * dup + IDX_DIM],
                               rows(d["cache_idx_k"], 2)).then_inc(past_landed, 16)
                pool.dma_start(kr_past[:, :, ROPE * dup:ROPE * dup + ROPE],
                               rows(d["cache_mla_krope"], 2)).then_inc(past_landed, 16)
            pool.wait_ge(xt_ready, KD)
            for t in (ik_t, kr_t):
                for half in range(2):
                    pool.memset(t[64 * (1 - half):64 * (1 - half) + 64, half, :], 0.0).then_inc(halves_cleared, 1)
            pool.dma_start(va_past[:], rows(d["cache_a_v"], 2)).then_inc(va_landed, 16)
            pool.dma_start(ckv_past[:], rows(d["cache_mla_ckv"], 2)).then_inc(ckv_past_landed, 16)
            pool.wait_ge(tr_copied, 7)
            for tt, (t0, n) in enumerate(TOK):
                def out(name):
                    return d[name + "_sample"] if tt == 0 else d[name + "_prompt"][t0 - DEC:t0 - DEC + n, :]
                pool.dma_start(out("new_a_k"), kv_tok[0:n, tt, 0:256]).then_inc(kv_out, 16)
                pool.dma_start(out("new_a_v"), kv_tok[0:n, tt, 256:512]).then_inc(kv_out, 16)
                pool.dma_start(out("new_idx_k"), ik_tok[0:n, tt, 0:IDX_DIM]).then_inc(kv_out, 16)
                pool.dma_start(out("new_krope"), kr_tok[0:n, tt, :]).then_inc(kv_out, 16)
            pool.wait_ge(tok_copied, 3)
            for tt, (t0, n) in enumerate(TOK):
                dst = d["new_ckv_sample"] if tt == 0 else d["new_ckv_prompt"][t0 - DEC:t0 - DEC + n, :]
                pool.dma_start(dst, ckv_tok[0:n, tt, :]).then_inc(ckv_out, 16)
            pool.wait_ge(m_done, 8)
            for tt, (t0, n) in enumerate(TOK):
                src = d["x_sample"] if tt == 0 else d["x_prompt"][t0 - DEC:t0 - DEC + n, :]
                pool.dma_start(h_tok[0:n, tt, :], src).then_inc(res_landed, 16)
            pool.dma_start(final_g[:], d["final_g"].rearrange("(a n) -> a n", a=1).partition_broadcast(P))\
                .then_inc(fg_landed, 16)
            pool.wait_ge(kv_out, 12 * 16)
            pool.wait_ge(ckv_out, 48)

        @block.tensor
        def _(pe):
            def three(out, hi, lo, x_h, x_l, first, last):
                nc.tensor.matmul(out, hi, x_h, start=first, stop=False)
                nc.tensor.matmul(out, hi, x_l, start=False, stop=False)
                return nc.tensor.matmul(out, lo, x_h, start=False, stop=last)

            def weights(step, k):
                cols = 1536 if STEP_UQ <= step < STEP_UK else 2048
                return [w[:, step % 2, 0:cols].rearrange("p (k n) -> p k n", k=k) for w in (w_hi, w_lo)]

            def tile_part(step, group, half, m, ks, x_h, x_l):
                hi, lo = weights(step, KH)
                cols = slice(m * P, (m + 1) * P)
                for k in ks:
                    last = three(pair(group)[:, m, :], hi[:, k, cols], lo[:, k, cols], x_h[:, KH * half + k, :],
                                 x_l[:, KH * half + k, :], half == 0 and k == 0, half == 1 and k == KH - 1)
                return last

            def half_group(step, group, half, x_h, x_l, it=0):
                pe.wait_ge(lo_done, step + 1 + RAW * it)
                tile_part(step, group, half, 0, range(KH), x_h, x_l)
                tile_part(step, group, half, 1, range(KH), x_h, x_l).then_inc(step_done, 1)

            def fill(first_group, part):
                for i in part:
                    quarter, k = i // HALF_TILE, i % HALF_TILE
                    group, half, m = first_group + quarter // 4, quarter // 2 % 2, quarter % 2
                    if quarter % 4 == 0 and k == 0:
                        pe.wait_ge(pair_read, group - 1)
                        if group in (G_FILL_B, G_FILL_B + 1):
                            pe.wait_ge(uv_copied, 10)
                    if m == 0 and k == 0:
                        pe.wait_ge(lo_done, steps_of(group) + half + 1)
                    last = tile_part(steps_of(group) + half, group, half, m, [k], x_hi, x_lo)
                    if m == 1 and k == HALF_TILE - 1:
                        last.then_inc(step_done, 1)

            def w_in_group(group, it=0):
                if group >= 2:
                    pe.wait_ge(pair_read, group - 1 + 2 * it)
                for half in range(2):
                    half_group(steps_of(group) + half, group, half, x_hi, x_lo, it)

            def w_in_groups(group, turns):
                with pe.Fori(0, turns) as it:
                    for j in range(2):
                        w_in_group(group + j, it)

            small = pair(G_SMALL)
            pe.wait_ge(diag_done, 1)
            for k in range(KD + LAG):
                if k < KD:
                    if k >= 6:
                        pe.wait_ge(xlo_done, k - 5)
                    for tt, (t0, n) in enumerate(TOK):
                        last = nc.tensor.matmul(ps[:, 2 + k % 6, t0:t0 + n], x_tok[0:n, tt, k * P:(k + 1) * P],
                                                diag[0:n, tt, 0:n], start=True, stop=True)
                    last.then_inc(xt_ready, 1)
                if k >= LAG:
                    kk = k - LAG
                    half, row_tile = kk // KH, kk % KH
                    if row_tile == 0:
                        pe.wait_ge(lo_done, half + 1)
                    pe.wait_ge(xlo_done, kk + 1)
                    hi, lo = weights(half, KH)
                    for m in range(2):
                        cols = slice(m * P, (m + 1) * P)
                        last = three(small[:, m, :], hi[:, row_tile, cols], lo[:, row_tile, cols], x_hi[:, kk, :],
                                     x_lo[:, kk, :], kk == 0, kk == KD - 1)
                    if row_tile == KH - 1:
                        last.then_inc(step_done, 1)
            w_in_groups(G_IQ, 2)

            pe.wait_ge(past_landed, 80)
            for g in range(A_KV):
                for t in range(2):
                    last = nc.tensor.transpose(ps[:, 4, (2 * g + t) * P:(2 * g + t + 1) * P],
                                               k_past[:, t, g * P:(g + 1) * P], ident[:])
            last.then_inc(tr_ready, 1)
            for i, past in enumerate((idx_past, kr_past)):
                for t in range(2):
                    last = nc.tensor.transpose(ps[:, 5, (2 * i + t) * P:(2 * i + t + 1) * P], past[:, t, :], ident[:])
            last.then_inc(tr_ready, 1)
            pe.wait_ge(roped, 2)
            for tt, (t0, n) in enumerate(TOK):
                last = nc.tensor.transpose(ps[0:n, 6, tt * P:(tt + 1) * P], ik_z[:, t0:t0 + n], ident[:])
            last.then_inc(tr_ready, 1)
            for tt, (t0, n) in enumerate(TOK):
                last = nc.tensor.transpose(ps[0:n, 7, tt * ROPE:(tt + 1) * ROPE], kr_t[0:ROPE, 0, NEW + t0:NEW + t0 + n],
                                           ident[0:ROPE, 0:ROPE])
            last.then_inc(tr_ready, 1)

            for i in range(IDX_PIECES):
                fill(G_AK, range(i * HALF_TILE, (i + 1) * HALF_TILE))
                if i == 1:
                    pe.wait_ge(tr_copied, 4)
                    pe.wait_ge(roped, 2 + G_AK - G_IQ)
                for u in units_after(i):
                    tt, heads = IDX_UNITS[u]
                    if u >= 4:
                        pe.wait_ge(relu_done, u - 3)
                    (t0, n), (k0, nk) = TOK[tt], KEYS[tt]
                    for j, h in enumerate(heads):
                        last = nc.tensor.matmul(ps[0:n, 4 + u % 4, j * nk:(j + 1) * nk], iq_t[:, h // 2, t0:t0 + n],
                                                ik_t[:, h % 2, k0:k0 + nk], start=True, stop=True)
                    last.then_inc(idx_ready, 1)

            w_in_group(G_CQ)
            pe.wait_ge(relu_done, len(IDX_UNITS))
            pe.wait_ge(roped, roped_by(G_AK))
            pe.wait_ge(pair_read, G_AV + 1)
            for tt, (t0, n) in enumerate(TOK):
                for g in range(A_KV):
                    nc.tensor.transpose(ps[0:n, 4 + tt, g * P:(g + 1) * P], ka_t[:, g, NEW + t0:NEW + t0 + n], ident[:])
                    last = nc.tensor.transpose(ps[0:n, 4 + tt, (2 + g) * P:(3 + g) * P],
                                               z_stage[:, G_AV % 2, g, t0:t0 + n], ident[:])
                last.then_inc(tr_ready, 1)

            def sums_of_squares(b):
                pe.wait_ge(sq_done, b + 1)
                for k in range(KL):
                    last = nc.tensor.matmul(ps[:, 4 + b, 0:NTOK], ones[:], sq_z[:, k, :], start=k == 0, stop=k == KL - 1)
                last.then_inc(sumsq_ready, 1)

            w_in_group(G_CQ + 1)
            w_in_group(G_CQ + 2)
            pe.wait_ge(ones_set, 1)
            pe.wait_ge(tr_copied, 7)
            sums_of_squares(0)
            pe.wait_ge(ckv_past_landed, 16)
            for b in range(2):
                for k in range(2):
                    for t in range(2):
                        last = nc.tensor.transpose(ps[:, 6 + b, (2 * k + t) * P:(2 * k + t + 1) * P],
                                                   ckv_past[:, t, (2 * b + k) * P:(2 * b + k + 1) * P], ident[:])
                last.then_inc(past_lat_ready, 1)
            w_in_group(G_CQ + 3)
            w_in_group(G_AQ)
            sums_of_squares(1)
            for g in range(1, 4):
                w_in_group(G_AQ + g)
            pe.wait_ge(lat_normed, 2 * KL)
            pe.wait_ge(past_lat_lo, 2)
            for tt, (t0, n) in enumerate(TOK):
                for k in range(KL):
                    last = nc.tensor.transpose(ps[0:n, 4 + tt, k * P:(k + 1) * P], lora_z[:, 1, k, t0:t0 + n], ident[:])
                last.then_inc(tok_ready, 1)

            def scores(u):
                branch, kind, h = UNITS[u]
                (t0, n), (k0, nk), bank = TOK[kind], KEYS[kind], 4 + u % 2
                if u >= 2:
                    pe.wait_ge(scores_read if UNITS[u - 2][0] == "A" else p_ready, u - 1)
                for i, hh in enumerate(range(4 * h, 4 * h + 4) if kind == 0 else [h]):
                    out = ps[n * i:n * i + n, bank, 0:nk]
                    if branch == "A":
                        last = nc.tensor.matmul(out, aq_t[:, hh, t0:t0 + n], ka_t[:, hh // GRP, k0:k0 + nk],
                                                start=True, stop=True)
                    else:
                        nc.tensor.matmul(out, qn_t[:, hh, t0:t0 + n], kb_t[:, hh, k0:k0 + nk], start=True, stop=False)
                        last = nc.tensor.matmul(out, qr_t[:, hh // 2, t0:t0 + n], kr_t[:, hh % 2, k0:k0 + nk],
                                                start=False, stop=True)
                last.then_inc(scores_ready, 1)

            def turn_probs(u):
                pe.wait_ge(pn_ready, u + 1)
                if u >= 1:
                    pe.wait_ge(pt_copied, u)
                probs = (probs_a, probs_b)[u >= N_A]
                for j, (off, nk, _) in enumerate(KEY_TILES[UNITS[u][1]]):
                    last = nc.tensor.transpose(ps[0:nk, 6, j * P:(j + 1) * P], probs[:, u % 2, off:off + nk], ident[:])
                last.then_inc(pt_ready, 1)

            def values(u):
                branch, kind, h = UNITS[u]
                pe.wait_ge(pt_copied, u + 1)
                if u >= 1:
                    pe.wait_ge(o_copied, u)
                tiles = KEY_TILES[kind]
                heads = range(4 * h, 4 * h + 4) if branch == "B" and kind == 0 else [h]
                width = P // len(heads)
                probs_t = (probs_ta, probs_tb)[u >= N_A]
                for i, hh in enumerate(heads):
                    for j, (_, nk, t) in enumerate(tiles):
                        if branch == "B":
                            v = vb[0:nk, t, hh * P:(hh + 1) * P]
                        else:
                            g = h if kind == 0 else h // GRP
                            v = va_past[:, t, g * P:(g + 1) * P] if t < 2 else \
                                kv_tok[0:nk, t - 2, (2 + g) * P:(3 + g) * P]
                        last = nc.tensor.matmul(ps[:, 7, width * i:width * (i + 1)], v,
                                                probs_t[0:nk, u % 2, j, width * i:width * (i + 1)],
                                                start=j == 0, stop=j == len(tiles) - 1)
                last.then_inc(o_ready, 1)

            def attention(first, end, group, filled):
                scores(first)
                for u in range(first, end):
                    fill(group, filling(u - first, end - first, filled))
                    if u + 1 < end:
                        scores(u + 1)
                    turn_probs(u)
                    if u > first:
                        values(u - 1)
                fill(group, filling(end - first, end - first, filled))
                values(end - 1)

            fill(G_FILL_A, range(FILLED_A))
            pe.wait_ge(tok_copied, 3)
            pe.wait_ge(roped, roped_by(G_AQ + 3))
            pe.wait_ge(va_landed, 16)
            attention(0, N_A, G_FILL_A, FILLED_A)

            pe.wait_ge(lat_lo, 2)
            pe.wait_ge(pair_read, G_FILL_B - 1)
            for j in range(4):
                step = STEP_UQ + j
                pe.wait_ge(lo_done, step + 1)
                hi, lo = weights(step, KL)
                for i in range(3):
                    n = 3 * j + i
                    if n >= 4:
                        pe.wait_ge(uq_copied, n - 3)
                    if n == 2:
                        pe.wait_ge(pair_read, G_FILL_B)
                    for k in range(KL):
                        cols = slice(i * P, (i + 1) * P)
                        last = three(ps[:, (n + 2) % 4, 0:NTOK], hi[:, k, cols], lo[:, k, cols], cq_hi[:, k, :],
                                     cq_lo[:, k, :], k == 0, k == KL - 1)
                    last.then_inc(uq_ready, 1)
                pe.wait_ge(uq_ready, 3 * j + 3)
                pe.sem_inc(step_done, 1)
            for h in range(B_HEADS):
                step = STEP_UK + h // 4
                if h % 4 == 0:
                    pe.wait_ge(lo_done, step + 1)
                if h < 2:
                    pe.wait_ge(uq_copied, 10 + 2 * h)
                else:
                    pe.wait_ge(uk_copied, h - 1)
                hi, lo = weights(step, KL)
                cols = slice((h % 4) * P, (h % 4 + 1) * P)
                for k in range(KL):
                    for half in range(2):
                        keys = slice(half * NKEY // 2, (half + 1) * NKEY // 2)
                        last = three(ps[:, 2 - 2 * (h % 2) + half, 0:NKEY // 2], hi[:, k, cols], lo[:, k, cols],
                                     ckv_hi[:, k, keys], ckv_lo[:, k, keys], k == 0, k == KL - 1)
                last.then_inc(uk_ready, 1)
                if h % 4 == 3:
                    pe.wait_ge(uk_ready, h + 1)
                    pe.sem_inc(step_done, 1)
            for n in range(10):
                step, w = STEP_UV + n // 5, n % 5
                if w == 0:
                    pe.wait_ge(lo_done, step + 1)
                if n < 4:
                    pe.wait_ge(uk_copied, B_HEADS - 1 + n // 2)
                else:
                    pe.wait_ge(uv_copied, n - 3)
                hi, lo = weights(step, KL)
                keys = slice(V_TILES[w], V_TILES[w] + P)
                for k in range(KL):
                    nc.tensor.matmul(ps[:, (n + 2) % 4, :], ckv_hi[:, k, keys], hi[:, k, :], start=k == 0, stop=False)
                    nc.tensor.matmul(ps[:, (n + 2) % 4, :], ckv_hi[:, k, keys], lo[:, k, :], start=False, stop=False)
                    last = nc.tensor.matmul(ps[:, (n + 2) % 4, :], ckv_lo[:, k, keys], hi[:, k, :],
                                            start=False, stop=k == KL - 1)
                last.then_inc(uv_ready, 1)
                if w == 4:
                    pe.wait_ge(uv_ready, n + 1)
                    pe.sem_inc(step_done, 1)

            pe.wait_ge(q_roped, 1)
            pe.wait_ge(uk_copied, B_HEADS)
            attention(N_A, len(UNITS), G_FILL_B, 0)

            w_in_groups(G_MG, 4)
            w_in_groups(G_GATE, 4)

            def branch_out(step, group, b, it=0):
                pe.wait_ge(lo_done, step + 1 + RAW * it)
                if isinstance(it, int) and group == 0:
                    pe.wait_ge(pair_read, G_END - 1 + b)
                else:
                    pe.wait_ge(y_read, 2 * group + b - 1 + 4 * it)
                hi, lo = weights(step, KH)
                for m in range(2):
                    for k in range(KH):
                        cols = slice(m * P, (m + 1) * P)
                        last = three(ps[:, 2 - 2 * b + m, 0:NTOK], hi[:, k, cols], lo[:, k, cols], og_hi[:, 8 * b + k, :],
                                     og_lo[:, 8 * b + k, :], k == 0, k == KH - 1)
                last.then_inc(step_done, 1)

            for j in range(4):
                if j < 2:
                    pe.wait_ge(gated_lo_done, 4 + 4 * j)
                branch_out(STEP_Y + j, j // 2, j % 2)
            with pe.Fori(0, 3) as it:
                for j in range(4, 8):
                    branch_out(STEP_Y + j, j // 2, j % 2, it)

            def out_half(j, half, it=0):
                if isinstance(it, int) and j < 2:
                    if j == 0:
                        pe.wait_ge(m_done, 4 + 4 * half)
                    if half == 0:
                        pe.wait_ge(y_read, 15 + j)
                elif half == 0:
                    pe.wait_ge(hT_copied, j - 1 + 2 * it)
                half_group(STEP_OUT + 2 * j + half, j + 1, half, m_hi, m_lo, it)

            def turn_out(j, it=0):
                pe.wait_ge(hT_copied, j + 1 + 2 * it)
                if not (isinstance(it, int) and j == 0):
                    pe.wait_ge(h_added, 3 * j + 6 * it)
                for tt, (t0, n) in enumerate(TOK):
                    for m in range(2):
                        last = nc.tensor.transpose(ps[0:n, 4 + tt, m * P:(m + 1) * P], h_stage[:, j % 2, m, t0:t0 + n],
                                                   ident[:])
                last.then_inc(ht_ready, 1)

            out_half(0, 0)
            out_half(0, 1)
            out_half(1, 0)
            turn_out(0)
            out_half(1, 1)
            with pe.Fori(0, 3) as it:
                for j in range(2, 4):
                    out_half(j, 0, it)
                    turn_out(j - 1, it)
                    out_half(j, 1, it)
            turn_out(7)

        @block.scalar
        def _(act):
            def split_hi(step, it=0):
                act.wait_ge(raw_landed[step % RAW], landed(step, it))
                if step >= 2:
                    act.wait_ge(step_done, step - 1 + RAW * it)
                n = 1536 if STEP_UQ <= step < STEP_UK else 2048
                nc.scalar.copy(w_hi[:, step % 2, 0:n], raw[:, step % RAW, 0:n]).then_inc(hi_done, 1)

            def group_ready(group, it=0):
                act.wait_ge(step_done, steps_of(group) + 2 + RAW * it)

            act.wait_ge(ss_cleared, 1)
            act.wait_ge(ones_set, 1)
            nc.scalar.activation(root[:, 3:4], ones[:, 0:1], ACT.Sqrt)
            n = TOK[1][1]
            act.wait_ge(x_landed[1], 16)
            nc.scalar.activation(x_sq[0:n, 0, :], x_tok[0:n, 1, :], ACT.Square, accum_out=ss[0:n, 1:2])
            act.wait_ge(x_landed[2], 16)
            nc.scalar.activation(x_sq[0:n, 1, 0:D_MODEL // 2], x_tok[0:n, 2, 0:D_MODEL // 2], ACT.Square,
                                 accum_out=ss[0:n, 2:3]).then_inc(ss_done, 1)
            act.wait_ge(var_done, 1)
            nc.scalar.activation(root[:, 0:3], var[:, 0:3], ACT.Sqrt).then_inc(root_done, 1)
            split_hi(0)
            act.wait_ge(consts_landed, 32)
            for k in range(KD):
                act.wait_ge(xt_ready, k + 1)
                nc.scalar.activation(x_hi[:, k, :], ps[:, 2 + k % 6, 0:NTOK], ACT.Copy,
                                     scale=norm_g[:, k:k + 1]).then_inc(xhi_done, 1)
                if k in SPLIT_AT:
                    split_hi(SPLIT_AT[k])

            def to_stage(group):
                group_ready(group)
                if group >= G_AQ:
                    act.wait_ge(stage_used, max(rotated_before(group) - 1, G_AK + 1))
                elif group >= 2:
                    act.wait_ge(stage_used, group - 1)
                nc.scalar.copy(z_stage[:, group % 2, :, :], pair(group)).then_inc(pair_read, 1)

            split_hi(3)
            group_ready(G_SMALL)
            for a, b in ((0, 32), (32, 0)):
                nc.scalar.copy(kr_swap[a:a + 32, :], ps[b:b + 32, 1, 0:NTOK]).then_inc(small_copied, 1)
            to_stage(G_SMALL)
            for g in range(G_IQ, G_AK):
                for half in range(2):
                    split_hi(2 * g + 2 + half)
                to_stage(g)

            act.wait_ge(tr_ready, 1)
            nc.scalar.copy(ka_t[:, :, 0:PAST], ps[:, 4, :].rearrange("p (g t) -> p g t", g=2)).then_inc(tr_copied, 1)
            act.wait_ge(tr_ready, 2)
            for i, dst in enumerate((ik_t, kr_t)):
                for half in range(2):
                    rows64 = slice(64 * half, 64 * half + 64)
                    last = nc.scalar.copy(dst[rows64, half, 0:PAST], ps[rows64, 5, i * PAST:(i + 1) * PAST])
            last.then_inc(tr_copied, 1)
            for i, dst in enumerate((ik_tok, kr_tok)):
                act.wait_ge(tr_ready, 3 + i)
                width = dst.shape[2]
                nc.scalar.copy(dst[0:DEC, 0, :], ps[0:DEC, 6 + i, 0:width])
                nc.scalar.copy(dst[:, 1:3, :], ps[:, 6 + i, width:3 * width].rearrange("p (t n) -> p t n", t=2))\
                    .then_inc(tr_copied, 1)

            for i in range(IDX_PIECES):
                if i % 2 == 1:
                    split_hi(STEP_AK + 2 + i // 2)
                if i % 4 == 3:
                    to_stage(G_AK + i // 4)
                for u in units_after(i):
                    tt, heads = IDX_UNITS[u]
                    act.wait_ge(idx_ready, u + 1)
                    if u >= 4:
                        act.wait_ge(idx_added, u - 3)
                    n, width = TOK[tt][1], KEYS[tt][1] * len(heads)
                    nc.scalar.activation(relu_ring[0:n, u % 4, 0:width], ps[0:n, 4 + u % 4, 0:width], ACT.Relu,
                                         scale=IDX_DIM ** -0.5).then_inc(relu_done, 1)

            lat_tiles = lora_z[:].rearrange("p b k t -> p (b k) t")
            for g in range(G_CQ, G_AQ):
                for half in range(2):
                    split_hi(2 * g + 2 + half)
                group_ready(g)
                nc.scalar.copy(lat_tiles[:, 2 * (g - G_CQ):2 * (g - G_CQ) + 2, :], pair(g)).then_inc(pair_read, 1)
                b = (g - G_CQ) // 2
                if g == G_CQ:
                    for tt, (_, n) in enumerate(TOK):
                        act.wait_ge(tr_ready, 5 + tt)
                        nc.scalar.copy(kv_tok[0:n, tt, :], ps[0:n, 4 + tt, :]).then_inc(tr_copied, 1)
                if g == G_CQ + 2:
                    act.wait_ge(idx_added, len(IDX_UNITS))
                    for c in range(2):
                        act.wait_ge(past_lat_ready, c + 1)
                        nc.scalar.copy(ckv_hi[:, 2 * c:2 * c + 2, 0:PAST],
                                       ps[:, 6 + c, :].rearrange("p (k t) -> p k t", k=2)).then_inc(past_lat_hi, 1)
                if g in (G_CQ + 1, G_CQ + 3):
                    act.wait_ge(pair_read, g + 1)
                    if b == 1:
                        act.wait_ge(sumsq_ready, 1)
                    nc.scalar.activation(sq_z[:], lora_z[:, b, :, :], ACT.Square).then_inc(sq_done, 1)

            for g in range(G_AQ, G_FILL_A):
                split_hi(2 * g + 2)
                if g == G_FILL_A - 1:
                    act.wait_ge(lat_normed, 2 * KL)
                    nc.scalar.copy(cq_hi[:], lora_z[:, 0, :, :]).then_inc(lat_hi, 1)
                    nc.scalar.copy(ckv_hi[:, :, NEW:NKEY], lora_z[:, 1, :, :]).then_inc(lat_hi, 1)
                    to_stage(g)
                split_hi(2 * g + 3)
                if g < G_FILL_A - 1:
                    to_stage(g)
                if g == G_AQ:
                    act.wait_ge(lat_var_done, 1)
                    nc.scalar.activation(lat_r[:], lat_var[:], ACT.Sqrt).then_inc(lat_root_done, 1)
                    nc.scalar.activation(root[:, 3:4], ones[:, 0:1], ACT.Exp)
            for tt, (_, n) in enumerate(TOK):
                act.wait_ge(tok_ready, tt + 1)
                nc.scalar.copy(ckv_tok[0:n, tt, :], ps[0:n, 4 + tt, :]).then_inc(tok_copied, 1)

            def exponentials(u):
                branch, kind, _ = UNITS[u]
                nk = KEYS[kind][1]
                act.wait_ge(neg_ready, u + 1)
                if u >= 2:
                    act.wait_ge(pt_ready, u - 1)
                probs = (probs_a, probs_b)[u >= N_A]
                src = masked[:, u % 2, 0:nk] if branch == "A" else ps[:, 4 + u % 2, 0:nk]
                nc.scalar.activation(probs[:, u % 2, 0:nk], src, ACT.Exp, bias=neg_mx[:, u % 2:u % 2 + 1],
                                     scale=A_SCALE if branch == "A" else B_SCALE,
                                     accum_out=sum_p[:, u % 2:u % 2 + 1]).then_inc(p_ready, 1)

            def copy_turned(u):
                act.wait_ge(pt_ready, u + 1)
                if u >= 2:
                    act.wait_ge(o_ready, u - 1)
                tiles = KEY_TILES[UNITS[u][1]]
                probs_t = (probs_ta, probs_tb)[u >= N_A]
                full = sum(nk == P for _, nk, _ in tiles)
                last = nc.scalar.copy(probs_t[:, u % 2, 0:full, :],
                                      ps[:, 6, 0:full * P].rearrange("p (j q) -> p j q", j=full))
                if full < len(tiles):
                    nk = tiles[full][1]
                    last = nc.scalar.copy(probs_t[0:nk, u % 2, full, :], ps[0:nk, 6, full * P:(full + 1) * P])
                last.then_inc(pt_copied, 1)

            def merge_tanh(group, it=0):
                group_ready(group, it)
                nc.scalar.activation(merge_g[:, bass.ds(it * 4 + merge_tile(group), 2), :], pair(group), ACT.Tanh,
                                     scale=0.5).then_inc(pair_read, 1)

            def after(group, part):
                for i in part:
                    if i % (2 * HALF_TILE) == 2 * HALF_TILE - 1:
                        split_hi(steps_of(group) + i // (2 * HALF_TILE) + 2)
                    if i % (4 * HALF_TILE) == 4 * HALF_TILE - 1:
                        if group == G_FILL_A:
                            act.wait_ge(lat_lo, 2)
                        merge_tanh(group + i // (4 * HALF_TILE))

            def attention(first, end, group, filled):
                exponentials(first)
                for u in range(first, end):
                    after(group, filling(u - first - 1, end - first, filled))
                    copy_turned(u)
                    if u + 1 < end:
                        exponentials(u + 1)
                for turn in range(end - first - 1, end - first + 1):
                    after(group, filling(turn, end - first, filled))

            after(G_FILL_A, range(FILLED_A))
            attention(0, N_A, G_FILL_A, FILLED_A)

            act.wait_ge(kv_out, 12 * 16)
            act.wait_ge(ckv_out, 48)
            act.wait_ge(o_ready, N_A)
            for j in range(4):
                for i in range(3):
                    n = 3 * j + i
                    act.wait_ge(uq_ready, n + 1)
                    if i == 2:
                        split_hi(STEP_UQ + 2 + j)
                    if i < 2:
                        nc.scalar.copy(qn_t[:, 2 * j + i, :], ps[:, (n + 2) % 4, 0:NTOK]).then_inc(uq_copied, 1)
                    else:
                        nc.scalar.copy(qr_z[:, j, :], ps[:, (n + 2) % 4, 0:NTOK])
                        for a, b in ((0, 32), (32, 0), (64, 96), (96, 64)):
                            last = nc.scalar.copy(qr_swap[a:a + 32, j, :], ps[b:b + 32, (n + 2) % 4, 0:NTOK])
                        last.then_inc(uq_copied, 1)
            for h in range(B_HEADS):
                act.wait_ge(uk_ready, h + 1)
                nc.scalar.copy(kb_t[:, h, :].rearrange("p (a t) -> p a t", a=2),
                               ps[:, 2 - 2 * (h % 2):4 - 2 * (h % 2), 0:NKEY // 2]).then_inc(uk_copied, 1)
                if h % 4 == 3:
                    split_hi(STEP_UV + h // 4)
            for half in range(2):
                split_hi(STEP_FILL_B + half)
            act.wait_ge(uv_ready, 10)
            attention(N_A, len(UNITS), G_FILL_B, 0)

            for half in range(2):
                split_hi(STEP_MG + 2 + half)
            act.wait_ge(o_copied, len(UNITS))
            merge_tanh(G_MG)
            with act.Fori(0, 3) as it:
                for j in range(2, 4):
                    for half in range(2):
                        split_hi(STEP_MG + 2 * j + half, it)
                    merge_tanh(G_MG + j - 1, it)
            for half in range(2):
                split_hi(STEP_GATE + half)
            merge_tanh(G_GATE - 1)

            def gate_tanh(group, it=0):
                group_ready(group, it)
                if not (isinstance(it, int) and group < G_GATE + 2):
                    act.wait_ge(gate_used, group - G_GATE - 1 + 2 * it)
                nc.scalar.activation(gate_t[:, group % 2, :, :], pair(group), ACT.Tanh, scale=0.5).then_inc(gate_ready, 1)

            def gated_hi(group, it=0):
                act.wait_ge(gate_used, group - G_GATE + 1 + 2 * it)
                nc.scalar.copy(og_hi[:, bass.ds(it * 4 + 2 * (group - G_GATE), 2), :], gate_x[:, group % 2, :, :])\
                    .then_inc(gated_hi_done, 1)

            for half in range(2):
                split_hi(STEP_GATE + 2 + half)
            gate_tanh(G_GATE)
            with act.Fori(0, 3) as it:
                for j in range(2, 4):
                    split_hi(STEP_GATE + 2 * j, it)
                    gated_hi(G_GATE + j - 2, it)
                    split_hi(STEP_GATE + 2 * j + 1, it)
                    gate_tanh(G_GATE + j - 1, it)
            split_hi(STEP_Y)
            gated_hi(G_END - 2)
            gate_tanh(G_END - 1)
            split_hi(STEP_Y + 1)
            gated_hi(G_END - 1)
            for half in range(2):
                split_hi(STEP_Y + 2 + half)
            with act.Fori(0, 3) as it:
                for j in range(4):
                    split_hi(STEP_Y + 4 + j, it)

            def to_h_stage(j):
                act.wait_ge(step_done, STEP_OUT + 2 * j + 2)
                if j >= 2:
                    act.wait_ge(ht_ready, j - 1)
                nc.scalar.activation(h_stage[:, j % 2, :, :], pair(j + 1), ACT.Copy, scale=0.25).then_inc(hT_copied, 1)

            def squares(j):
                if j == 0:
                    act.wait_ge(h_cleared, 1)
                for tt, (_, n) in enumerate(TOK):
                    act.wait_ge(h_added, 3 * j + tt + 1)
                    if j + tt:
                        act.wait_ge(h_squared, 3 * j + tt)
                    nc.scalar.activation(h_sq[0:n, :], h_sum[0:n, j % 2, tt, :], ACT.Square,
                                         accum_out=h_ss[0:n, tt, j:j + 1]).then_inc(h_squared, 1)

            for half in range(2):
                split_hi(STEP_OUT + half)
            nc.scalar.activation(root[:, 3:4], ones[:, 0:1], ACT.Sqrt)
            act.wait_ge(m_done, 8)
            for j in range(1, 8):
                for half in range(2):
                    split_hi(STEP_OUT + 2 * j + half)
                to_h_stage(j - 1)
                if j >= 2:
                    squares(j - 2)
            squares(6)
            to_h_stage(7)
            squares(7)
            act.wait_ge(h_var_done, 1)
            nc.scalar.activation(root[:, 0:3], var[:, 0:3], ACT.Sqrt).then_inc(h_root_done, 1)
            act.wait_ge(h_rstd, 1)
            act.wait_ge(h_weighted, 1)
            n = TOK[ACT_LAST][1]
            for half in range(2):
                cols = slice(half * D_MODEL // 2, (half + 1) * D_MODEL // 2)
                nc.scalar.activation(h_tok[0:n, ACT_LAST, cols], h_tok[0:n, ACT_LAST, cols], ACT.Copy,
                                     scale=rstd[0:n, ACT_LAST:ACT_LAST + 1]).then_inc(h_ready_act, 1)

        @block.vector
        def _(dve):
            own = Tally(dve_self)

            def settled(ins):
                dve.wait_ge(dve_self, own.add(ins))

            def split_lo(step, it=0):
                dve.wait_ge(hi_done, step + 1 + RAW * it)
                n = 1536 if STEP_UQ <= step < STEP_UK else 2048
                nc.vector.tensor_tensor(w_lo[:, step % 2, 0:n], raw[:, step % RAW, 0:n],
                                        w_hi[:, step % 2, 0:n].bitcast(F32), ALU.subtract).then_inc(lo_done, 1)

            def refine(r, v, t):
                settled(nc.vector.tensor_tensor(t, r, r, ALU.mult))
                settled(nc.vector.tensor_tensor(t, t, v, ALU.mult))
                settled(nc.vector.tensor_scalar(t, t, -0.5, 1.5, ALU.mult, ALU.add))
                settled(nc.vector.tensor_tensor(r, r, t, ALU.mult))

            nc.vector.memset(ss[:], 1.0).then_inc(ss_cleared, 1)
            dve.wait_ge(ss_cleared, 1)
            for i, (tt, part) in enumerate(((0, slice(0, D_MODEL)), (2, slice(D_MODEL // 2, D_MODEL)))):
                n = TOK[tt][1]
                dve.wait_ge(x_landed[tt], 16)
                col = (0, 3)[i]
                settled(nc.vector.tensor_tensor_reduce(
                    out=dve_sq[0:n, part], in0=x_tok[0:n, tt, part], in1=x_tok[0:n, tt, part], scale=1.0, scalar=0.0,
                    op0=ALU.mult, op1=ALU.add, accum_out=ss[0:n, col:col + 1]))
            dve.wait_ge(ss_done, 1)
            settled(nc.vector.tensor_tensor(ss[:, 2:3], ss[:, 2:3], ss[:, 3:4], ALU.add))
            nc.vector.tensor_scalar(var[:, 0:3], ss[:, 0:3], 1.0 / D_MODEL, EPS, ALU.mult, ALU.add).then_inc(var_done, 1)
            dve.wait_ge(root_done, 1)
            settled(nc.vector.reciprocal(rstd[:, 0:3], root[:, 0:3]))
            refine(rstd[:, 0:3], var[:, 0:3], root[:, 0:3])
            dve.wait_ge(consts_landed, 32)
            for tt in range(3):
                last = nc.vector.tensor_scalar(diag[:, tt, :], ident[:], rstd[:, tt:tt + 1], None, ALU.mult)
            last.then_inc(diag_done, 1)
            split_lo(0)
            for k in range(KD):
                dve.wait_ge(xhi_done, k + 1)
                nc.vector.scalar_tensor_tensor(out=x_lo[:, k, :], in0=ps[:, 2 + k % 6, 0:NTOK], scalar=norm_g[:, k:k + 1],
                                               in1=x_hi[:, k, :].bitcast(F32), op0=ALU.mult,
                                               op1=ALU.subtract).then_inc(xlo_done, 1)
                if k in SPLIT_AT:
                    split_lo(SPLIT_AT[k])
            dve.wait_ge(rope_landed, 16)

            def table(i, like):
                return rope_tab[:, i:i + 1, :].broadcast_to(like)

            def rotate(group, dst, kind, mask):
                shape = [P, 2, NTOK]
                dve.wait_ge(pair_read, group + 1)
                z = z_stage[:, group % 2, :, :]
                settled(nc.vector.stream_shuffle(z_shuf[:], z, mask))
                nc.vector.tensor_tensor(z_cos[:], z, table(2 * kind, shape), ALU.mult).then_inc(stage_used, 1)
                settled(nc.vector.tensor_tensor(z_shuf[:], z_shuf[:], table(2 * kind + 1, shape), ALU.mult))
                dve.wait_ge(stage_used, rotated_before(group) + 1)
                nc.vector.tensor_tensor(dst, z_cos[:], z_shuf[:], ALU.add).then_inc(roped, 1)
                dve.wait_ge(roped, roped_by(group))

            split_lo(3)
            dve.wait_ge(halves_cleared, 4)
            dve.wait_ge(pair_read, 1)
            z, zk = z_stage[:, 0, 0, :], z_stage[0:ROPE, 0, 1, :]
            settled(nc.vector.stream_shuffle(z_shuf[0:64, 0, :], z[0:64, :], SWAP_8))
            settled(nc.vector.tensor_copy(ik_z[64:P, :], z[64:P, :]))
            settled(nc.vector.tensor_tensor(z_cos[0:64, 0, :], z[0:64, :], rope_tab[0:64, 2, :], ALU.mult))
            settled(nc.vector.tensor_tensor(z_shuf[0:64, 0, :], z_shuf[0:64, 0, :], rope_tab[0:64, 3, :], ALU.mult))
            settled(nc.vector.tensor_tensor(ik_z[0:64, :], z_cos[0:64, 0, :], z_shuf[0:64, 0, :], ALU.add))
            for half in range(2):
                settled(nc.vector.tensor_copy(ik_t[64 * half:64 * half + 64, half, NEW:NKEY], ik_z[0:64, :]))
            settled(nc.vector.tensor_tensor(z_cos[0:ROPE, 1, :], zk, rope_tab[0:ROPE, 4, :], ALU.mult))
            dve.wait_ge(small_copied, 2)
            settled(nc.vector.tensor_tensor(z_shuf[0:ROPE, 1, :], kr_swap[0:ROPE, :], rope_tab[0:ROPE, 5, :], ALU.mult))
            for half in range(2):
                if half == 1:
                    nc.vector.sem_inc(stage_used, 1)
                settled(nc.vector.tensor_tensor(kr_t[64 * half:64 * half + 64, half, NEW:NKEY], z_cos[0:ROPE, 1, :],
                                                z_shuf[0:ROPE, 1, :], ALU.add))
            nc.vector.sem_inc(roped, 2)
            for g in range(G_IQ, G_AK):
                for half in range(2):
                    split_lo(2 * g + 2 + half)
                rotate(g, iq_t[:, 2 * (g - G_IQ):2 * (g - G_IQ) + 2, :], 1, SWAP_8)

            dve.wait_ge(tr_copied, 3)
            settled(nc.vector.tensor_scalar(iw_tok[0:DEC, 0, :], ik_tok[0:DEC, 0, IDX_DIM:IDX_DIM + IDX_HEADS],
                                            IDX_HEADS ** -0.5, None, ALU.mult))
            settled(nc.vector.tensor_scalar(iw_tok[:, 1:3, :], ik_tok[:, 1:3, IDX_DIM:IDX_DIM + IDX_HEADS],
                                            IDX_HEADS ** -0.5, None, ALU.mult))
            begun = set()
            for i in range(IDX_PIECES):
                if i % 2 == 1:
                    split_lo(STEP_AK + 2 + i // 2)
                if i == 3:
                    rotate(G_AK, ka_t[:, :, NEW:NKEY], 0, SWAP_16)
                for u in units_after(i):
                    tt, heads = IDX_UNITS[u]
                    dve.wait_ge(relu_done, u + 1)
                    n, nk = TOK[tt][1], KEYS[tt][1]
                    for j, h in enumerate(heads):
                        r, s = relu_ring[0:n, u % 4, j * nk:(j + 1) * nk], score[0:n, tt, 0:nk]
                        w = iw_tok[0:n, tt, h:h + 1]
                        if tt not in begun:
                            ins = nc.vector.tensor_scalar(s, r, w, None, ALU.mult)
                            begun.add(tt)
                        else:
                            ins = nc.vector.scalar_tensor_tensor(out=s, in0=r, scalar=w, in1=s, op0=ALU.mult,
                                                                 op1=ALU.add)
                        if j < len(heads) - 1:
                            settled(ins)
                    ins.then_inc(idx_added, 1)
                    dve.wait_ge(idx_added, u + 1)
            for tt in (1, 2):
                settled(nc.vector.memset(score[0:CHUNK, tt, KEYS[tt][1] - CHUNK:KEYS[tt][1]], TAKEN))

            def take_eight(tt, r):
                n, nk = TOK[tt][1], KEYS[tt][1]
                src = score if r == 0 else work
                settled(nc.vector.max(top8[0:n, 0, :], src[0:n, tt, 0:nk]))
                settled(nc.vector.match_replace(work[0:n, tt, 0:nk], top8[0:n, 0, :], src[0:n, tt, 0:nk], TAKEN))

            def selection(tt):
                n, nk = TOK[tt][1], KEYS[tt][1]
                w = work[0:n, tt, 0:nk]
                settled(nc.vector.tensor_tensor(w, w, score[0:n, tt, 0:nk], ALU.not_equal))
                settled(nc.vector.tensor_scalar(w, w, -1.0, -NEG, ALU.add, ALU.mult))

            rounds = [(1, r) for r in range(TOPK_PROMPT // 8)] + [(2, r) for r in range(TOPK_PROMPT // 8)] \
                + [(0, r) for r in range(TOPK_SAMPLE // 8)]
            def take_rounds(i):
                n_steps = 9
                for tt, r in rounds[i * len(rounds) // n_steps:(i + 1) * len(rounds) // n_steps]:
                    take_eight(tt, r)
                if i in (11, 14):
                    selection(i // 14)
                if i == 14:
                    selection(2)

            for i in range(STEP_FILL_A - STEP_CQ):
                g, half = G_CQ + i // 2, i % 2
                if g < G_FILL_A - 1 or half == 0:
                    split_lo(STEP_CQ + 2 + i)
                take_rounds(i)
                if g >= G_AQ and half == 1:
                    rotate(g, aq_t[:, 2 * (g - G_AQ):2 * (g - G_AQ) + 2, :], 0, SWAP_16)
                if g == G_CQ + 3 and half == 0:
                    for b in range(2):
                        dve.wait_ge(past_lat_hi, b + 1)
                        cols = slice(2 * b, 2 * b + 2)
                        nc.vector.tensor_tensor(ckv_lo[:, cols, 0:PAST], ps[:, 6 + b, :].rearrange("p (k t) -> p k t", k=2),
                                                ckv_hi[:, cols, 0:PAST].bitcast(F32), ALU.subtract).then_inc(past_lat_lo, 1)
                if g == G_AQ and half == 1:
                    for b in range(2):
                        dve.wait_ge(sumsq_ready, b + 1)
                        last = nc.vector.tensor_scalar(lat_var[:, b, :], ps[:, 4 + b, 0:NTOK], 1.0 / LORA, EPS, ALU.mult,
                                                       ALU.add)
                    last.then_inc(lat_var_done, 1)
                if g == G_AQ + 1 and half == 0:
                    dve.wait_ge(lat_root_done, 1)
                    settled(nc.vector.reciprocal(lat_r[:], lat_r[:]))
                if g == G_AQ + 2 and half == 0:
                    refine(lat_r[:], lat_var[:], z_cos[:])
                if g == G_AQ + 2:
                    if half == 0:
                        dve.wait_ge(lora_g_landed, 32)
                    b = half
                    for k in range(KL):
                        nc.vector.scalar_tensor_tensor(
                            out=lora_z[:, b, k, :], in0=lora_z[:, b, k, :], scalar=lora_g[:, b, k:k + 1],
                            in1=lat_r[:, b, :], op0=ALU.mult, op1=ALU.mult).then_inc(lat_normed, 1)
            dve.wait_ge(lat_normed, 2 * KL)
            split_lo(STEP_FILL_A + 1)
            for q in range(1, 4):
                settled(nc.vector.tensor_copy(work[DEC * q:DEC * q + DEC, 0, :], work[0:DEC, 0, :]))

            def cq_low():
                dve.wait_ge(lat_hi, 1)
                nc.vector.tensor_tensor(cq_lo[:], lora_z[:, 0, :, :], cq_hi[:].bitcast(F32), ALU.subtract)\
                    .then_inc(lat_lo, 1)

            def ckv_low():
                dve.wait_ge(lat_hi, 2)
                nc.vector.tensor_tensor(ckv_lo[:, :, NEW:NKEY], lora_z[:, 1, :, :], ckv_hi[:, :, NEW:NKEY].bitcast(F32),
                                        ALU.subtract).then_inc(lat_lo, 1)

            def row_max(u):
                branch, kind, _ = UNITS[u]
                nk, bank, i = KEYS[kind][1], 4 + u % 2, u % 2
                dve.wait_ge(scores_ready, u + 1)
                if branch == "A":
                    nc.vector.tensor_tensor_reduce(out=masked[:, i, 0:nk], in0=ps[:, bank, 0:nk], in1=work[:, kind, 0:nk],
                                                   scale=1.0, scalar=TAKEN, op0=ALU.add, op1=ALU.max,
                                                   accum_out=mx[:, i:i + 1]).then_inc(scores_read, 1)
                    dve.wait_ge(scores_read, u + 1)
                else:
                    if kind:
                        settled(nc.vector.memset(ps[0:CHUNK, bank, nk - CHUNK:nk], NEG))
                    settled(nc.vector.tensor_reduce(mx[:, i:i + 1], ps[:, bank, 0:nk], AX_X, ALU.max))
                nc.vector.tensor_scalar(neg_mx[:, i:i + 1], mx[:, i:i + 1], -(A_SCALE if branch == "A" else B_SCALE),
                                        None, ALU.mult).then_inc(neg_ready, 1)

            def normalise(u):
                nk, i = KEYS[UNITS[u][1]][1], u % 2
                probs = (probs_a, probs_b)[u >= N_A]
                dve.wait_ge(p_ready, u + 1)
                settled(nc.vector.reciprocal(inv_p[:, i:i + 1], sum_p[:, i:i + 1]))
                nc.vector.tensor_scalar(probs[:, i, 0:nk], probs[:, i, 0:nk], inv_p[:, i:i + 1], None,
                                        ALU.mult).then_inc(pn_ready, 1)

            def copy_out(u):
                branch, kind, h = UNITS[u]
                t0, n = TOK[kind]
                base = 0 if branch == "A" else 8
                dve.wait_ge(o_ready, u + 1)
                if kind == 0:
                    ins = nc.vector.tensor_copy(o_t[:, base + 4 * h:base + 4 * h + 4, 0:DEC],
                                                ps[:, 7, 0:P].rearrange("p (h t) -> p h t", h=4))
                else:
                    ins = nc.vector.tensor_copy(o_t[:, base + h, t0:t0 + n], ps[:, 7, 0:P])
                ins.then_inc(o_copied, 1)

            def after(group, part, first=True, last=True):
                for i in part:
                    if i % (2 * HALF_TILE) == 2 * HALF_TILE - 1:
                        step = steps_of(group) + i // (2 * HALF_TILE) + 2
                        dve.wait_ge(hi_done, step + 1)
                        for cols, wanted in ((slice(0, 1024), first), (slice(1024, 2048), last)):
                            if wanted:
                                ins = nc.vector.tensor_tensor(w_lo[:, step % 2, cols], raw[:, step % RAW, cols],
                                                              w_hi[:, step % 2, cols].bitcast(F32), ALU.subtract)
                        if last:
                            ins.then_inc(lo_done, 1)

            def attention(first, end, group, filled, late):
                row_max(first)
                for u in range(first, end):
                    normalise(u)
                    done = filling(u - first - 1, end - first, filled)
                    after(group, done, last=False)
                    if u + 1 < end:
                        row_max(u + 1)
                    after(group, done, first=False)
                    if u - first in late:
                        late[u - first]()
                    if u > first:
                        copy_out(u - 1)
                after(group, filling(end - first - 1, end - first, filled))
                copy_out(end - 1)
                after(group, filling(end - first, end - first, filled))

            attention(0, N_A, G_FILL_A, FILLED_A, late={0: cq_low, 2: ckv_low})
            for j in range(2, 6):
                split_lo(STEP_UQ + j)
            dve.wait_ge(uq_copied, 12)
            shape = [P, 4, NTOK]
            settled(nc.vector.tensor_tensor(qr_z[:], qr_z[:], table(4, shape), ALU.mult))
            settled(nc.vector.tensor_tensor(qr_swap[:], qr_swap[:], table(5, shape), ALU.mult))
            nc.vector.tensor_tensor(qr_t[:], qr_z[:], qr_swap[:], ALU.add).then_inc(q_roped, 1)
            for half in range(2):
                split_lo(STEP_UV + half)
            dve.wait_ge(q_roped, 1)
            dve.wait_ge(ckv_out, 48)
            for n in range(10):
                dve.wait_ge(uv_ready, n + 1)
                nc.vector.tensor_copy(vb[:, n % 5, 512 * (n // 5):512 * (n // 5) + 512], ps[:, (n + 2) % 4, :])\
                    .then_inc(uv_copied, 1)
                if n == 7:
                    split_lo(STEP_FILL_B)
            attention(N_A, len(UNITS), G_FILL_B, 0, late={0: lambda: split_lo(STEP_FILL_B + 1)})

            for half in range(2):
                split_lo(STEP_MG + 2 + half)
            with dve.Fori(0, 3) as it:
                for j in range(4):
                    split_lo(STEP_MG + 4 + j, it)
            for half in range(2):
                split_lo(STEP_GATE + half)

            def gated(group, it=0):
                dve.wait_ge(gate_ready, group - G_GATE + 1 + 2 * it)
                t, x = gate_t[:, group % 2, :, :], gate_x[:, group % 2, :, :]
                nc.vector.scalar_tensor_tensor(out=t, in0=t, scalar=1.0, in1=pair(group), op0=ALU.add, op1=ALU.mult)\
                    .then_inc(pair_read, 1)
                dve.wait_ge(pair_read, group + 1 + 2 * it)
                nc.vector.tensor_tensor(x, t, o_t[:, bass.ds(it * 4 + 2 * (group - G_GATE), 2), :], ALU.mult)\
                    .then_inc(gate_used, 1)

            def gated_lo(group, it=0):
                dve.wait_ge(gated_hi_done, group - G_GATE + 1 + 2 * it)
                tiles = bass.ds(it * 4 + 2 * (group - G_GATE), 2)
                nc.vector.tensor_tensor(og_lo[:, tiles, :], gate_x[:, group % 2, :, :], og_hi[:, tiles, :].bitcast(F32),
                                        ALU.subtract).then_inc(gated_lo_done, 1)

            for half in range(2):
                split_lo(STEP_GATE + 2 + half)
            gated(G_GATE)
            with dve.Fori(0, 3) as it:
                for j in range(2, 4):
                    split_lo(STEP_GATE + 2 * j, it)
                    gated_lo(G_GATE + j - 2, it)
                    split_lo(STEP_GATE + 2 * j + 1, it)
                    gated(G_GATE + j - 1, it)
            split_lo(STEP_Y)
            gated_lo(G_END - 2)
            gated(G_END - 1)
            split_lo(STEP_Y + 1)
            gated_lo(G_END - 1)

            def merge_a(j, it=0):
                dve.wait_ge(step_done, STEP_Y + 2 * j + 1 + RAW * it)
                settled(nc.vector.scalar_tensor_tensor(out=y_a[:], in0=merge_g[:, bass.ds(it * 4 + 2 * j, 2), :],
                                                       scalar=1.0, in1=ps[:, 2:4, 0:NTOK], op0=ALU.add, op1=ALU.mult))
                nc.vector.sem_inc(y_read, 1)

            def merge_b(j, it=0):
                dve.wait_ge(step_done, STEP_Y + 2 * j + 2 + RAW * it)
                tiles = bass.ds(it * 4 + 2 * j, 2)
                nc.vector.scalar_tensor_tensor(out=y_b[:], in0=merge_g[:, bass.ds(it * 4 + 16 + 2 * j, 2), :],
                                               scalar=1.0, in1=ps[:, 0:2, 0:NTOK], op0=ALU.add, op1=ALU.mult)\
                    .then_inc(y_read, 1)
                dve.wait_ge(y_read, 2 * j + 2 + 4 * it)
                settled(nc.vector.tensor_tensor(y_a[:], y_a[:], y_b[:], ALU.add))
                settled(nc.vector.tensor_copy(m_hi[:, tiles, :], y_a[:]))
                nc.vector.tensor_tensor(m_lo[:, tiles, :], y_a[:], m_hi[:, tiles, :].bitcast(F32),
                                        ALU.subtract).then_inc(m_done, 1)
                dve.wait_ge(m_done, j + 1 + 2 * it)

            merge_a(0)
            split_lo(STEP_Y + 2)
            merge_b(0)
            split_lo(STEP_Y + 3)
            merge_a(1)
            with dve.Fori(0, 3) as it:
                own.enter(it, 6)
                for j in range(2, 4):
                    split_lo(STEP_Y + 2 * j, it)
                    merge_b(j - 1, it)
                    split_lo(STEP_Y + 2 * j + 1, it)
                    merge_a(j, it)
            own.leave(3)
            split_lo(STEP_OUT)
            merge_b(7)
            split_lo(STEP_OUT + 1)

            def add_residual(j):
                dve.wait_ge(ht_ready, j + 1)
                if j >= 2:
                    dve.wait_ge(h_squared, 3 * (j - 1))
                cols = slice(256 * j, 256 * j + 256)
                for tt, (_, n) in enumerate(TOK):
                    nc.vector.tensor_tensor(h_sum[0:n, j % 2, tt, :], h_tok[0:n, tt, cols],
                                            ps[0:n, 4 + tt, 0:256], ALU.add).then_inc(h_added, 1)
                dve.wait_ge(h_added, 3 * j + 3)
                for tt, (_, n) in enumerate(TOK):
                    last = nc.vector.tensor_tensor(h_tok[0:n, tt, cols], h_sum[0:n, j % 2, tt, :],
                                                   final_g[0:n, cols], ALU.mult)
                return last

            for half in range(2):
                split_lo(STEP_OUT + 2 + half)
            nc.vector.memset(h_ss[:], 1.0).then_inc(h_cleared, 1)
            dve.wait_ge(res_landed, 48)
            dve.wait_ge(fg_landed, 16)
            for j in range(2, 8):
                split_lo(STEP_OUT + 2 * j)
                add_residual(j - 2)
                split_lo(STEP_OUT + 2 * j + 1)
            add_residual(6)
            add_residual(7).then_inc(h_weighted, 1)

            dve.wait_ge(h_squared, 24)
            settled(nc.vector.tensor_reduce(ss[:, 0:3], h_ss[:], AX_X, ALU.add))
            nc.vector.tensor_scalar(var[:, 0:3], ss[:, 0:3], 1.0 / D_MODEL, EPS, ALU.mult, ALU.add)\
                .then_inc(h_var_done, 1)
            dve.wait_ge(h_root_done, 1)
            settled(nc.vector.reciprocal(rstd[:, 0:3], root[:, 0:3]))
            refine(rstd[:, 0:3], var[:, 0:3], root[:, 0:3])
            nc.vector.sem_inc(h_rstd, 1)
            dve.wait_ge(h_weighted, 1)
            for tt in DVE_LAST:
                n = TOK[tt][1]
                for half in range(2):
                    cols = slice(half * D_MODEL // 2, (half + 1) * D_MODEL // 2)
                    nc.vector.tensor_scalar(h_tok[0:n, tt, cols], h_tok[0:n, tt, cols], rstd[0:n, tt:tt + 1], None,
                                            ALU.mult).then_inc(h_ready, 1)


def rope_tables():
    pos = np.concatenate([PAST + np.arange(DEC), np.arange(SEQ)]).astype(np.float32)
    tables = np.zeros((6, P, NTOK), np.float32)
    for kind, (width, rot) in enumerate(((A_DIM, A_DIM // 4), (IDX_DIM, IDX_DIM // 4), (ROPE, ROPE))):
        half = rot // 2
        freq = (np.float32(ROPE_THETA) ** (-np.arange(half, dtype=np.float32) * np.float32(2.0 / rot))).astype(np.float32)
        angle = (freq[:, None] * pos[None, :]).astype(np.float32)
        tables[2 * kind] = 1.0
        for start in range(0, P, width):
            tables[2 * kind, start:start + half] = np.cos(angle)
            tables[2 * kind, start + half:start + rot] = np.cos(angle)
            tables[2 * kind + 1, start:start + half] = -np.sin(angle)
            tables[2 * kind + 1, start + half:start + rot] = np.sin(angle)
    return tables


OUTPUTS = [("y_prompt", (SEQ, D_MODEL)), ("y_sample", (DEC, D_MODEL))] + [
    (f"{name}_{part}", (n, width)) for part, n in (("prompt", SEQ), ("sample", DEC))
    for name, width in (("new_a_k", 256), ("new_a_v", 256), ("new_idx_k", IDX_DIM), ("new_ckv", LORA),
                        ("new_krope", ROPE))]
SHAPES = [(1, SEQ, D_MODEL), (1, DEC, D_MODEL)] + [
    (1, 1, n, *width) for n in (SEQ, DEC)
    for width in ((A_KV, A_DIM), (A_KV, A_DIM), (IDX_DIM,), (LORA,), (ROPE,))]


def kernel(**inputs):
    import concourse.bacc as bacc
    from concourse.bass_utils import run_bass_kernel_spmd

    flat = {
        "x_prompt": (SEQ, D_MODEL), "x_sample": (DEC, D_MODEL), "cache_a_k": (PAST, 256), "cache_a_v": (PAST, 256),
        "cache_idx_k": (PAST, IDX_DIM), "cache_mla_ckv": (PAST, LORA), "cache_mla_krope": (PAST, ROPE),
        "norm_g": (D_MODEL,), "w_in": (D_MODEL, PROJ), "w_uq": (LORA, 1536), "q_norm_g": (LORA,),
        "kv_norm_g": (LORA,), "w_uk": (LORA, 1024), "w_uv": (LORA, 1024), "w_o_a": (1024, D_MODEL),
        "w_o_b": (1024, D_MODEL), "w_out": (D_MODEL, D_MODEL), "final_g": (D_MODEL,)}
    arrays = {f"in_{k}": np.ascontiguousarray(np.asarray(inputs[k]).reshape(s)) for k, s in flat.items()}
    uq = arrays["in_w_uq"].reshape(LORA, 4, 2, NOPE + ROPE)
    arrays["in_w_uq"] = np.concatenate([uq[..., :NOPE].reshape(LORA, 4, -1), uq[..., NOPE:].reshape(LORA, 4, -1)],
                                       axis=2).reshape(LORA, -1)
    for name in ("norm_g", "q_norm_g", "kv_norm_g"):
        arrays[f"in_{name}"] = np.ascontiguousarray(arrays[f"in_{name}"].reshape(-1, P).T)
    arrays["in_ident"] = np.eye(P, dtype=np.float32)
    arrays["in_rope_tab"] = rope_tables()

    nc = bacc.Bacc("TRN2", target_bir_lowering=False, num_devices=1)
    d = {k[3:]: nc.dram_tensor(k, a.shape, F32, kind="ExternalInput").ap() for k, a in arrays.items()}
    for name, shape in OUTPUTS:
        d[name] = nc.dram_tensor(f"out_{name}", shape, F32, kind="ExternalOutput").ap()
    hybrid_layer(nc, d)
    got = run_bass_kernel_spmd(nc, [arrays], core_ids=[0]).results[0]
    return tuple(got[f"out_{name}"].reshape(shape) for (name, _), shape in zip(OUTPUTS, SHAPES))
```
